# Optimizing a Trainium2 kernel written in Bass

```python
import math
import jax, jax.numpy as jnp
from jax import lax
import numpy as np

D_MODEL = 1024
BATCH = 1
SEQ = 512
DEPTH = 2

GRID_W = 64
CTX_LEN = 256
HEAD_DIM = 64
N_MIXERS = 4
N_HEADS = D_MODEL // HEAD_DIM
GROUP_HEADS = N_HEADS // N_MIXERS
GROUP_W = GROUP_HEADS * HEAD_DIM
D_MIX = N_MIXERS * GROUP_W
CHUNK = 64
DN_CONV = 3
NA_KH = 8
NA_KW = 16
DF_HEAD_DIM = HEAD_DIM // 2
Q_BLOCK = 128
ROPE_BASE = 10000.0
D_FF = 2816
FFN_CONV = 3
EPS = 1e-6
DN_W = 4 * GROUP_W + 4 * GROUP_HEADS
NA_W = 3 * GROUP_W
DF_W = 3 * GROUP_W
HG_W = 5 * GROUP_W
P_IN = DN_W + NA_W + DF_W + HG_W

kernel_name = "hybrid_parallel_group_diffusion_block"

def _split(x, sizes, axis=-1):
    return jnp.split(x, np.cumsum(sizes)[:-1].tolist(), axis=axis)

def _rmsnorm(x, w):
    xf = x.astype(jnp.float32)
    y = xf * lax.rsqrt(jnp.mean(jnp.square(xf), axis=-1, keepdims=True) + EPS)
    return (y * w.astype(jnp.float32)).astype(x.dtype)

def _l2norm(x):
    xf = x.astype(jnp.float32)
    return (xf * lax.rsqrt(jnp.sum(jnp.square(xf), axis=-1, keepdims=True) + EPS)).astype(x.dtype)

def _dwconv(x, w):
    k, ch = w.shape
    return lax.conv_general_dilated(x, w[:, None, :].astype(x.dtype), window_strides=(1,),
                                    padding=[(k // 2, k // 2)], dimension_numbers=("NWC", "WIO", "NWC"),
                                    feature_group_count=ch)

def _heads(x, n):
    b, l, _ = x.shape
    return x.reshape(b, l, n, -1).transpose(0, 2, 1, 3)

def _merge(x):
    b, h, l, d = x.shape
    return x.transpose(0, 2, 1, 3).reshape(b, l, h * d)

def _rope_2d_tables(length, dh):
    t = jnp.arange(length)
    row = (t // GRID_W).astype(jnp.float32)
    col = (t % GRID_W).astype(jnp.float32)
    half = dh // 2
    inv = 1.0 / (ROPE_BASE ** (jnp.arange(0, half, 2, dtype=jnp.float32) / half))
    ang_r = row[:, None] * inv
    ang_c = col[:, None] * inv
    return jnp.cos(ang_r), jnp.sin(ang_r), jnp.cos(ang_c), jnp.sin(ang_c)

def _rotate(x, cos, sin):
    x1, x2 = jnp.split(x, 2, axis=-1)
    cos = cos.astype(x.dtype)
    sin = sin.astype(x.dtype)
    return jnp.concatenate([x1 * cos - x2 * sin, x2 * cos + x1 * sin], axis=-1)

def _rope_2d(x, cos_r, sin_r, cos_c, sin_c):
    xr, xc = jnp.split(x, 2, axis=-1)
    return jnp.concatenate([_rotate(xr, cos_r, sin_r), _rotate(xc, cos_c, sin_c)], axis=-1)

def _gated_delta_rule(q, k, v, beta, log_a, s0):
    f32 = jnp.float32
    b, h, length, dk = q.shape
    dv = v.shape[-1]
    n = length // CHUNK
    ch = lambda t: t.astype(f32).reshape(b, h, n, CHUNK, *t.shape[3:])
    q = ch(q) * (dk ** -0.5)
    k = ch(k)
    v = ch(v)
    beta = ch(beta)
    g = jnp.cumsum(ch(log_a), axis=-1)
    incl = jnp.tril(jnp.ones((CHUNK, CHUNK), bool))
    strict = jnp.tril(jnp.ones((CHUNK, CHUNK), bool), -1)
    gdiff = g[..., :, None] - g[..., None, :]
    decay = jnp.where(incl, jnp.exp(jnp.where(incl, gdiff, 0.0)), 0.0)
    kb = k * beta[..., None]
    a_mat = jnp.where(strict, jnp.einsum("bhncd,bhnsd->bhncs", kb, k) * decay, 0.0)
    eye = jnp.eye(CHUNK, dtype=f32)
    t_mat = lax.linalg.triangular_solve(a_mat + eye, jnp.broadcast_to(eye, a_mat.shape),
                                        left_side=True, lower=True, unit_diagonal=True)
    eg = jnp.exp(g)
    w = t_mat @ (kb * eg[..., None])
    u = t_mat @ (v * beta[..., None])
    attn = jnp.einsum("bhncd,bhnsd->bhncs", q, k) * decay
    qg = q * eg[..., None]
    kdec = k * jnp.exp(g[..., -1:] - g)[..., None]
    glast = jnp.exp(g[..., -1])

    def step(s, xs):
        qg_c, w_c, u_c, attn_c, kdec_c, gl_c = xs
        v_new = u_c - w_c @ s
        o = qg_c @ s + attn_c @ v_new
        s = s * gl_c[..., None, None] + jnp.swapaxes(kdec_c, -1, -2) @ v_new
        return s, o

    xs = tuple(jnp.moveaxis(t, 2, 0) for t in (qg, w, u, attn, kdec, glast))
    s_fin, o = lax.scan(step, s0.astype(f32), xs)
    return jnp.moveaxis(o, 0, 2).reshape(b, h, length, dv), s_fin

def _hgrn2_chunked(q, k, v, log_f, s0):
    f32 = jnp.float32
    b, h, length, dk = q.shape
    dv = v.shape[-1]
    n = length // CHUNK
    ch = lambda t: t.astype(f32).reshape(b, h, n, CHUNK, t.shape[-1])
    q = ch(q) * (dk ** -0.5)
    k = ch(k)
    v = ch(v)
    cum = jnp.cumsum(ch(log_f), axis=-2)
    qb = q * jnp.exp(cum)
    kend = k * jnp.exp(cum[..., -1:, :] - cum)
    dend = jnp.exp(cum[..., -1, :])
    incl = jnp.tril(jnp.ones((CHUNK, CHUNK), bool))[:, :, None]

    def step(s, xs):
        q_c, k_c, v_c, b_c, qb_c, ke_c, de_c = xs
        bd = b_c[..., :, None, :] - b_c[..., None, :, :]
        dec = jnp.where(incl, jnp.exp(jnp.where(incl, bd, 0.0)), 0.0)
        att = jnp.einsum("bhtd,bhsd,bhtsd->bhts", q_c, k_c, dec)
        o = qb_c @ s + att @ v_c
        s = s * de_c[..., None] + jnp.swapaxes(ke_c, -1, -2) @ v_c
        return s, o

    xs = tuple(jnp.moveaxis(t, 2, 0) for t in (q, k, v, cum, qb, kend, dend))
    s_fin, o = lax.scan(step, s0.astype(f32), xs)
    return jnp.moveaxis(o, 0, 2).reshape(b, h, length, dv), s_fin

def _flip(t, d):
    return jnp.flip(t, axis=2) if d == 1 else t

def _bidir_scan(scan_fn, ctx_dirs, lat_dirs, s0):
    o_ctx = 0.0
    o_lat = 0.0
    for d in range(2):
        oc, sc = scan_fn(*[_flip(t, d) for t in ctx_dirs[d]], s0)
        ox, _ = scan_fn(*[_flip(t, d) for t in lat_dirs[d]], sc)
        o_ctx = o_ctx + _flip(oc, d)
        o_lat = o_lat + _flip(ox, d)
    return o_lat, o_ctx

def _deltanet_mixer(p_lat, p_ctx, need_ctx, conv_w, a_log, dt_bias, norm_w):
    nh = GROUP_HEADS
    f32 = jnp.float32

    def prep(p):
        b, length, _ = p.shape
        qkv, gate, ba = _split(p, [3 * GROUP_W, GROUP_W, 4 * nh])
        q, k, v = _split(jax.nn.silu(_dwconv(qkv, conv_w)), [GROUP_W] * 3)
        q = _l2norm(_heads(q, nh))
        k = _l2norm(_heads(k, nh))
        v = _heads(v, nh)
        ba = ba.astype(f32).reshape(b, length, 4, nh).transpose(2, 0, 3, 1)
        dirs = []
        for d in range(2):
            beta = jax.nn.sigmoid(ba[d])
            log_a = -jnp.exp(a_log[d].astype(f32))[None, :, None] * jax.nn.softplus(
                ba[2 + d] + dt_bias[d].astype(f32)[None, :, None])
            dirs.append((q, k, v, beta, log_a))
        return dirs, gate

    lat_dirs, g_lat = prep(p_lat)
    ctx_dirs, g_ctx = prep(p_ctx)
    s0 = jnp.zeros((p_lat.shape[0], nh, HEAD_DIM, HEAD_DIM), jnp.float32)
    o_lat, o_ctx = _bidir_scan(_gated_delta_rule, ctx_dirs, lat_dirs, s0)
    post = lambda o, g: (_merge(_rmsnorm(o, norm_w)) * jax.nn.silu(g.astype(f32))).astype(p_lat.dtype)
    return post(o_lat, g_lat), (post(o_ctx, g_ctx) if need_ctx else None)

def _na_mixer(p_lat, p_ctx, need_ctx, rpb):
    nh = GROUP_HEADS
    d = HEAD_DIM
    scale = d ** -0.5
    q, k, v = [_heads(t, nh) for t in _split(p_lat, [GROUP_W] * 3)]
    qc, kc, vc = [_heads(t, nh) for t in _split(p_ctx, [GROUP_W] * 3)]
    b, h, length, _ = q.shape
    rows = length // GRID_W
    kh = min(NA_KH, rows)
    kw = min(NA_KW, GRID_W)
    grid = lambda t: t.reshape(b, h, rows, GRID_W, d)
    q = grid(q) * scale
    k = grid(k)
    v = grid(v)
    cols = np.arange(GRID_W)
    c_start = np.clip(cols - kw // 2, 0, GRID_W - kw)
    col_idx = c_start[:, None] + np.arange(kw)[None, :]
    col_bias_idx = col_idx - cols[:, None] + (NA_KW - 1)
    rpb_cols = rpb[:, :, col_bias_idx]

    def row_block(r):
        r_start = jnp.clip(r - kh // 2, 0, rows - kh)
        k_band = lax.dynamic_slice_in_dim(k, r_start, kh, axis=2)[:, :, :, col_idx, :]
        v_band = lax.dynamic_slice_in_dim(v, r_start, kh, axis=2)[:, :, :, col_idx, :]
        q_r = lax.dynamic_index_in_dim(q, r, axis=2, keepdims=False)
        row_bias_idx = r_start + jnp.arange(kh) - r + (NA_KH - 1)
        bias = jnp.take(rpb_cols, row_bias_idx, axis=1).transpose(0, 2, 1, 3)
        s_loc = jnp.einsum("bhwd,bhiwjd->bhwij", q_r, k_band) + bias[None]
        s_ctx = jnp.einsum("bhwd,bhmd->bhwm", q_r, kc)
        logits = jnp.concatenate([s_loc.reshape(b, h, GRID_W, kh * kw), s_ctx], axis=-1).astype(jnp.float32)
        prob = jax.nn.softmax(logits, axis=-1).astype(v.dtype)
        p_loc = prob[..., :kh * kw].reshape(b, h, GRID_W, kh, kw)
        p_ctx_r = prob[..., kh * kw:]
        return (jnp.einsum("bhwij,bhiwjd->bhwd", p_loc, v_band)
                + jnp.einsum("bhwm,bhmd->bhwd", p_ctx_r, vc))

    o = lax.map(row_block, jnp.arange(rows))
    o_lat = o.transpose(1, 0, 3, 2, 4).reshape(b, length, h * d)
    o_ctx = None
    if need_ctx:
        pc = jax.nn.softmax(jnp.einsum("bhmd,bhnd->bhmn", qc * scale, kc).astype(jnp.float32), axis=-1)
        o_ctx = _merge(jnp.einsum("bhmn,bhnd->bhmd", pc.astype(vc.dtype), vc))
    return o_lat, o_ctx

def _diff_mixer(p_lat, p_ctx, need_ctx, lam_p, norm_w, lam_init, rope):
    nh = GROUP_HEADS
    dh = DF_HEAD_DIM
    scale = dh ** -0.5

    def prep(p):
        b, length, _ = p.shape
        q, k, v = _split(p, [GROUP_W] * 3)
        q = q.reshape(b, length, nh, 2, dh).transpose(0, 2, 3, 1, 4)
        k = k.reshape(b, length, nh, 2, dh).transpose(0, 2, 3, 1, 4)
        return q, k, _heads(v, nh)

    q, k, v = prep(p_lat)
    qc, kc, vc = prep(p_ctx)
    q = _rope_2d(q, *rope) * scale
    k = _rope_2d(k, *rope)
    lp = lam_p.astype(jnp.float32)
    lam = jnp.exp(jnp.sum(lp[0] * lp[1])) - jnp.exp(jnp.sum(lp[2] * lp[3])) + lam_init

    def diff_attend(qb, kk, vv):
        s = jnp.einsum("bhjqd,bhjkd->bhjqk", qb, kk).astype(jnp.float32)
        pr = jax.nn.softmax(s, axis=-1)
        a = pr[:, :, 0] - lam * pr[:, :, 1]
        return jnp.einsum("bhqk,bhkd->bhqd", a.astype(vv.dtype), vv)

    k_all = jnp.concatenate([kc, k], axis=3)
    v_all = jnp.concatenate([vc, v], axis=2)
    b, h, _, length, _ = q.shape
    nb = length // Q_BLOCK
    q_blocks = jnp.moveaxis(q.reshape(b, h, 2, nb, Q_BLOCK, dh), 3, 0)
    o = lax.map(lambda qb: diff_attend(qb, k_all, v_all), q_blocks)
    o = jnp.moveaxis(o, 0, 2).reshape(b, h, length, 2 * dh)
    post = lambda t: _merge(_rmsnorm(t, norm_w) * (1.0 - lam_init))
    o_ctx = post(diff_attend(qc * scale, kc, vc)) if need_ctx else None
    return post(o), o_ctx

def _hgrn2_mixer(p_lat, p_ctx, need_ctx, lb, norm_w):
    nh = GROUP_HEADS
    f32 = jnp.float32

    def prep(p):
        q, i, f_fwd, f_bwd, gate = _split(p, [GROUP_W] * 5)
        q = _heads(q, nh)
        v = _heads(i, nh)
        dirs = []
        for d, f_raw in enumerate((f_fwd, f_bwd)):
            f = lb[d] + (1.0 - lb[d]) * jax.nn.sigmoid(f_raw.astype(f32))
            dirs.append((q, _heads(1.0 - f, nh), v, _heads(jnp.log(f), nh)))
        return dirs, gate

    lat_dirs, g_lat = prep(p_lat)
    ctx_dirs, g_ctx = prep(p_ctx)
    s0 = jnp.zeros((p_lat.shape[0], nh, HEAD_DIM, HEAD_DIM), jnp.float32)
    o_lat, o_ctx = _bidir_scan(_hgrn2_chunked, ctx_dirs, lat_dirs, s0)
    post = lambda o, g: (_merge(_rmsnorm(o, norm_w)) * jax.nn.silu(g.astype(f32))).astype(p_lat.dtype)
    return post(o_lat, g_lat), (post(o_ctx, g_ctx) if need_ctx else None)

def _token_mixers(p_lat, p_ctx, need_ctx, layer, rope, dn_conv_w, dn_a_log, dn_dt_bias, dn_norm_w,
                  na_rpb, df_lambda, df_norm_w, hg_lb, hg_norm_w):
    sizes = [DN_W, NA_W, DF_W, HG_W]
    dn_x, na_x, df_x, hg_x = _split(p_lat, sizes)
    dn_c, na_c, df_c, hg_c = _split(p_ctx, sizes)
    lam_init = 0.8 - 0.6 * math.exp(-0.3 * layer)
    outs = [
        _deltanet_mixer(dn_x, dn_c, need_ctx, dn_conv_w, dn_a_log, dn_dt_bias, dn_norm_w),
        _na_mixer(na_x, na_c, need_ctx, na_rpb),
        _diff_mixer(df_x, df_c, need_ctx, df_lambda, df_norm_w, lam_init, rope),
        _hgrn2_mixer(hg_x, hg_c, need_ctx, hg_lb, hg_norm_w),
    ]
    y_lat = jnp.concatenate([o[0].astype(p_lat.dtype) for o in outs], axis=-1)
    y_ctx = jnp.concatenate([o[1].astype(p_ctx.dtype) for o in outs], axis=-1) if need_ctx else None
    return y_lat, y_ctx

def _conv_ffn(h, w_up, conv_w, w_down):
    gate, val = jnp.split(h @ w_up, 2, axis=-1)
    return (jax.nn.silu(_dwconv(gate, conv_w)) * val) @ w_down

def _modulate(t, w, shift, scale):
    return _rmsnorm(t, w) * (1.0 + scale) + shift

def setup_inputs(seed: int = 0) -> dict:
    key = jax.random.key(seed)
    ks = jax.random.split(key, 24)
    f32 = jnp.float32
    nrm = lambda k, shape, s: jax.random.normal(k, shape, f32) * s
    gain = lambda k, shape: 1.0 + 0.02 * jax.random.normal(k, shape, f32)
    dt = jnp.exp(jax.random.uniform(ks[10], (DEPTH, 2, GROUP_HEADS), f32, math.log(1e-3), math.log(1e-1)))
    return {
        "x": nrm(ks[0], (BATCH, SEQ, D_MODEL), 1.0),
        "c": nrm(ks[1], (BATCH, D_MODEL), 1.0),
        "ctx": nrm(ks[2], (BATCH, CTX_LEN, D_MODEL), 1.0),
        "c_ctx": nrm(ks[3], (D_MODEL,), 1.0),
        "w_ada": nrm(ks[4], (DEPTH, D_MODEL, 6 * D_MODEL), 0.5 * D_MODEL ** -0.5),
        "b_ada": nrm(ks[5], (DEPTH, 6 * D_MODEL), 0.02),
        "norm1_w": gain(ks[6], (DEPTH, D_MODEL)),
        "norm2_w": gain(ks[7], (DEPTH, D_MODEL)),
        "w_in": nrm(ks[8], (DEPTH, D_MODEL, P_IN), D_MODEL ** -0.5),
        "dn_conv_w": nrm(ks[9], (DEPTH, DN_CONV, 3 * GROUP_W), DN_CONV ** -0.5),
        "dn_a_log": jnp.log(jax.random.uniform(ks[11], (DEPTH, 2, GROUP_HEADS), f32, 1.0, 16.0)),
        "dn_dt_bias": dt + jnp.log(-jnp.expm1(-dt)),
        "dn_norm_w": gain(ks[12], (DEPTH, HEAD_DIM)),
        "na_rpb": nrm(ks[13], (DEPTH, GROUP_HEADS, 2 * NA_KH - 1, 2 * NA_KW - 1), 0.02),
        "df_lambda": nrm(ks[14], (DEPTH, 4, DF_HEAD_DIM), 0.1),
        "df_norm_w": gain(ks[15], (DEPTH, 2 * DF_HEAD_DIM)),
        "hg_lb_raw": nrm(ks[16], (DEPTH, 2, GROUP_W), 0.1),
        "hg_norm_w": gain(ks[17], (DEPTH, HEAD_DIM)),
        "w_out": nrm(ks[18], (DEPTH, D_MIX, D_MODEL), D_MIX ** -0.5),
        "w_up": nrm(ks[19], (DEPTH, D_MODEL, 2 * D_FF), D_MODEL ** -0.5),
        "ffn_conv_w": nrm(ks[20], (DEPTH, FFN_CONV, D_FF), FFN_CONV ** -0.5),
        "w_down": nrm(ks[21], (DEPTH, D_FF, D_MODEL), D_FF ** -0.5),
        "final_norm_w": gain(ks[22], (D_MODEL,)),
    }

def reference(x, c, ctx, c_ctx, w_ada, b_ada, norm1_w, norm2_w, w_in, dn_conv_w, dn_a_log, dn_dt_bias,
              dn_norm_w, na_rpb, df_lambda, df_norm_w, hg_lb_raw, hg_norm_w, w_out, w_up, ffn_conv_w,
              w_down, final_norm_w):
    length = x.shape[1]
    rope = _rope_2d_tables(length, DF_HEAD_DIM)
    lb_all = jnp.cumsum(jax.nn.softmax(hg_lb_raw.astype(jnp.float32), axis=0), axis=0)
    lb_all = lb_all - lb_all[0]
    silu_c = jax.nn.silu(c)
    silu_cc = jax.nn.silu(c_ctx)
    h_ctx = ctx
    for l in range(DEPTH):
        need_ctx = l < DEPTH - 1
        mx = jnp.split((silu_c @ w_ada[l] + b_ada[l])[:, None, :], 6, axis=-1)
        mc = jnp.split(silu_cc @ w_ada[l] + b_ada[l], 6, axis=-1)
        p_lat = _modulate(x, norm1_w[l], mx[0], mx[1]) @ w_in[l]
        p_ctx = _modulate(h_ctx, norm1_w[l], mc[0], mc[1]) @ w_in[l]
        y_lat, y_ctx = _token_mixers(p_lat, p_ctx, need_ctx, l, rope, dn_conv_w[l], dn_a_log[l],
                                     dn_dt_bias[l], dn_norm_w[l], na_rpb[l], df_lambda[l], df_norm_w[l],
                                     lb_all[l], hg_norm_w[l])
        x = x + mx[2] * (y_lat @ w_out[l])
        x = x + mx[5] * _conv_ffn(_modulate(x, norm2_w[l], mx[3], mx[4]), w_up[l], ffn_conv_w[l], w_down[l])
        if need_ctx:
            h_ctx = h_ctx + mc[2] * (y_ctx @ w_out[l])
            h_ctx = h_ctx + mc[5] * _conv_ffn(_modulate(h_ctx, norm2_w[l], mc[3], mc[4]),
                                              w_up[l], ffn_conv_w[l], w_down[l])
    return _rmsnorm(x, final_norm_w)


_drawn_inputs = setup_inputs


def setup_inputs(seed=0):
    import zlib

    import numpy as np

    out = dict(_drawn_inputs(seed))
    spreads = {}
    factors = {'norm1_w': 6.572,
     'norm2_w': 6.422,
     'dn_norm_w': 8.0,
     'na_rpb': 64.0,
     'df_lambda': 3.155,
     'df_norm_w': 64.0,
     'hg_lb_raw': 7.949,
     'hg_norm_w': 8.0,
     'final_norm_w': 8.055}
    for name, (base, spread) in spreads.items():
        noise = np.random.default_rng([zlib.crc32(name.encode()), seed]).standard_normal(out[name].shape)
        drawn = base * np.exp(spread * noise) if base else spread * noise
        out[name] = __import__('jax').numpy.asarray(drawn.astype(out[name].dtype))
    for name, factor in factors.items():
        out[name] = (out[name] * factor).astype(out[name].dtype)
    return out
```

```python
import math
from contextlib import ExitStack

import numpy as np

import concourse.bass as bass
from concourse import mybir

P = 128
DM = 1024
KT = DM // P
LAT, CTX = 512, 256
T = LAT + CTX
TT = T // P
CT = CTX // P
SEG = ((0, CTX), (CTX, T))
DEPTH = 2
GW = 256
HD = 64
NH = 4
CH = 64
DFF = 2816
FT = DFF // P
P_IN = 3856
EPS = 1e-6
LEVELS = 6
NEG = -1e30
GRID = 64

C_ID, C_MEAN, C_BLK, C_ROT = 0, 128, 256, 384
C_NEG = 512
C_INC = 768
C_AJ = 1024
C_NAM = 1278
C_CHK = 1342
C_EPS, C_ONE = 1344, 1345
C_COS, C_SIN, C_SCAN = 1346, 1858, 2370
NC_ = C_SCAN + T

W_N1, W_N2, W_BADA, W_DNC, W_FFC = 0, 8, 16, 64, 82
W_ALOG, W_DTB, W_DNN, W_DFN, W_HGN = 148, 156, 164, 228, 292
W_LAM, W_LB, W_RPB, W_BA = 356, 484, 492, 548
NW = W_BA + KT * 16
COL = dict(dnq=0, dnk=256, dnv=512, dng=768, naq=1040, nak=1296, nav=1552, dfq=1808, dfk=2064,
           dfv=2320, hgq=2576, hgv=2832, hgf=3088, hgb=3344, hgg=3600)
COL_BA = 1024


def shape_constants():
    c = np.zeros((P, NC_), np.float32)
    i = np.arange(P)
    c[:, C_ID:C_ID + P] = np.eye(P)
    c[:, C_MEAN:C_MEAN + P] = 1.0 / DM
    blk = (i[:, None] // CH) == (i[None, :] // CH)
    c[:, C_BLK:C_BLK + P] = blk
    for m in range(P):
        first = m % 16 < 8
        c[m + 8 if first else m - 8, C_ROT + m] = -1.0 if first else 1.0
    for d in range(2):
        inc = blk & ((i[:, None] <= i[None, :]) if d == 0 else (i[:, None] >= i[None, :]))
        c[:, C_NEG + d * P:C_NEG + (d + 1) * P] = np.where(inc, 0.0, NEG)
        c[:, C_INC + d * P:C_INC + (d + 1) * P] = inc
    for b in range(2):
        for dl in range(31):
            c[32 * b + dl, C_AJ + 64 * b + 78 - dl] = 1.0
    q = i % GRID
    start = np.clip(q - 8, 0, GRID - 16)
    k = np.arange(GRID)
    c[:, C_NAM:C_NAM + GRID] = np.where((k >= start[:, None]) & (k < start[:, None] + 16), 0.0, NEG)
    c[:, C_CHK] = i < CH
    c[:, C_CHK + 1] = i >= CH
    c[:, C_EPS] = EPS
    c[:, C_ONE] = 1.0
    t = np.arange(LAT)
    inv = (1.0 / (np.float32(10000.0) ** (np.arange(0, 16, 2, dtype=np.float32) / np.float32(16)))).astype(np.float32)
    for p in range(P):
        pos = (t // GRID if p % 32 < 16 else t % GRID).astype(np.float32)
        ang = pos * inv[p % 8]
        c[p, C_COS:C_COS + LAT] = np.cos(ang)
        c[p, C_SIN:C_SIN + LAT] = np.sin(ang)
    c[:, C_SCAN:C_SCAN + T] = (np.arange(T) % CH != 0)
    m = np.zeros((2, LEVELS + 1, P, P), np.float32)
    for d in range(2):
        m[d, 0] = np.eye(P)
        for lv in range(1, LEVELS + 1):
            s = 1 << (lv - 1)
            same = (i[:, None] // (2 * s)) == (i[None, :] // (2 * s))
            right = (i // s) % 2 == 1
            row, col = (~right, right) if d == 0 else (right, ~right)
            m[d, lv] = same & row[:, None] & col[None, :]
    return c, np.ascontiguousarray(m.transpose(2, 0, 1, 3).reshape(P, -1))


def lay_out(a):
    f = np.float32
    out = {}
    x = np.concatenate([np.asarray(a["ctx"])[0], np.asarray(a["x"])[0]], 0)
    out["x"] = x.T.reshape(KT, P, T).transpose(1, 0, 2).reshape(P, -1)
    both = np.stack([np.asarray(a["c_ctx"]), np.asarray(a["c"])[0]]).reshape(1, -1)
    out["c"] = np.repeat(both, P, 0)
    w = np.asarray(a["w_ada"]).reshape(DEPTH, DM, 24, 2, P)
    out["ada"] = w.transpose(0, 2, 4, 3, 1).reshape(DEPTH, 24, P, 2 * DM)
    w_in = np.asarray(a["w_in"])
    cut = [w_in[:, :, o:o + GW] for o in COL.values()]
    out["win"] = np.stack(cut, 1).reshape(DEPTH, 15, KT, P, GW).transpose(0, 1, 3, 2, 4).reshape(DEPTH, 15, P, -1)
    out["wout"] = np.asarray(a["w_out"]).reshape(DEPTH, KT, P, 4, GW).transpose(0, 3, 2, 1, 4).reshape(DEPTH, 4, P, -1)
    out["wup"] = np.asarray(a["w_up"]).reshape(DEPTH, KT, P, 22, GW).transpose(0, 3, 2, 1, 4).reshape(DEPTH, 22, P, -1)
    out["wdn"] = np.asarray(a["w_down"]).reshape(DEPTH, FT, P, KT, P).transpose(0, 3, 2, 1, 4).reshape(DEPTH, KT, P, -1)
    s = np.zeros((DEPTH, P, NW), f)
    vec = lambda v, n: np.asarray(v).reshape(DEPTH, n, P).transpose(0, 2, 1)
    s[:, :, W_N1:W_N1 + 8] = vec(a["norm1_w"], 8)
    s[:, :, W_N2:W_N2 + 8] = vec(a["norm2_w"], 8)
    s[:, :, W_BADA:W_BADA + 48] = vec(a["b_ada"], 48)
    s[:, :, W_DNC:W_DNC + 18] = np.asarray(a["dn_conv_w"]).reshape(DEPTH, 3, 6, P).transpose(0, 3, 2, 1).reshape(DEPTH, P, 18)
    s[:, :, W_FFC:W_FFC + 66] = np.asarray(a["ffn_conv_w"]).reshape(DEPTH, 3, FT, P).transpose(0, 3, 2, 1).reshape(DEPTH, P, 66)
    s[:, :, W_ALOG:W_ALOG + 8] = np.asarray(a["dn_a_log"]).reshape(DEPTH, 1, 8)
    s[:, :, W_DTB:W_DTB + 8] = np.asarray(a["dn_dt_bias"]).reshape(DEPTH, 1, 8)
    s[:, :, W_DNN:W_DNN + 64] = np.asarray(a["dn_norm_w"])[:, None, :]
    s[:, :, W_DFN:W_DFN + 64] = np.asarray(a["df_norm_w"])[:, None, :]
    s[:, :, W_HGN:W_HGN + 64] = np.asarray(a["hg_norm_w"])[:, None, :]
    s[:, :, W_LAM:W_LAM + 128] = np.asarray(a["df_lambda"]).reshape(DEPTH, 1, 128)
    lb = np.asarray(a["hg_lb_raw"]).reshape(DEPTH, 2, 2, P).transpose(3, 0, 1, 2).reshape(P, 8)
    s[:, :, W_LB:W_LB + 8] = lb
    rpb = np.asarray(a["na_rpb"])
    for b in range(2):
        r = rpb[:, :, 1 - b:15 - b, :].transpose(0, 3, 1, 2).reshape(DEPTH, 31, 56)
        s[:, 32 * b:32 * b + 31, W_RPB:W_RPB + 56] = r
    s[:, :, W_BA:] = w_in[:, :, COL_BA:COL_BA + 16].reshape(DEPTH, KT, P, 16).transpose(0, 2, 1, 3).reshape(DEPTH, P, -1)
    out["small"] = s
    out["fin"] = np.asarray(a["final_norm_w"]).reshape(KT, P).T
    out["const"], out["masks"] = shape_constants()
    return {k: np.ascontiguousarray(v) for k, v in out.items()}


INPUTS = ["x", "c", "ada", "win", "wout", "wup", "wdn", "small", "fin", "const", "masks"]


def schedule():
    steps, units = [], []

    def unit(**u):
        u["n"] = len(units)
        units.append(u)
        steps.append(("unit", u))

    def group(l, g):
        names = [["dnq", "dnk", "dnv", "dng"], ["hgf", "hgb", "hgq", "hgv", "hgg"],
                 ["naq", "nak", "nav"], ["dfq", "dfk", "dfv"]][g]
        return l, g, names

    def emit_group(l, g, names):
        base = (g % 2) * ZG
        fm, tm = 0, 0
        for name in names:
            last = l == DEPTH - 1
            if name in ("dng", "hgg", "nav", "dfv", "hgv"):
                t0 = CT if last and name in ("dng", "hgg") else 0
                unit(kind="tm", l=l, col=list(COL).index(name), z=base + 6 * T + tm * TT * GW, t0=t0)
                tm += 1
            else:
                segs = SEG[1:] if last and name in ("naq", "dfq") else SEG
                scale = {"naq": HD ** -0.5, "dfq": 32 ** -0.5, "hgq": HD ** -0.5}.get(name, 1.0)
                unit(kind="fm", l=l, col=list(COL).index(name), z=base + FMPOS[name] * T, segs=segs, scale=scale)
                fm += 1
        if g == 0:
            unit(kind="ba", l=l)

    for l in range(DEPTH):
        last = l == DEPTH - 1
        segs = SEG[1:] if last else SEG
        if l == 0:
            for u in range(8):
                unit(kind="ada", l=0, u=u)
        steps.append(("norm", l, 0, SEG))
        rest = [(0, u) for u in range(8, 24)] if l == 0 else []
        for g in range(4):
            emit_group(*group(l, g))
            for _ in range(4):
                if rest:
                    la, u = rest.pop(0)
                    unit(kind="ada", l=la, u=u)
            steps.append((("dn", "hg", "na", "df")[g], l))
        for u in range(4):
            unit(kind="out", l=l, u=u, segs=segs)
        steps.append(("norm", l, 1, segs))
        rest = [(1, u) for u in range(24)] if l == 0 else []
        pair = 0
        for part, (a, b) in enumerate(PARTS):
            for u in range(a // 2, b // 2):
                unit(kind="upg", l=l, u=u, part=part, segs=segs)
                unit(kind="upv", l=l, u=u, part=part, segs=segs)
                for _ in range(3 if u % 2 else 2):
                    if rest:
                        la, ua = rest.pop(0)
                        unit(kind="ada", l=la, u=ua)
            for m in range(KT):
                unit(kind="down", l=l, m=m, part=part, segs=segs)
    steps.append(("norm", DEPTH, 0, SEG[1:]))
    return steps, units


FMPOS = dict(dnq=0, dnk=1 * 2, dnv=2 * 2, hgq=0, hgf=2, hgb=4, naq=0, nak=2, dfq=0, dfk=2)
ZG = 6 * T + 2 * TT * GW
PARTS = ((0, 12), (12, 22))
SLOT = KT * GW
SLOTS = 3


def bank_table(units):
    banks, turns = [], {"act": 0, "dve": 0}
    for u in units:
        u["banks"] = []
        k = u["kind"]
        if k == "ada":
            continue
        if k == "tm":
            outs = [("act", (t, t + 1)) for t in range(u["t0"], TT, 2)]
        elif k == "ba":
            outs = [("act", None)]
        elif k == "fm":
            outs = [("act", (f, s)) for f in range(2) for s in u["segs"]]
        elif k in ("out", "upv"):
            outs = [("dve", (f, s)) for f in range(2) for s in u["segs"]]
        elif k == "upg":
            outs = [("act", (f, s)) for f in range(2) for s in u["segs"]]
        else:
            outs = [("dve", (0, s)) for s in u["segs"]]
        for who, what in outs:
            turns[who] += 1
            b = dict(n=len(banks), who=who, turn=turns[who], what=what)
            u["banks"].append(b)
            banks.append(b)
    return banks


DN_PE = ["tr", "R", "kb", "kk", "kq", "N"] + [f"{x}{i}" for i in range(5) for x in "XY"] + \
        [f"{x}{j}" for j in range(2) for x in "KVO"]
DN_ACT = ["init", "kbT", "exp"] + [f"X{i}" for i in range(5)] + ["V0", "V1"]
DN_DVE = ["kb", "R", "NT", "at", "M"] + [f"L{i}" for i in range(5)] + ["R0", "S0", "R1", "S1", "O"]
HG_PE = ["T"] + [f"L{i}" for i in range(7)] + ["C0", "C1"]
HG_ACT = ["E", "T"]
HG_DVE = ["D", "E", "M1", "M2", "M3", "P0", "M4", "P1", "M5", "P2", "M6", "P3", "P4", "P5", "P6", "U0", "U1", "O"]


class Turns:

    def __init__(self, chain):
        self.chain, self.counts, self.last = chain, {}, None

    def __call__(self, sem=None):
        sem = self.chain if sem is None else sem
        self.counts[sem.name] = self.counts.get(sem.name, 0) + 1
        self.last = (sem, self.counts[sem.name])
        return sem, 1


PR_PE = [f"n{i}" for i in range(4)] + ["cum"]
PR_ACT = [f"{x}{i}" for i in range(6) for x in "ms"] + [f"{x}{i}" for i in range(4) for x in "qr"] + ["b1", "b2", "b3"]
PR_DVE = [f"c{i}" for i in range(6)] + [f"l{i}" for i in range(4)] + ["b1", "b2", "b3", "b4"]
HP_ACT = ["lb1", "lb2"] + [f"{x}{i}" for i in range(4) for x in "ek"]
HP_DVE = ["lb1", "lb2"] + [f"{x}{i}" for i in range(4) for x in "clb"]
DP_PE = [f"r{i}" for i in range(4)]
DP_DVE = ["d"] + [f"r{i}" for i in range(4)] + ["lam"]


def at(order, n, name):
    return n * len(order) + order.index(name) + 1


def at2(order, n, name, d):
    return 2 * (n * len(order) + order.index(name)) + d + 1


def hybrid_backbone(nc, A, out):
    fp32, bf16, u8 = mybir.dt.float32, mybir.dt.bfloat16, mybir.dt.uint8
    ALU = mybir.AluOpType
    ACT = mybir.ActivationFunctionType
    AX = mybir.AxisListType
    MUL, ADD, SUB, MAX, MIN = ALU.mult, ALU.add, ALU.subtract, ALU.max, ALU.min

    steps, units = schedule()
    banks = bank_table(units)
    del banks
    ctx = ExitStack()
    with ctx:
        def sb(name, cols, dt=fp32):
            return ctx.enter_context(nc.sbuf_tensor(name, [P, cols], dt))

        def sem(name):
            return ctx.enter_context(nc.semaphore(name))

        X = sb("residual", KT * T)
        H = sb("normed", KT * T)
        Y = sb("mixed", KT * T)
        Z = sb("projected", 2 * ZG)
        RING = sb("ring", SLOTS * SLOT)
        SC = sb("silu_c", 2 * DM)
        JUNK = sb("junk", DM, bf16)
        CST = sb("constants", NC_)
        MSK = sb("level_masks", 2 * (LEVELS + 1) * P, u8)
        SM = sb("small", DEPTH * NW)
        FIN = sb("final_w", KT)
        MOD = sb("modulation", DEPTH * 2 * 48)
        AB = sb("norm_gain", 5 * 2 * KT)
        LBV = sb("lower_bounds", 16)
        ST = sb("stats", 192)
        SCR = sb("scratch", 5120)
        PS = ctx.enter_context(nc.psum_tensor("psum", [P, 8 * 512], fp32))

        def bank(b, a=0, e=512):
            return PS[:, 512 * b + a:512 * b + e]

        def seg3(t, n, w=T):
            return t.rearrange("p (n w) -> p n w", n=n, w=w)

        Xv, Hv, Yv = seg3(X[:, :], KT), seg3(H[:, :], KT), seg3(Y[:, :], KT)
        IDN = CST[:, C_ID:C_ID + P]
        cc = lambda c, n=1: CST[:, c:c + n]
        sm = lambda l, c, n=1: SM[:, l * NW + c:l * NW + c + n]
        mod = lambda l, v, c, n=1: MOD[:, (2 * l + v) * 48 + c:(2 * l + v) * 48 + c + n]
        mask = lambda d, lv: MSK[:, ((LEVELS + 1) * d + lv) * P:((LEVELS + 1) * d + lv + 1) * P]
        h4 = lambda ap: ap.rearrange("p (h n) -> p h n", h=NH)
        four = lambda ap: ap[:, None, :].to_broadcast([ap.shape[0], NH, ap.shape[1]])

        loaded = sem("small_inputs_loaded")
        stored = sem("output_stored")
        arrived = [sem(f"weights_arrived_{i}") for i in range(SLOTS)]
        masks_ready = sem("level_masks_are_bytes")
        silu_ready = sem("silu_c_ready")
        ada_done = sem("ada_unit_done")
        gemm_ready = sem("gemm_bank_filled")
        gemm_act = sem("gemm_bank_emptied_by_act")
        gemm_dve = sem("gemm_bank_emptied_by_dve")
        sq_ready = sem("norm_square_ready")
        sq_used = sem("norm_square_summed")
        rstd_ready = sem("norm_rstd_ready")
        scaled = sem("norm_scaled")
        normed = sem("norm_shifted")
        conv_done = sem("ffn_conv_done")
        silu_done = sem("ffn_silu_done")
        prep_pe, prep_act, prep_dve = sem("prep_pe"), sem("prep_act"), sem("prep_dve")
        dn_pe, dn_act, dn_dve = sem("dn_pe"), sem("dn_act"), sem("dn_dve")
        hg_pe, hg_act, hg_dve = sem("hg_pe"), sem("hg_act"), sem("hg_dve")
        hp_act, hp_dve = sem("hg_prep_act"), sem("hg_prep_dve")
        dp_pe, dp_act, dp_dve = sem("df_prep_pe"), sem("df_prep_act"), sem("df_prep_dve")
        bias_pe, bias_dve = sem("na_bias_filled"), sem("na_bias_masked")
        at_s, at_max, at_exp, at_p = sem("at_scores"), sem("at_max"), sem("at_exp"), sem("at_probs")
        at_tr, at_pt, at_pv, at_o = sem("at_transposed"), sem("at_pt"), sem("at_pv"), sem("at_o")
        post_dve, post_act, post_pe, y_done = sem("post_dve"), sem("post_act"), sem("post_pe"), sem("y_tile_pair_done")
        pe_chain, act_chain, dve_chain = sem("pe_chain"), sem("act_chain"), sem("dve_chain")
        N_LOADS = 7

        release, nb, na = [], 0, 0
        ring_units = [u for u in units if u["kind"] != "ba"]
        for u in units:
            nb += len(u["banks"])
            if u["kind"] == "ada":
                na += 1
            if u["kind"] != "ba":
                u["r"] = len(release)
                release.append((ada_done, na) if u["kind"] == "ada" else (gemm_ready, nb))

        def slot(u, n=SLOT):
            o = (u["r"] % SLOTS) * SLOT
            return RING[:, o:o + n]

        def weights(u):
            return arrived[u["r"] % SLOTS], 16 * (u["r"] // SLOTS + 1)

        acts_before, dves_before = {}, {}
        turn = {"act": 0, "dve": 0}
        norms = pairs = pair = 0
        vals = []
        for st in steps:
            if st[0] == "unit":
                u = st[1]
                u["norms"], u["pairs"], u["acts"] = norms, pairs, turn["dve"]
                if u["kind"] == "upg":
                    u["pair"], u["vals2"] = pair, vals[-2] if pair >= 2 else 0
                for b in u["banks"]:
                    turn[b["who"]] = b["turn"]
                if u["kind"] == "upv":
                    u["pair"] = pair
                    pair += 1
                    vals.append(turn["dve"])
                if u["kind"] == "down" and u["m"]:
                    u["acts"] = part_acts
                else:
                    part_acts = u["acts"]
            elif st[0] == "norm":
                dves_before[norms] = turn["dve"]
                norms += 1
            else:
                acts_before[st] = turn["act"]
                pairs += (TT - (CT if st[1] == DEPTH - 1 else 0)) // 2

        ORD = ([0, 1, 2, 3, 4, 5], [1, 0, 5, 4, 3, 2])

        YS = 2 * T
        def dn_buf(d, name, n):
            off = dict(kb=0, rhs=0, kbT=256, vn=256, vb=512, kdec=768, D=1024, X=1024, t=1024, NT=1536,
                       at=2048, Tm=2560, TTm=3072)[name]
            return Y[:, YS + off:YS + off + n] if d == 0 else SCR[:, 1536 + off:1536 + off + n]
        O = SCR[:, 0:TT * GW]
        DNS = [Y[:, YS + 3584 + 128 * d:YS + 3712 + 128 * d] for d in range(2)]
        BAO = YS + 3840
        ba = lambda i: Y[:, BAO + 48 * i:BAO + 48 * (i + 1)]
        BETA, NBETA, LOGA, G, EG, EDEC, NEGB, TOT, EGL = 2, 3, 4, 5, 6, 7, 8, 9, 10
        PRB = SCR[:, 1536:1536 + 3 * T]
        FFG = [Y[:, p * 2 * T:(p + 1) * 2 * T] for p in range(2)]
        FFC = [Y[:, (p + 2) * 2 * T:(p + 3) * 2 * T] for p in range(2)]
        NSQ = [SCR[:, p * T:(p + 1) * T] for p in range(2)]
        RSTD = SCR[:, 2 * T:3 * T]
        HB = lambda d, f: Y[:, (2 + 2 * d + f) * T:(3 + 2 * d + f) * T]
        HE = Y[:, 6 * T:8 * T].rearrange("p (l n) -> p l n", l=LEVELS)
        QKT = [SCR[:, 1536 + 512 * i:2048 + 512 * i] for i in range(3)]
        ATT = SCR[:, 3072:3584]
        HQB, HKE, HKT = SCR[:, 3584:3840], SCR[:, 3840:4096], SCR[:, 4096:4352]
        HGS = [SCR[:, 4352 + 128 * d:4480 + 128 * d] for d in range(2)]
        HDE = ST[:, 96:100]
        NAB = SCR[:, 1536:3328]
        NPT = [SCR[:, 3328 + T * i:3328 + T * (i + 1)] for i in range(2)]
        NP_ = [Y[:, (4 + i) * T:(5 + i) * T] for i in range(2)]
        DPP = [SCR[:, 1536 + 1536 * i:3072 + 1536 * i] for i in range(2)]
        DPT = [Y[:, (4 + i) * T:(5 + i) * T] for i in range(2)]

        region = {"dn": 0, "hg": ZG, "na": 0, "df": ZG}
        fm = lambda g, f: Z[:, region[g] + f * T:region[g] + (f + 1) * T]
        tm = lambda g, i: Z[:, region[g] + 6 * T + i * TT * GW:region[g] + 6 * T + (i + 1) * TT * GW]

        items = {}
        n_items = 0
        for st in steps:
            if st[0] in ("na", "df"):
                l = st[1]
                qt = range(CT if l == DEPTH - 1 else 0, TT)
                items[st] = (n_items, [(h, t) for h in range(NH) for t in qt])
                n_items += len(items[st][1])
        posts, n_norm, n_pair = {}, 0, 0
        mixers = [st for st in steps if st[0] in ("dn", "hg", "na", "df")]
        for st in mixers:
            t0 = CT if st[1] == DEPTH - 1 else 0
            posts[st] = (n_norm, n_pair, t0)
            n_norm += st[0] != "na"
            n_pair += (TT - t0) // 2
        YT = {"dn": 0, "na": 2, "df": 4, "hg": 6}
        before = {st: sum((TT - posts[m][2]) // 2 for m in mixers[:i]) for i, st in enumerate(mixers)}
        norm_at = [st for st in steps if st[0] == "norm"]
        block = ctx.enter_context(nc.Block())

        @block.sync
        def _(sp):
            for dst, src in ((CST[:, :], A["const"]), (SC[:, :], A["c"]), (Z[:, 0:2 * (LEVELS + 1) * P], A["masks"]), (FIN[:, :], A["fin"])):
                sp.dma_start(dst, src[:, :]).then_inc(loaded, 16)
            for l in range(DEPTH):
                sp.dma_start(SM[:, l * NW:(l + 1) * NW], A["small"][l]).then_inc(loaded, 16)
            sp.dma_start(X[:, :], A["x"][:, :]).then_inc(loaded, 16)
            for r, u in enumerate(ring_units):
                if r >= SLOTS:
                    sp.wait_ge(*release[r - SLOTS])
                k, l = u["kind"], u["l"]
                n = SLOT
                if k == "ada":
                    src = A["ada"][l, u["u"]]
                elif k in ("fm", "tm"):
                    src = A["win"][l, u["col"]]
                elif k == "out":
                    src = A["wout"][l, u["u"]]
                elif k in ("upg", "upv"):
                    src = A["wup"][l, u["u"] + (0 if k == "upg" else FT // 2)]
                else:
                    a, b = PARTS[u["part"]]
                    n = (b - a) * P
                    src = A["wdn"][l, u["m"]][:, a * P:b * P]
                sp.dma_start(slot(u, n), src).then_inc(arrived[r % SLOTS], 16)
            sp.wait_ge(scaled, KT * len(norm_at))
            sp.dma_start(out[:, :, :], Hv[:, :, CTX:T]).then_inc(stored, 16)
            sp.wait_ge(stored, 16)

        @block.tensor
        def _(pe):
            own = Turns(pe_chain)
            mm, tr = nc.tensor.matmul, nc.tensor.transpose
            emptied = []

            def gemm_unit(u):
                k, l = u["kind"], u["l"]
                if k == "ada":
                    return
                if k != "ba":
                    pe.wait_ge(*weights(u))
                if k in ("fm", "tm", "ba", "upg", "upv"):
                    pe.wait_ge(normed, KT * u["norms"])
                if k == "out":
                    pe.wait_ge(y_done, u["pairs"])
                if k == "down":
                    pe.wait_ge(gemm_dve, u["acts"])
                for b in u["banks"]:
                    if len(emptied) >= 2:
                        pe.wait_ge(*emptied[-2])
                    emptied.append((gemm_act if b["who"] == "act" else gemm_dve, b["turn"]))
                    ps = bank(b["n"] % 2)
                    if k == "tm":
                        for i, t in enumerate(b["what"]):
                            for kk in range(KT):
                                last = mm(ps[:, i * GW:(i + 1) * GW], Hv[:, kk, t * P:(t + 1) * P],
                                          slot(u)[:, kk * GW:(kk + 1) * GW], start=kk == 0, stop=kk == KT - 1)
                    elif k == "ba":
                        for t in range(TT):
                            for kk in range(KT):
                                last = mm(ps[:, t * 16:(t + 1) * 16], Hv[:, kk, t * P:(t + 1) * P],
                                          sm(l, W_BA + kk * 16, 16), start=kk == 0, stop=kk == KT - 1)
                    else:
                        f, (a, e) = b["what"]
                        if k == "down":
                            p0, p1 = PARTS[u["part"]]
                            nk, src, step = p1 - p0, Z, P
                        else:
                            nk, src, step = KT, (Y if k == "out" else H), GW
                        for kk in range(nk):
                            o = kk * step + f * P
                            last = mm(ps[:, 0:e - a], slot(u)[:, o:o + P], src[:, kk * T + a:kk * T + e],
                                      start=kk == 0, stop=kk == nk - 1)
                    last.then_inc(*own(gemm_ready))

            def norm(ni, segs):
                pe.wait_ge(rstd_ready, ni)
                for k in range(KT):
                    pe.wait_ge(sq_ready, KT * ni + k + 1)
                    for i, (a, e) in enumerate(segs):
                        last = mm(bank(2 + i, 0, e - a), cc(C_MEAN, P), NSQ[k % 2][:, a:e],
                                  start=k == 0, stop=k == KT - 1)
                    last.then_inc(*own(sq_used))

            def dn(l):
                for i in range(4):
                    pe.wait_ge(prep_act, at(PR_ACT, l, f"q{i}"))
                    mm(bank(2, 0, CTX), cc(C_BLK, P), PRB[:, (i % 2) * T:(i % 2) * T + CTX], start=True, stop=True)
                    mm(bank(3), cc(C_BLK, P), PRB[:, (i % 2) * T + CTX:(i % 2 + 1) * T], start=True, stop=True).then_inc(*own(prep_pe))
                pe.wait_ge(prep_dve, at(PR_DVE, l, "b2"))
                LG = ba(LOGA).rearrange("p (t d h) -> p t d h", t=TT, d=2)
                gp = bank(4, 0, 48).rearrange("p (t d h) -> p t d h", t=TT, d=2)
                for d in range(2):
                    mm(gp[:, :, d, :], cc(C_INC + d * P, P), LG[:, :, d, :], start=True, stop=True)
                mm(bank(4, 48, 96), cc(C_BLK, P), ba(LOGA), start=True, stop=True)
                for t in range(TT):
                    for d in range(2):
                        for hp in range(2):
                            o = 96 + ((t * 2 + d) * 2 + hp) * 2
                            for h in range(2):
                                last = mm(bank(4, o, o + 2)[64 * h:64 * h + 64, :],
                                          LG[:, t, d, 2 * hp + h:2 * hp + h + 1].to_broadcast([P, HD]),
                                          cc(C_CHK, 2), start=True, stop=True)
                last.then_inc(*own(prep_pe))
                pe.wait_ge(prep_dve, at(PR_DVE, l, "b4"))
                pe.wait_ge(prep_act, at(PR_ACT, l, "b3"))
                for n in range(TT):
                    g = TT * l + n
                    A, B, C = [bank(2), bank(5)], [bank(3), bank(6)], [bank(4), bank(7)]
                    tile = [ORD[d][n] for d in range(2)]
                    cols = [slice(t * P, (t + 1) * P) for t in tile]

                    def done(ins):
                        ins.then_inc(*own(dn_pe))

                    def by_rows(product):
                        for odd in range(2):
                            if odd:
                                last.then_inc(*own())
                                pe.wait_ge(*own.last)
                            for h in (odd, odd + 2):
                                last = product(h, slice(64 * odd, 64 * odd + 64))
                        done(last)

                    for d in range(2):
                        if g:
                            pe.wait_ge(dn_dve, at2(DN_DVE, g - 1, "O", d))
                        for i, f in enumerate((2, 3, 4, 5)):
                            last = tr(A[d][:, i * P:(i + 1) * P], fm("dn", f)[:, cols[d]], IDN)
                        done(last)
                    for d in range(2):
                        for h in range(NH):
                            last = mm(C[d][:, h * P:(h + 1) * P], LG[:, tile[d], d, h:h + 1].to_broadcast([P, P]),
                                      cc(C_INC + d * P, P), start=True, stop=True)
                        done(last)
                    for d in range(2):
                        pe.wait_ge(dn_dve, at2(DN_DVE, g, "kb", d))
                        for i in range(2):
                            last = tr(B[d][:, i * P:(i + 1) * P], dn_buf(d, "kb", 256)[:, i * P:(i + 1) * P], IDN)
                        done(last)
                    for d in range(2):
                        pe.wait_ge(dn_act, at2(DN_ACT, g, "kbT", d))
                        by_rows(lambda h, r: mm(
                            A[d][:, h * P:(h + 1) * P], fm("dn", 2 + h // 2)[r, cols[d]],
                            dn_buf(d, "kbT", 256)[r, (h // 2) * P:(h // 2 + 1) * P], start=True, stop=True))
                    for d in range(2):
                        by_rows(lambda h, r: mm(
                            B[d][:, h * P:(h + 1) * P], fm("dn", 2 + h // 2)[r, cols[d]],
                            fm("dn", h // 2)[r, cols[d]], start=True, stop=True))
                    for d in range(2):
                        pe.wait_ge(dn_dve, at2(DN_DVE, g, "NT", d))
                        for h in range(NH):
                            last = tr(C[d][:, h * P:(h + 1) * P], dn_buf(d, "NT", 512)[:, h * P:(h + 1) * P], IDN)
                        done(last)
                    for i in range(5):
                        for d in range(2):
                            pe.wait_ge(dn_dve, at2(DN_DVE, g, "M" if i == 0 else f"L{i - 1}", d))
                            if i < 5:
                                for h in range(NH):
                                    hs = slice(h * P, (h + 1) * P)
                                    last = mm(A[d][:, hs], dn_buf(d, "NT", 512)[:, hs], dn_buf(d, "Tm", 512)[:, hs],
                                              start=True, stop=True)
                            done(last)
                        for d in range(2):
                            pe.wait_ge(dn_act, at2(DN_ACT, g, f"X{i}", d))
                            for h in range(NH):
                                hs = slice(h * P, (h + 1) * P)
                                last = mm(B[d][:, hs], dn_buf(d, "X", 512)[:, hs], dn_buf(d, "TTm", 512)[:, hs],
                                          start=True, stop=True)
                            if i < 4:
                                for h in range(NH):
                                    hs = slice(h * P, (h + 1) * P)
                                    last = mm(C[d][:, hs], dn_buf(d, "TTm", 512)[:, hs], dn_buf(d, "X", 512)[:, hs],
                                              start=True, stop=True)
                            done(last)
                    for j in range(2):
                        for d in range(2):
                            pe.wait_ge(dn_dve, at2(DN_DVE, g, "L4" if j == 0 else "S0", d))
                            c = j if d == 0 else 1 - j
                            rows = slice(64 * c, 64 * c + 64)
                            t0 = tile[d] * P + 64 * c

                            def read(h, r):
                                for w in range(2):
                                    f = (2 if w == 0 else 0) + h // 2
                                    o = w * GW + h * HD
                                    last = mm(A[d][rows, o:o + HD], fm("dn", f)[r, t0:t0 + 64],
                                              DNS[d][r, (h // 2) * HD:(h // 2 + 1) * HD], start=True, stop=True)
                                return last
                            by_rows(read)
                        for d in range(2):
                            pe.wait_ge(dn_dve, at2(DN_DVE, g, f"R{j}", d))
                            c = j if d == 0 else 1 - j
                            rows = slice(64 * c, 64 * c + 64)
                            for h in range(NH):
                                last = mm(B[d][rows, h * HD:(h + 1) * HD],
                                          dn_buf(d, "TTm", 512)[rows, h * P + 64 * c:h * P + 64 * c + 64],
                                          dn_buf(d, "rhs", 256)[rows, h * HD:(h + 1) * HD], start=True, stop=True)
                            done(last)
                        for d in range(2):
                            pe.wait_ge(dn_act, at2(DN_ACT, g, f"V{j}", d))
                            c = j if d == 0 else 1 - j
                            rows = slice(64 * c, 64 * c + 64)
                            vn = dn_buf(d, "vn", 256)
                            for h in range(NH):
                                r = slice(64 * (h % 2), 64 * (h % 2) + 64)
                                mm(B[d][r, 256 + (h // 2) * HD:256 + (h // 2 + 1) * HD],
                                   dn_buf(d, "kdec", 256)[rows, h * HD:(h + 1) * HD], vn[rows, h * HD:(h + 1) * HD],
                                   start=True, stop=True)
                            for h in range(NH):
                                last = mm(C[d][rows, h * HD:(h + 1) * HD],
                                          dn_buf(d, "at", 512)[rows, h * P + 64 * c:h * P + 64 * c + 64],
                                          vn[rows, h * HD:(h + 1) * HD], start=True, stop=True)
                            done(last)

            def hg(l):
                pe.wait_ge(hp_dve, at(HP_DVE, l, "b3"))
                pe.wait_ge(hp_act, at(HP_ACT, l, "k3"))
                for n in range(TT):
                    for d in range(2):
                        q = 2 * (TT * l + n) + d
                        t = ORD[d][n]
                        cs = slice(t * P, (t + 1) * P)
                        pe.wait_ge(hg_dve, at(HG_DVE, q, "E"))
                        if q:
                            pe.wait_ge(hg_act, at(HG_ACT, q - 1, "T"))
                        for i in range(2):
                            last = tr(bank(2, i * P, (i + 1) * P), HKE[:, i * P:(i + 1) * P], IDN)
                        last.then_inc(*own(hg_pe))
                        for lv in range(LEVELS + 1):
                            if lv:
                                pe.wait_ge(hg_dve, at(HG_DVE, q, f"M{lv}"))
                            b = 3 + lv % 3
                            if lv >= 3:
                                pe.wait_ge(hg_dve, at(HG_DVE, q, f"P{lv - 3}"))
                            elif q:
                                pe.wait_ge(hg_dve, at(HG_DVE, q - 1, "P6"))
                            for h in (0, 2, 1, 3):
                                r = slice(64 * (h % 2), 64 * (h % 2) + 64)
                                f = h // 2
                                if h == 1:
                                    last.then_inc(*own())
                                    pe.wait_ge(*own.last)
                                if lv == 0:
                                    kk, qq = fm("hg", 2 + 2 * d + f)[r, cs], fm("hg", f)[r, cs]
                                else:
                                    w = QKT[lv % 3]
                                    qq, kk = w[r, f * P:(f + 1) * P], w[r, 256 + f * P:256 + (f + 1) * P]
                                last = mm(bank(b, h * P, (h + 1) * P), kk, qq, start=True, stop=True)
                            last.then_inc(*own(hg_pe))
                        for j in range(2):
                            c = j if d == 0 else 1 - j
                            rows = slice(64 * c, 64 * c + 64)
                            pe.wait_ge(hg_dve, at(HG_DVE, q, "P6" if j == 0 else "U0"))
                            pe.wait_ge(hg_act, at(HG_ACT, q, "T"))
                            if q:
                                pe.wait_ge(hg_dve, at(HG_DVE, q - 1, "O"))
                            v = tm("hg", 0)[:, t * GW:(t + 1) * GW]
                            for h in range(NH):
                                hc = slice(h * HD, (h + 1) * HD)
                                last = mm(bank(6)[rows, hc], ATT[rows, h * P + 64 * c:h * P + 64 * c + 64], v[rows, hc],
                                          start=h == 0, stop=False, skip_group_check=True)
                            for h in (0, 2, 1, 3):
                                r = slice(64 * (h % 2), 64 * (h % 2) + 64)
                                f = h // 2
                                hc = slice(h * HD, (h + 1) * HD)
                                if h < 2:
                                    last.then_inc(*own())
                                    pe.wait_ge(*own.last)
                                last = mm(bank(6)[rows, hc], HQB[r, f * P + 64 * c:f * P + 64 * c + 64],
                                          HGS[d][r, f * HD:(f + 1) * HD], start=False, stop=True, skip_group_check=True)
                            for h in range(NH):
                                r = slice(64 * (h % 2), 64 * (h % 2) + 64)
                                f = h // 2
                                hc = slice(h * HD, (h + 1) * HD)
                                last = mm(bank(7)[r, f * HD:(f + 1) * HD], HKT[rows, hc], v[rows, hc], start=True, stop=True)
                            last.then_inc(*own(hg_pe))

            def attend(st):
                kind, l = st
                i0, todo = items[st]
                na = kind == "na"
                v = tm(kind, 0)
                SB = [bank(2, 0, 512), bank(4, 0, 512)]
                tr_b, pv_b = PS[:, 6 * 512:6 * 512 + T], bank(7, 256, 256 + HD)

                def scores(i):
                    h, t = todo[i]
                    g = i0 + i
                    f = h // 2
                    for j in range(1 if na else 2):
                        pair = (g % 2 if na else j)
                        if na:
                            if i >= 2:
                                pe.wait_ge(at_exp, g - 1)
                            if h % 2 == 0 and (i == 0 or todo[i - 1][0] != h):
                                pe.wait_ge(bias_dve, 4 * (2 * l + h // 2) + 4)
                            r = slice(64 * (h % 2), 64 * (h % 2) + 64)
                        else:
                            if i:
                                pe.wait_ge(at_exp, g)
                            s = 64 * (h % 2) + 32 * j
                            r = slice(s, s + 32)
                        qq = fm(kind, f)[r, t * P:(t + 1) * P]
                        kk = fm(kind, 2 + f)
                        b0 = 512 * (2 + 2 * pair)
                        if t >= CT:
                            mm(PS[:, b0:b0 + LAT], qq, kk[r, CTX:T], start=True, stop=True)
                        last = mm(PS[:, b0 + LAT:b0 + T], qq, kk[r, 0:CTX], start=True, stop=True)
                    last.then_inc(*own(at_s))

                def values(i):
                    h, t = todo[i]
                    g = i0 + i
                    prob = NP_[g % 2] if na else DPP[g % 2][:, 0:T]
                    pt = NPT[g % 2] if na else DPT[g % 2]
                    pe.wait_ge(at_p, g + 1)
                    pe.wait_ge(at_o, g)
                    kts = [(o, (o + CT) if o < 4 else o - 4) for o in (range(6) if t >= CT else (4, 5))]
                    for o, _t in kts:
                        last = tr(tr_b[:, o * P:(o + 1) * P], prob[:, o * P:(o + 1) * P], IDN)
                    last.then_inc(*own(at_tr))
                    pe.wait_ge(at_pt, g + 1)
                    for o, kt in kts:
                        last = mm(pv_b, pt[:, o * P:(o + 1) * P], v[:, kt * GW + h * HD:kt * GW + (h + 1) * HD],
                                  start=o == kts[0][0], stop=o == kts[-1][0])
                    last.then_inc(*own(at_pv))

                for i in range(len(todo) + 1):
                    if na and i < len(todo) and todo[i][0] % 2 == 0 and (i == 0 or todo[i - 1][0] != todo[i][0]):
                        if i:
                            values(i - 1)
                        hp = todo[i][0] // 2
                        for rnd in range(4):
                            gi = 4 * (2 * l + hp) + rnd
                            if i or rnd:
                                pe.wait_ge(at_exp, i0 + i)
                            if rnd >= 2:
                                pe.wait_ge(bias_dve, gi - 1)
                            for k in range(16):
                                s = 63 - (rnd * 16 + k)
                                last = mm(bank(2 + 2 * (rnd % 2), k * 28, (k + 1) * 28),
                                          CST[0:64, C_AJ + s:C_AJ + s + P],
                                          SM[0:64, l * NW + W_RPB + hp * 28:l * NW + W_RPB + (hp + 1) * 28],
                                          start=True, stop=True)
                            last.then_inc(*own(bias_pe))
                        scores(i)
                        continue
                    if i < len(todo):
                        scores(i)
                    if i:
                        values(i - 1)

            def df(st):
                l = st[1]
                for i in range(4):
                    mm(bank(2 + i), cc(C_ROT, P), fm("df", i)[:, CTX:T], start=True, stop=True).then_inc(*own(dp_pe))
                pe.wait_ge(dp_dve, at(DP_DVE, l, "lam"))
                attend(st)

            def post(st):
                _, p0, t0 = posts[st]
                if st[0] != "na":
                    pe.wait_ge(post_dve, 2 * (posts[st][0] + 1))
                else:
                    pe.wait_ge(at_o, items[st][0] + len(items[st][1]))
                for i, t in enumerate(range(t0, TT, 2)):
                    b = 2 + i
                    for f in range(2):
                        for k in range(2):
                            o = f * GW + k * P
                            last = tr(bank(b, o, o + P), O[:, (t + k) * GW + f * P:(t + k) * GW + (f + 1) * P], IDN)
                    last.then_inc(*own(post_pe))

            pe.wait_ge(loaded, 16 * N_LOADS)
            for st in steps:
                kind = st[0]
                if kind == "unit":
                    gemm_unit(st[1])
                elif kind == "norm":
                    norm(norm_at.index(st), st[3])
                else:
                    pe.wait_ge(gemm_act, acts_before[st])
                    pe.wait_ge(y_done, before[st])
                    if kind == "dn":
                        dn(st[1])
                    elif kind == "hg":
                        hg(st[1])
                    elif kind == "na":
                        attend(st)
                    else:
                        df(st)
                    post(st)

        @block.scalar
        def _(act):
            own = Turns(act_chain)
            af = nc.scalar.activation
            eps, one = cc(C_EPS), cc(C_ONE)

            def gemm_unit(u):
                k, l = u["kind"], u["l"]
                for b in u["banks"]:
                    if b["who"] != "act":
                        continue
                    act.wait_ge(gemm_ready, b["n"] + 1)
                    ps = bank(b["n"] % 2)
                    if k == "ba":
                        af(Y[:, BAO:BAO + 96], ps[:, 0:96], ACT.Copy).then_inc(*own(gemm_act))
                    elif k == "tm":
                        t = b["what"][0]
                        o = u["z"] + t * GW
                        af(Z[:, o:o + 2 * GW], ps, ACT.Copy).then_inc(*own(gemm_act))
                    elif k == "fm":
                        f, (a, e) = b["what"]
                        o = u["z"] + f * T
                        af(Z[:, o + a:o + e], ps[:, 0:e - a], ACT.Copy, scale=u["scale"]).then_inc(*own(gemm_act))
                    else:
                        f, (a, e) = b["what"]
                        p = u["pair"]
                        if p >= 2:
                            act.wait_ge(conv_done, p - 1)
                            act.wait_ge(gemm_dve, u["vals2"])
                        af(FFG[p % 2][:, f * T + a:f * T + e], ps[:, 0:e - a], ACT.Copy).then_inc(*own())
                        w1 = sm(l, W_FFC + (2 * u["u"] + f) * 3 + 1)
                        af(FFC[p % 2][:, f * T + a:f * T + e], ps[:, 0:e - a], ACT.Copy, scale=w1).then_inc(*own(gemm_act))
                if k == "upv":
                    p = u["pair"]
                    act.wait_ge(conv_done, p + 1)
                    a = u["segs"][0][0]
                    v = seg3(FFC[p % 2], 2)[:, :, a:T]
                    af(v, v, ACT.Silu).then_inc(*own(silu_done))

            def rsqrt(dst, src, scale=1.0, last=None):
                af(dst, src, ACT.Ln, bias=eps, scale=scale).then_inc(*own())
                act.wait_ge(*own.last)
                af(dst, dst, ACT.Exp, scale=-0.5).then_inc(*own(last))

            def norm(ni, segs, l):
                a0 = segs[0][0]
                if ni:
                    act.wait_ge(gemm_dve, dves_before[ni])
                for k in range(KT):
                    if KT * ni + k >= 2:
                        act.wait_ge(sq_used, KT * ni + k - 1)
                    af(NSQ[k % 2][:, a0:T], Xv[:, k, a0:T], ACT.Square).then_inc(*own(sq_ready))
                act.wait_ge(sq_used, KT * (ni + 1))
                for i, (a, e) in enumerate(segs):
                    af(RSTD[:, a:e], bank(2 + i, 0, e - a), ACT.Ln, bias=eps).then_inc(*own())
                act.wait_ge(*own.last)
                af(RSTD[:, a0:T], RSTD[:, a0:T], ACT.Exp, scale=-0.5).then_inc(*own(rstd_ready))
                if l == DEPTH:
                    return
                for k in range(KT):
                    act.wait_ge(scaled, KT * ni + k + 1)
                    for i, (a, e) in enumerate(segs):
                        shift = mod(l, 0 if a == 0 else 1, (0 if ni % 2 == 0 else 24) + k)
                        last = af(Hv[:, k, a:e], Hv[:, k, a:e], ACT.Identity, bias=shift)
                        last.then_inc(*own(normed if i == len(segs) - 1 else None))

            def dn(l):
                P3 = lambda i: PRB[:, i * T:(i + 1) * T]
                for f in range(6):
                    if f >= 2:
                        act.wait_ge(prep_act, at(PR_ACT, l, f"s{f - 2}"))
                    af(P3(f % 2), fm("dn", f), ACT.Copy, scale=sm(l, W_DNC + f * 3 + 1)).then_inc(*own(prep_act))
                    act.wait_ge(prep_dve, at(PR_DVE, l, f"c{f}"))
                    af(fm("dn", f), P3(f % 2), ACT.Silu).then_inc(*own(prep_act))
                for f in range(4):
                    act.wait_ge(prep_act, at(PR_ACT, l, f"s{f if f > 3 else 5}"))
                    if f >= 2:
                        act.wait_ge(prep_pe, at(PR_PE, l, f"n{f - 2}"))
                    af(P3(f % 2), fm("dn", f), ACT.Square).then_inc(*own(prep_act))
                    act.wait_ge(prep_pe, at(PR_PE, l, f"n{f}"))
                    if f:
                        act.wait_ge(prep_dve, at(PR_DVE, l, f"l{f - 1}"))
                    af(P3(2)[:, 0:CTX], bank(2, 0, CTX), ACT.Ln, bias=eps).then_inc(*own())
                    af(P3(2)[:, CTX:T], bank(3), ACT.Ln, bias=eps).then_inc(*own())
                    act.wait_ge(*own.last)
                    af(P3(2), P3(2), ACT.Exp, scale=-0.5).then_inc(*own(prep_act))
                act.wait_ge(prep_dve, at(PR_DVE, l, "b1"))
                af(ba(BETA), ba(NEGB), ACT.Exp, scale=-1.0).then_inc(*own())
                af(ba(EDEC), ba(EG), ACT.Exp, scale=-1.0).then_inc(*own())
                af(ba(TOT)[:, 0:8], sm(l, W_ALOG, 8), ACT.Exp).then_inc(*own())
                act.wait_ge(*own.last)
                af(ba(EDEC), ba(EDEC), ACT.Ln, bias=one).then_inc(*own(prep_act))
                act.wait_ge(prep_pe, at(PR_PE, l, "cum"))
                af(ba(G), bank(4, 0, 48), ACT.Copy).then_inc(*own())
                af(ba(TOT), bank(4, 48, 96), ACT.Copy).then_inc(*own())
                af(ba(EG), bank(4, 0, 48), ACT.Exp).then_inc(*own())
                af(ba(EGL), bank(4, 96, 144), ACT.Exp).then_inc(*own(prep_act))
                act.wait_ge(prep_dve, at(PR_DVE, l, "b3"))
                af(ba(EDEC), ba(EDEC), ACT.Exp).then_inc(*own(prep_act))
                for n in range(TT):
                    g = TT * l + n
                    B, A = [bank(3), bank(6)], [bank(2), bank(5)]
                    for d in range(2):
                        if n:
                            act.wait_ge(dn_dve, at2(DN_DVE, g - 1, "O", d))
                        af(h4(dn_buf(d, "Tm", 512)), four(IDN), ACT.Copy).then_inc(*own())
                        af(h4(dn_buf(d, "TTm", 512)), four(IDN), ACT.Copy).then_inc(*own(dn_act))
                    for d in range(2):
                        act.wait_ge(dn_pe, at2(DN_PE, g, "kb", d))
                        af(dn_buf(d, "kbT", 256), B[d][:, 0:256], ACT.Copy).then_inc(*own(dn_act))
                    for d in range(2):
                        act.wait_ge(dn_dve, at2(DN_DVE, g, "R", d))
                        af(dn_buf(d, "D", 512), dn_buf(d, "D", 512), ACT.Exp).then_inc(*own(dn_act))
                    for i in range(5):
                        for d in range(2):
                            act.wait_ge(dn_pe, at2(DN_PE, g, f"X{i}", d))
                            af(dn_buf(d, "X", 512), A[d], ACT.Copy).then_inc(*own(dn_act))
                    for j in range(2):
                        for d in range(2):
                            act.wait_ge(dn_pe, at2(DN_PE, g, f"V{j}", d))
                            c = j if d == 0 else 1 - j
                            rows = slice(64 * c, 64 * c + 64)
                            af(dn_buf(d, "vn", 256)[rows, :], B[d][rows, 0:256], ACT.Copy).then_inc(*own(dn_act))

            def hg(l):
                E1, L2 = PRB[:, 0:T], PRB[:, T:2 * T]
                act.wait_ge(hp_dve, at(HP_DVE, l, "lb1"))
                af(ST[:, 108:116], ST[:, 108:116], ACT.Exp).then_inc(*own(hp_act))
                act.wait_ge(hp_dve, at(HP_DVE, l, "lb2"))
                af(LBV[:, 4:8], LBV[:, 4:8], ACT.Ln).then_inc(*own(hp_act))
                act.wait_ge(*own.last)
                for i in range(4):
                    F = fm("hg", 2 + i)
                    act.wait_ge(hp_dve, at(HP_DVE, l, f"c{i}"))
                    if i:
                        act.wait_ge(hp_dve, at(HP_DVE, l, f"l{i - 1}"))
                    af(E1, F, ACT.Exp, scale=-1.0).then_inc(*own())
                    act.wait_ge(*own.last)
                    af(L2, E1, ACT.Ln, scale=LBV[:, i:i + 1], bias=one).then_inc(*own())
                    af(E1, E1, ACT.Ln, bias=one).then_inc(*own(hp_act))
                    act.wait_ge(hp_dve, at(HP_DVE, l, f"l{i}"))
                    af(F, F, ACT.Exp, scale=-1.0, bias=LBV[:, 4 + i:5 + i]).then_inc(*own(hp_act))
                for n in range(TT):
                    for d in range(2):
                        q = 2 * (TT * l + n) + d
                        act.wait_ge(hg_dve, at(HG_DVE, q, "D"))
                        he = Y[:, 6 * T:8 * T]
                        af(he, he, ACT.Abs).then_inc(*own())
                        act.wait_ge(*own.last)
                        af(he, he, ACT.Exp, scale=-1.0).then_inc(*own())
                        t = ORD[d][n]
                        if q:
                            act.wait_ge(hg_pe, at(HG_PE, q - 1, "C1"))
                        hbt = Y[:, (2 + 2 * d) * T:(4 + 2 * d) * T].rearrange("p (f n) -> p f n", f=2)[:, :, t * P:(t + 1) * P]
                        af(HQB.rearrange("p (f n) -> p f n", f=2), hbt, ACT.Exp).then_inc(*own())
                        ed = 63 if d == 0 else 0
                        bl = hbt.rearrange("p f (c j) -> p f c j", c=2)[:, :, :, ed]
                        af(HDE.rearrange("p (f c) -> p f c", f=2), bl, ACT.Exp).then_inc(*own())
                        af(HKE, HKE, ACT.Exp, scale=-1.0).then_inc(*own(hg_act))
                        act.wait_ge(hg_pe, at(HG_PE, q, "T"))
                        af(HKT, bank(2, 0, 256), ACT.Copy).then_inc(*own(hg_act))

            def attend(st):
                kind, l = st
                i0, todo = items[st]
                na = kind == "na"
                def exps(i):
                    h, t = todo[i]
                    g = i0 + i
                    a = 0 if t >= CT else LAT
                    s = ST[:, 8 * (g % 4):8 * (g % 4) + 8]
                    act.wait_ge(at_max, g + 1)
                    if i >= 2:
                        act.wait_ge(at_tr, g - 1)
                    if na:
                        pr = NP_[g % 2]
                        b0 = 512 * (2 + 2 * (g % 2))
                        if a == 0:
                            af(pr[:, 0:LAT], pr[:, 0:LAT], ACT.Exp, bias=s[:, 0:1], accum_out=s[:, 2:3]).then_inc(*own())
                        af(pr[:, LAT:T], PS[:, b0 + LAT:b0 + T], ACT.Exp, bias=s[:, 0:1], accum_out=s[:, 3:4]).then_inc(*own(at_exp))
                    else:
                        for j in range(2):
                            b0 = 512 * (2 + 2 * j)
                            af(DPP[g % 2][:, j * T + a:(j + 1) * T], PS[:, b0 + a:b0 + T], ACT.Exp,
                                     bias=s[:, j:j + 1], accum_out=s[:, 2 + j:3 + j]).then_inc(*own(at_exp if j else None))

                def evac(i):
                    g = i0 + i
                    a = 0 if todo[i][1] >= CT else LAT
                    act.wait_ge(at_tr, g + 1)
                    if i:
                        act.wait_ge(at_pv, g)
                    af((NPT if na else DPT)[g % 2][:, a:T], PS[:, 6 * 512 + a:6 * 512 + T], ACT.Copy).then_inc(*own(at_pt))

                for i in range(len(todo) + 1):
                    new_pair = na and i < len(todo) and todo[i][0] % 2 == 0 and (i == 0 or todo[i - 1][0] != todo[i][0])
                    if i and new_pair:
                        evac(i - 1)
                    if i < len(todo):
                        exps(i)
                    if i and not new_pair:
                        evac(i - 1)

            def post(st):
                m, p0, t0 = posts[st]
                kind, l = st
                w = (TT - t0) * GW
                nt = TT - t0
                o = O[:, t0 * GW:TT * GW]
                if kind != "na":
                    if kind in ("dn", "hg"):
                        gate = tm(kind, 0 if kind == "dn" else 1)[:, t0 * GW:TT * GW]
                        af(gate, gate, ACT.Silu).then_inc(*own())
                    act.wait_ge(post_dve, 2 * m)
                    if kind == "dn":
                        act.wait_ge(dn_dve, at2(DN_DVE, TT * l + TT - 1, "O", 1))
                    elif kind == "hg":
                        act.wait_ge(hg_dve, at(HG_DVE, 2 * TT * (l + 1) - 1, "O"))
                        act.wait_ge(hg_pe, at(HG_PE, 2 * TT * (l + 1) - 1, "C1"))
                    else:
                        act.wait_ge(at_o, items[st][0] + len(items[st][1]))
                    sq = SCR[:, 1536:1536 + w]
                    af(sq, o, ACT.Square).then_inc(*own(post_act))
                    act.wait_ge(post_dve, 2 * m + 1)
                    rsqrt(ST[:, 40:40 + 4 * nt], ST[:, 40:40 + 4 * nt], 1.0 / HD, post_act)
                f = YT[kind]
                for i, t in enumerate(range(t0, TT, 2)):
                    act.wait_ge(post_pe, p0 + i + 1)
                    dst = Yv[:, f:f + 2, t * P:(t + 2) * P]
                    af(dst, bank(2 + i).rearrange("p (f n) -> p f n", f=2), ACT.Copy).then_inc(*own(y_done))

            act.wait_ge(loaded, 16 * N_LOADS)
            act.wait_ge(masks_ready, 1)
            af(SC[:, :], SC[:, :], ACT.Silu).then_inc(*own(silu_ready))
            for st in steps:
                kind = st[0]
                if kind == "unit":
                    gemm_unit(st[1])
                elif kind == "norm":
                    norm(norm_at.index(st), st[3], st[1])
                else:
                    act.wait_ge(y_done, before[st])
                    if kind == "dn":
                        dn(st[1])
                    elif kind == "hg":
                        hg(st[1])
                    elif kind == "na":
                        attend(st)
                    if kind == "df":
                        act.wait_ge(dp_dve, at(DP_DVE, st[1], "d"))
                        af(ST[:, 36:38], ST[:, 34:36], ACT.Exp).then_inc(*own(dp_act))
                        attend(st)
                    post(st)

        @block.vector
        def _(dve):
            own = Turns(dve_chain)
            v = nc.vector
            tt, ts, stt, ttr = v.tensor_tensor, v.tensor_scalar, v.scalar_tensor_tensor, v.tensor_tensor_reduce

            def taps(dst, src, w, a, e, sem_=None):
                dve.wait_ge(*own.last)
                stt(dst[:, a + 1:e], src[:, a:e - 1], w(0), dst[:, a + 1:e], MUL, ADD).then_inc(*own())
                dve.wait_ge(*own.last)
                stt(dst[:, a:e - 1], src[:, a + 1:e], w(2), dst[:, a:e - 1], MUL, ADD).then_inc(*own(sem_))

            def gemm_unit(u):
                k, l = u["kind"], u["l"]
                if k == "ada":
                    dve.wait_ge(*weights(u))
                    dve.wait_ge(silu_ready, 1)
                    vecs = (0, 1) if (l < DEPTH - 1 or u["u"] < 8) else (1,)
                    for j in range(2):
                        m = 2 * u["u"] + j
                        for vec in vecs:
                            last = (j, vec) == (1, vecs[-1])
                            dve.wait_ge(*own.last) if own.last else None
                            ttr(out=JUNK[:, :], in0=slot(u)[:, j * DM:(j + 1) * DM], in1=SC[:, vec * DM:(vec + 1) * DM],
                                      scale=1.0, scalar=sm(l, W_BADA + m), op0=MUL, op1=ADD,
                                      accum_out=mod(l, vec, m)).then_inc(*own(ada_done if last else None))
                    return
                if k == "upg":
                    p = u["pair"]
                    dve.wait_ge(gemm_act, u["banks"][-1]["turn"])
                    for f in range(2):
                        for i, (a, e) in enumerate(u["segs"]):
                            last = f == 1 and i == len(u["segs"]) - 1
                            taps(FFC[p % 2][:, f * T:(f + 1) * T], FFG[p % 2][:, f * T:(f + 1) * T],
                                 lambda tap: sm(l, W_FFC + (2 * u["u"] + f) * 3 + tap), a, e, conv_done if last else None)
                for b in u["banks"]:
                    if b["who"] != "dve":
                        continue
                    dve.wait_ge(gemm_ready, b["n"] + 1)
                    f, (a, e) = b["what"]
                    ps = bank(b["n"] % 2)[:, 0:e - a]
                    if k == "upv":
                        p = u["pair"]
                        dve.wait_ge(silu_done, p + 1)
                        ft = 2 * u["u"] + f - PARTS[u["part"]][0]
                        tt(Z[:, ft * T + a:ft * T + e], ps, FFC[p % 2][:, f * T + a:f * T + e], MUL).then_inc(*own(gemm_dve))
                    else:
                        m = 2 * u["u"] + f if k == "out" else u["m"]
                        gate = mod(l, 0 if a == 0 else 1, (16 if k == "out" else 40) + m)
                        dve.wait_ge(*own.last)
                        stt(Xv[:, m, a:e], ps, gate, Xv[:, m, a:e], MUL, ADD).then_inc(*own(gemm_dve))

            def norm(ni, segs, l):
                for i, (a, e) in enumerate(segs):
                    g = AB[:, (2 * ni + i) * KT:(2 * ni + i + 1) * KT]
                    if l == DEPTH:
                        v.tensor_copy(g, FIN[:, :]).then_inc(*own())
                    else:
                        dve.wait_ge(*own.last)
                        stt(g, mod(l, 0 if a == 0 else 1, 8 if ni % 2 == 0 else 32, KT), 1.0,
                                  sm(l, W_N1 if ni % 2 == 0 else W_N2, KT), ADD, MUL).then_inc(*own())
                dve.wait_ge(*own.last)
                dve.wait_ge(rstd_ready, ni + 1)
                for k in range(KT):
                    for i, (a, e) in enumerate(segs):
                        g = AB[:, (2 * ni + i) * KT + k:(2 * ni + i) * KT + k + 1]
                        last = stt(Hv[:, k, a:e], Xv[:, k, a:e], g, RSTD[:, a:e], MUL, MUL)
                        last.then_inc(*own(scaled if i == len(segs) - 1 else None))

            def dn(l):
                for f in range(6):
                    dve.wait_ge(prep_act, at(PR_ACT, l, f"m{f}"))
                    dst = PRB[:, (f % 2) * T:(f % 2 + 1) * T]
                    w = lambda tap: sm(l, W_DNC + f * 3 + tap)
                    taps(dst, fm("dn", f), w, 0, CTX)
                    taps(dst, fm("dn", f), w, CTX, T, prep_dve)
                for f in range(4):
                    dve.wait_ge(prep_act, at(PR_ACT, l, f"r{f}"))
                    stt(fm("dn", f), fm("dn", f), HD ** -0.5 if f < 2 else 1.0, PRB[:, 2 * T:3 * T], MUL, MUL).then_inc(*own(prep_dve))
                raw = Y[:, BAO:BAO + 96].rearrange("p (t g h) -> p t g h", t=TT, g=4)
                as48 = lambda i: ba(i).rearrange("p (t d h) -> p t d h", t=TT, d=2)
                at8 = lambda i: ba(i).rearrange("p (t g) -> p t g", t=TT)
                raw8 = Y[:, BAO:BAO + 96].rearrange("p (t g) -> p t g", t=TT)
                ts(at8(NEGB), raw8[:, :, 0:8], -80.0, None, MAX).then_inc(*own())
                tt(at8(G), raw8[:, :, 8:16], sm(l, W_DTB, 8)[:, None, :].to_broadcast([P, TT, 8]), ADD).then_inc(*own())
                dve.wait_ge(*own.last)
                stt(ba(EG), ba(G), -1.0, ba(G), MUL, MAX).then_inc(*own(prep_dve))
                dve.wait_ge(prep_act, at(PR_ACT, l, "b1"))
                v.tensor_scalar_add(ba(BETA), ba(BETA), 1.0).then_inc(*own())
                stt(ba(G), ba(G), 0.0, ba(EDEC), MAX, ADD).then_inc(*own())
                dve.wait_ge(*own.last)
                v.reciprocal(ba(BETA), ba(BETA)).then_inc(*own())
                dve.wait_ge(*own.last)
                v.tensor_scalar_mul(ba(NBETA), ba(BETA), -1.0).then_inc(*own())
                stt(at8(LOGA), at8(G), -1.0, ba(TOT)[:, None, 0:8].to_broadcast([P, TT, 8]), MUL, MUL).then_inc(*own(prep_dve))
                dve.wait_ge(prep_act, at(PR_ACT, l, "b2"))
                tt(ba(EDEC), ba(TOT), ba(G), SUB).then_inc(*own(prep_dve))
                stt(ba(NEGB), ba(EG), -1.0, ba(BETA), MUL, MUL).then_inc(*own())
                v.memset(Y[:, YS + 3584:YS + 3840], 0.0).then_inc(*own(prep_dve))
                dve.wait_ge(prep_act, at(PR_ACT, l, "b3"))
                for n in range(TT):
                    g = TT * l + n
                    A, B, C = [bank(2), bank(5)], [bank(3), bank(6)], [bank(4), bank(7)]
                    tile = [ORD[d][n] for d in range(2)]

                    def col(i, d):
                        return ba(i)[:, tile[d] * 8 + d * 4:tile[d] * 8 + d * 4 + 4]

                    def over(i, d, rows=slice(0, P)):
                        c = col(i, d)[rows, :]
                        return c[:, :, None].to_broadcast([c.shape[0], NH, HD])

                    for d in range(2):
                        dve.wait_ge(dn_pe, at2(DN_PE, g, "tr", d))
                        kt, vt = h4(A[d][:, 0:256]), h4(A[d][:, 256:512])
                        tt(h4(dn_buf(d, "kdec", 256)), kt, over(EDEC, d), MUL).then_inc(*own())
                        tt(h4(dn_buf(d, "vb", 256)), vt, over(BETA, d), MUL).then_inc(*own())
                        tt(h4(dn_buf(d, "kb", 256)), kt, over(NBETA, d), MUL).then_inc(*own(dn_dve))
                    for d in range(2):
                        dve.wait_ge(dn_pe, at2(DN_PE, g, "R", d))
                        for h in range(NH):
                            hs = slice(h * P, (h + 1) * P)
                            last = stt(dn_buf(d, "D", 512)[:, hs], C[d][:, hs], col(G, d)[:, h:h + 1],
                                       cc(C_NEG + d * P, P), SUB, MIN)
                            last.then_inc(*own(dn_dve if h == NH - 1 else None))
                    for d in range(2):
                        dve.wait_ge(dn_pe, at2(DN_PE, g, "kk", d))
                        dve.wait_ge(dn_act, at2(DN_ACT, g, "exp", d))
                        tt(dn_buf(d, "NT", 512), A[d], dn_buf(d, "D", 512), MUL).then_inc(*own(dn_dve))
                    for d in range(2):
                        dve.wait_ge(dn_pe, at2(DN_PE, g, "kq", d))
                        tt(dn_buf(d, "at", 512), B[d], dn_buf(d, "D", 512), MUL).then_inc(*own(dn_dve))

                    def grow(dst, lv, d, src, transposed, sem_=None):
                        m = mask(d if transposed else 1 - d, lv)
                        v.copy_predicated(h4(dn_buf(d, dst, 512)), four(m), h4(src)).then_inc(*own(sem_))

                    for d in range(2):
                        dve.wait_ge(dn_pe, at2(DN_PE, g, "N", d))
                        dve.wait_ge(dn_dve, at2(DN_DVE, g, "NT", d))
                        grow("Tm", 1, d, C[d], False)
                        grow("TTm", 1, d, dn_buf(d, "NT", 512), True, dn_dve)
                    for i in range(5):
                        for d in range(2):
                            dve.wait_ge(dn_pe, at2(DN_PE, g, f"Y{i}", d))
                            dve.wait_ge(dn_dve, at2(DN_DVE, g, "M" if i == 0 else f"L{i - 1}", d))
                            if i < 4:
                                grow("Tm", i + 2, d, C[d], False)
                            grow("TTm", i + 2, d, B[d], True, dn_dve)
                    for j in range(2):
                        for d in range(2):
                            c = j if d == 0 else 1 - j
                            rows = slice(64 * c, 64 * c + 64)
                            rhs = dn_buf(d, "rhs", 256)[rows, :]
                            dve.wait_ge(dn_pe, at2(DN_PE, g, f"K{j}", d))
                            tt(h4(rhs), h4(A[d][rows, 0:256]), over(NEGB, d, rows), MUL).then_inc(*own())
                            dve.wait_ge(*own.last)
                            tt(rhs, rhs, dn_buf(d, "vb", 256)[rows, :], ADD).then_inc(*own(dn_dve))
                        for d in range(2):
                            c = j if d == 0 else 1 - j
                            dve.wait_ge(dn_pe, at2(DN_PE, g, f"O{j}", d))
                            for hp in range(2):
                                S = DNS[d][:, hp * HD:(hp + 1) * HD]
                                o = ((tile[d] * 2 + d) * 2 + hp) * 2 + c
                                last = stt(S, S, ba(EGL)[:, o:o + 1], B[d][:, 256 + hp * HD:256 + (hp + 1) * HD], MUL, ADD)
                                last.then_inc(*own(dn_dve if hp else None))
                    for d in range(2):
                        t = dn_buf(d, "t", 256)
                        o = O[:, tile[d] * GW:(tile[d] + 1) * GW]
                        first = ORD[1 - d].index(tile[d]) > n
                        tt(h4(t), h4(A[d][:, 256:512]), over(EG, d), MUL).then_inc(*own())
                        dve.wait_ge(*own.last)
                        if first:
                            tt(o, t, C[d][:, 0:256], ADD).then_inc(*own(dn_dve))
                        else:
                            tt(t, t, C[d][:, 0:256], ADD).then_inc(*own())
                            dve.wait_ge(*own.last)
                            tt(o, t, o, ADD).then_inc(*own(dn_dve))

            def hg(l):
                E1, L2, LF = PRB[:, 0:T], PRB[:, T:2 * T], PRB[:, 2 * T:3 * T]
                raw = [sm(i, W_LB, 8)[:, 4 * i:4 * i + 4] for i in range(DEPTH)]
                e = ST[:, 108:116]
                tt(ST[:, 104:108], raw[0], raw[1], MAX).then_inc(*own())
                dve.wait_ge(*own.last)
                for i in range(DEPTH):
                    tt(e[:, 4 * i:4 * i + 4], raw[i], ST[:, 104:108], SUB).then_inc(*own(hp_dve if i else None))
                dve.wait_ge(hp_act, at(HP_ACT, l, "lb1"))
                tt(ST[:, 104:108], e[:, 0:4], e[:, 4:8], ADD).then_inc(*own())
                dve.wait_ge(*own.last)
                v.reciprocal(ST[:, 104:108], ST[:, 104:108]).then_inc(*own())
                dve.wait_ge(*own.last)
                for i in range(DEPTH):
                    tt(e[:, 4 * i:4 * i + 4], e[:, 4 * i:4 * i + 4], ST[:, 104:108], MUL).then_inc(*own())
                dve.wait_ge(*own.last)
                if l == 0:
                    tt(LBV[:, 0:4], e[:, 0:4], e[:, 0:4], SUB).then_inc(*own())
                else:
                    tt(LBV[:, 0:4], e[:, 0:4], e[:, 4:8], ADD).then_inc(*own())
                    dve.wait_ge(*own.last)
                    tt(LBV[:, 0:4], LBV[:, 0:4], e[:, 0:4], SUB).then_inc(*own())
                dve.wait_ge(*own.last)
                ts(LBV[:, 4:8], LBV[:, 0:4], -1.0, 1.0, MUL, ADD).then_inc(*own())
                dve.wait_ge(*own.last)
                ts(LBV[:, 4:8], LBV[:, 4:8], 1e-18, None, MAX).then_inc(*own(hp_dve))
                for i in range(4):
                    F = fm("hg", 2 + i)
                    d, f = i // 2, i % 2
                    ts(F, F, -40.0, None, MAX).then_inc(*own(hp_dve))
                    dve.wait_ge(hp_act, at(HP_ACT, l, f"e{i}"))
                    tt(LF, L2, E1, SUB).then_inc(*own())
                    tt(F, F, E1, ADD).then_inc(*own(hp_dve))
                    hb, lf = HB(d, f), LF
                    if d == 1:
                        hb, lf = hb[:, ::-1], LF[:, ::-1]
                    dve.wait_ge(*own.last)
                    v.tensor_tensor_scan(hb, cc(C_SCAN, T), lf, 0.0, MUL, ADD).then_inc(*own(hp_dve))
                v.memset(SCR[:, 4352:4608], 0.0).then_inc(*own())
                dve.wait_ge(*own.last)
                dve.wait_ge(hp_act, at(HP_ACT, l, "k3"))
                for n in range(TT):
                    for d in range(2):
                        q = 2 * (TT * l + n) + d
                        t = ORD[d][n]
                        cs = slice(t * P, (t + 1) * P)
                        hb2 = Y[:, (2 + 2 * d) * T:(4 + 2 * d) * T].rearrange("p (f n) -> p f n", f=2)[:, :, cs]
                        two = lambda ap: ap.rearrange("p (f n) -> p f n", f=2)
                        if q:
                            dve.wait_ge(hg_pe, at(HG_PE, q - 1, "T"))
                        for lv in range(1, LEVELS + 1):
                            s = 1 << (lv - 1)
                            w = hb2.rearrange("p f (b j) -> p f b j", j=2 * s)
                            m = w[:, :, :, s - 1:s] if d == 0 else w[:, :, :, s:s + 1]
                            tt(two(HE[:, lv - 1, :]).rearrange("p f (b j) -> p f b j", j=2 * s), w,
                                     m.to_broadcast([P, 2, P // (2 * s), 2 * s]), SUB).then_inc(*own())
                        w = hb2.rearrange("p f (c j) -> p f c j", c=2)
                        m = w[:, :, :, 63:64] if d == 0 else w[:, :, :, 0:1]
                        tt(two(HKE).rearrange("p f (c j) -> p f c j", c=2), w, m.to_broadcast([P, 2, 2, 64]), SUB).then_inc(*own(hg_dve))
                        qk = Z[:, ZG:ZG + 6 * T].rearrange("p (x f n) -> p x f n", x=3, f=2)
                        qs, ks = qk[:, 0, :, cs], qk[:, 1 + d, :, cs]
                        dve.wait_ge(hg_act, at(HG_ACT, q, "E"))
                        tt(two(HQB), two(HQB), qs, MUL).then_inc(*own())
                        tt(two(HKE), two(HKE), ks, MUL).then_inc(*own(hg_dve))
                        if q:
                            dve.wait_ge(hg_pe, at(HG_PE, q - 1, "C1"))
                        v.memset(ATT, 0.0).then_inc(*own())

                        def weigh(lv):
                            if lv >= 4:
                                dve.wait_ge(hg_pe, at(HG_PE, q, f"L{lv - 3}"))
                            dst = QKT[lv % 3].rearrange("p (x f n) -> p x f n", x=2, f=2)
                            E = two(HE[:, lv - 1, :])
                            tt(dst[:, 0], qs, E, MUL).then_inc(*own())
                            tt(dst[:, 1], ks, E, MUL).then_inc(*own(hg_dve))

                        def take(lv):
                            dve.wait_ge(hg_pe, at(HG_PE, q, f"L{lv}"))
                            dve.wait_ge(*own.last)
                            v.copy_predicated(h4(ATT), four(mask(d, lv)), h4(bank(3 + lv % 3))).then_inc(*own(hg_dve))

                        for name in HG_DVE[2:15]:
                            (weigh if name[0] == "M" else take)(int(name[1]))
                        for j in range(2):
                            c = j if d == 0 else 1 - j
                            dve.wait_ge(hg_pe, at(HG_PE, q, f"C{j}"))
                            for f in range(2):
                                S = HGS[d][:, f * HD:(f + 1) * HD]
                                stt(S, S, HDE[:, 2 * f + c:2 * f + c + 1], bank(7, f * HD, (f + 1) * HD), MUL, ADD).then_inc(*own(hg_dve if f else None))
                        o = O[:, t * GW:(t + 1) * GW]
                        if ORD[1 - d].index(t) > n or (ORD[1 - d].index(t) == n and d == 0):
                            v.tensor_copy(o, bank(6, 0, 256)).then_inc(*own(hg_dve))
                        else:
                            tt(o, o, bank(6, 0, 256), ADD).then_inc(*own(hg_dve))

            def attend(st):
                kind, l = st
                i0, todo = items[st]
                na = kind == "na"
                stat = lambda g: ST[:, 8 * (g % 4):8 * (g % 4) + 8]

                def bias(hp):
                    for rnd in range(4):
                        gi = 4 * (2 * l + hp) + rnd
                        dve.wait_ge(bias_pe, gi + 1)
                        if rnd == 0:
                            dve.wait_ge(*own.last)
                        src = bank(2 + 2 * (rnd % 2), 0, 448).rearrange("p (k x) -> p k x", k=16)
                        dst = NAB.rearrange("p (x k) -> p k x", k=GRID)[:, rnd * 16:(rnd + 1) * 16, :]
                        m = cc(C_NAM + rnd * 16, 16)[:, :, None].to_broadcast([P, 16, 28])
                        tt(dst, src, m, ADD).then_inc(*own(bias_dve))
                    dve.wait_ge(*own.last)

                def maxes(i):
                    h, t = todo[i]
                    g = i0 + i
                    s = stat(g)
                    if i >= 2:
                        dve.wait_ge(at_tr, g - 1)
                    dve.wait_ge(at_s, g + 1)
                    if na:
                        b0 = 512 * (2 + 2 * (g % 2))
                        if t < CT:
                            v.tensor_reduce(s[:, 0:1], PS[:, b0 + LAT:b0 + T], AX.X, MAX, negate=True).then_inc(*own(at_max))
                            return
                        qa = t - CT
                        o = ((h % 2) * 14 + 6 - 2 * qa) * GRID
                        ttr(out=NP_[g % 2][:, 0:LAT], in0=PS[:, b0:b0 + LAT], in1=NAB[:, o:o + LAT], scale=1.0,
                                  scalar=-3e38, op0=ADD, op1=MAX, accum_out=s[:, 4:5]).then_inc(*own())
                        v.tensor_reduce(s[:, 5:6], PS[:, b0 + LAT:b0 + T], AX.X, MAX).then_inc(*own())
                        dve.wait_ge(*own.last)
                        ts(s[:, 0:1], s[:, 4:5], s[:, 5:6], -1.0, MAX, MUL).then_inc(*own(at_max))
                    else:
                        a = 0 if t >= CT else LAT
                        for j in range(2):
                            b0 = 512 * (2 + 2 * j)
                            v.tensor_reduce(s[:, j:j + 1], PS[:, b0 + a:b0 + T], AX.X, MAX, negate=True).then_inc(*own(at_max if j else None))

                def probs(i):
                    h, t = todo[i]
                    g = i0 + i
                    s = stat(g)
                    dve.wait_ge(at_exp, g + 1)
                    if na:
                        if t >= CT:
                            tt(s[:, 6:7], s[:, 2:3], s[:, 3:4], ADD).then_inc(*own())
                            dve.wait_ge(*own.last)
                            v.reciprocal(s[:, 6:7], s[:, 6:7]).then_inc(*own(at_p))
                        else:
                            v.reciprocal(s[:, 6:7], s[:, 3:4]).then_inc(*own(at_p))
                    else:
                        a = 0 if t >= CT else LAT
                        v.reciprocal(s[:, 4:6], s[:, 2:4]).then_inc(*own())
                        dve.wait_ge(*own.last)
                        stt(s[:, 7:8], s[:, 2:3], s[:, 5:6], ST[:, 38:39], MUL, MUL).then_inc(*own())
                        dve.wait_ge(*own.last)
                        p0, p1 = DPP[g % 2][:, a:T], DPP[g % 2][:, T + a:2 * T]
                        stt(p0, p1, s[:, 7:8], p0, MUL, ADD).then_inc(*own(at_p))

                def outs(i):
                    h, t = todo[i]
                    g = i0 + i
                    s = stat(g)
                    dve.wait_ge(at_pv, g + 1)
                    dve.wait_ge(*own.last)
                    v.tensor_scalar_mul(O[:, t * GW + h * HD:t * GW + (h + 1) * HD], bank(7, 256, 256 + HD),
                                              s[:, 6:7] if na else s[:, 4:5]).then_inc(*own(at_o))

                n = len(todo)
                for i in range(n + 2):
                    if na and i < n and todo[i][0] % 2 == 0 and (i == 0 or todo[i - 1][0] != todo[i][0]):
                        if i:
                            probs(i - 1)
                            outs(i - 2)
                        bias(todo[i][0] // 2)
                        maxes(i)
                        continue
                    if i < n:
                        maxes(i)
                    if 0 < i <= n:
                        probs(i - 1)
                    if i >= 2:
                        outs(i - 2)

            def df(st):
                l = st[1]
                li = 0.8 - 0.6 * math.exp(-0.3 * l)
                lp = sm(l, W_LAM, 128)
                for k in range(2):
                    ttr(out=SCR[:, 1536:1568], in0=lp[:, 64 * k:64 * k + 32], in1=lp[:, 64 * k + 32:64 * k + 64], scale=1.0,
                              scalar=0.0, op0=MUL, op1=ADD, accum_out=ST[:, 34 + k:35 + k]).then_inc(*own(dp_dve if k else None))
                    dve.wait_ge(*own.last)
                for i in range(4):
                    dve.wait_ge(dp_pe, 4 * l + i + 1)
                    x = fm("df", i)[:, CTX:T]
                    tmp = SCR[:, 1536:2048]
                    dve.wait_ge(*own.last)
                    tt(tmp, bank(2 + i), cc(C_SIN, LAT), MUL).then_inc(*own())
                    tt(x, x, cc(C_COS, LAT), MUL).then_inc(*own())
                    dve.wait_ge(*own.last)
                    tt(x, x, tmp, ADD).then_inc(*own(dp_dve))
                dve.wait_ge(dp_act, at(["e"], l, "e"))
                ts(sm(l, W_DFN, HD), sm(l, W_DFN, HD), 1.0 - li, None, MUL).then_inc(*own())
                tt(ST[:, 38:39], ST[:, 37:38], ST[:, 36:37], SUB).then_inc(*own())
                dve.wait_ge(*own.last)
                v.tensor_scalar_add(ST[:, 38:39], ST[:, 38:39], -li).then_inc(*own(dp_dve))
                dve.wait_ge(*own.last)
                attend(st)

            def post(st):
                m, p0, t0 = posts[st]
                kind, l = st
                if kind == "na":
                    return
                n = (TT - t0) * NH
                w = (TT - t0) * GW
                o = O[:, t0 * GW:TT * GW]
                o3 = o.rearrange("p (n e) -> p n e", e=HD)
                ss = ST[:, 40:40 + n]
                dve.wait_ge(post_act, 2 * m + 1)
                v.tensor_reduce(ss, SCR[:, 1536:1536 + w].rearrange("p (n e) -> p n e", e=HD), AX.X, ADD).then_inc(*own(post_dve))
                dve.wait_ge(post_act, 2 * m + 2)
                tt(o3, o3, ss[:, :, None].to_broadcast([P, n, HD]), MUL).then_inc(*own())
                dve.wait_ge(*own.last)
                nw = sm(l, {"dn": W_DNN, "df": W_DFN, "hg": W_HGN}[kind], HD)[:, None, :].to_broadcast([P, n, HD])
                if kind == "df":
                    tt(o3, o3, nw, MUL).then_inc(*own(post_dve))
                    return
                tt(o3, o3, nw, MUL).then_inc(*own())
                dve.wait_ge(*own.last)
                gate = tm(kind, 0 if kind == "dn" else 1)[:, t0 * GW:TT * GW]
                tt(o, o, gate, MUL).then_inc(*own(post_dve))

            dve.wait_ge(loaded, 16 * N_LOADS)
            v.tensor_copy(MSK[:, :], Z[:, 0:2 * (LEVELS + 1) * P]).then_inc(*own(masks_ready))
            for st in steps:
                kind = st[0]
                if kind == "unit":
                    gemm_unit(st[1])
                elif kind == "norm":
                    norm(norm_at.index(st), st[3], st[1])
                else:
                    dve.wait_ge(gemm_act, acts_before[st])
                    dve.wait_ge(y_done, before[st])
                    if kind == "dn":
                        dn(st[1])
                    elif kind == "hg":
                        hg(st[1])
                    elif kind == "na":
                        attend(st)
                    else:
                        df(st)
                    post(st)


_OUT = (P, KT, LAT)


def kernel(**inputs):
    import concourse.bacc as _bacc
    from concourse import mybir as _mybir
    from concourse.bass_utils import run_bass_kernel_spmd as _run

    nc = _bacc.Bacc("TRN2", target_bir_lowering=False, num_devices=1)
    arrays = lay_out(inputs)
    aps = {}
    for name in INPUTS:
        a = arrays[name]
        aps[name] = nc.dram_tensor(f"in_{name}", a.shape, _mybir.dt.from_np(a.dtype), kind="ExternalInput").ap()
    out = nc.dram_tensor("out_0", _OUT, _mybir.dt.float32, kind="ExternalOutput").ap()
    hybrid_backbone(nc, aps, out)
    r = _run(nc, [{f"in_{k}": arrays[k] for k in INPUTS}], core_ids=[0])
    y = np.asarray(r.results[0]["out_0"])
    return np.ascontiguousarray(y.transpose(2, 1, 0).reshape(1, LAT, DM))
```

```python
import math
from contextlib import ExitStack
from itertools import chain

import numpy as np

import concourse.bass as bass
from concourse import mybir

P = 128
DM = 1024
KT = DM // P
LAT, CTX = 512, 256
T = LAT + CTX
TT = T // P
CT = CTX // P
SEG = ((0, CTX), (CTX, T))
DEPTH = 2
GW = 256
HD = 64
NH = 4
CH = 64
DFF = 2816
FT = DFF // P
P_IN = 3856
EPS = 1e-6
LEVELS = 6
NEG = -1e30
GRID = 64

C_ID, C_MEAN, C_BLK, C_ROT = 0, 128, 256, 384
C_NEG = 512
C_INC = 768
C_AJ = 1024
C_NAM = 1278
C_CHK = 1342
C_EPS, C_ONE = 1344, 1345
C_COS, C_SIN, C_SCAN = 1346, 1858, 2370
NC_ = C_SCAN + T

W_N1, W_N2, W_BADA, W_DNC, W_FFC = 0, 8, 16, 64, 82
W_ALOG, W_DTB, W_DNN, W_DFN, W_HGN = 148, 156, 164, 228, 292
W_LAM, W_LB, W_RPB, W_BA = 356, 484, 492, 548
NW = W_BA + KT * 16
COL = dict(dnq=0, dnk=256, dnv=512, dng=768, naq=1040, nak=1296, nav=1552, dfq=1808, dfk=2064,
           dfv=2320, hgq=2576, hgv=2832, hgf=3088, hgb=3344, hgg=3600)
COL_BA = 1024


def shape_constants():
    c = np.zeros((P, NC_), np.float32)
    i = np.arange(P)
    c[:, C_ID:C_ID + P] = np.eye(P)
    c[:, C_MEAN:C_MEAN + P] = 1.0 / DM
    blk = (i[:, None] // CH) == (i[None, :] // CH)
    c[:, C_BLK:C_BLK + P] = blk
    for m in range(P):
        first = m % 16 < 8
        c[m + 8 if first else m - 8, C_ROT + m] = -1.0 if first else 1.0
    for d in range(2):
        inc = blk & ((i[:, None] <= i[None, :]) if d == 0 else (i[:, None] >= i[None, :]))
        c[:, C_NEG + d * P:C_NEG + (d + 1) * P] = np.where(inc, 0.0, NEG)
        c[:, C_INC + d * P:C_INC + (d + 1) * P] = inc
    for b in range(2):
        for dl in range(31):
            c[32 * b + dl, C_AJ + 64 * b + 78 - dl] = 1.0
    q = i % GRID
    start = np.clip(q - 8, 0, GRID - 16)
    k = np.arange(GRID)
    c[:, C_NAM:C_NAM + GRID] = np.where((k >= start[:, None]) & (k < start[:, None] + 16), 0.0, NEG)
    c[:, C_CHK] = i < CH
    c[:, C_CHK + 1] = i >= CH
    c[:, C_EPS] = EPS
    c[:, C_ONE] = 1.0
    t = np.arange(LAT)
    inv = (1.0 / (np.float32(10000.0) ** (np.arange(0, 16, 2, dtype=np.float32) / np.float32(16)))).astype(np.float32)
    for p in range(P):
        pos = (t // GRID if p % 32 < 16 else t % GRID).astype(np.float32)
        ang = pos * inv[p % 8]
        c[p, C_COS:C_COS + LAT] = np.cos(ang)
        c[p, C_SIN:C_SIN + LAT] = np.sin(ang)
    c[:, C_SCAN:C_SCAN + T] = (np.arange(T) % CH != 0)
    m = np.zeros((2, LEVELS + 1, P, P), np.float32)
    for d in range(2):
        m[d, 0] = np.eye(P)
        for lv in range(1, LEVELS + 1):
            s = 1 << (lv - 1)
            same = (i[:, None] // (2 * s)) == (i[None, :] // (2 * s))
            right = (i // s) % 2 == 1
            row, col = (~right, right) if d == 0 else (right, ~right)
            m[d, lv] = same & row[:, None] & col[None, :]
    return c, np.ascontiguousarray(m.transpose(2, 0, 1, 3).reshape(P, -1))


def lay_out(a):
    f = np.float32
    out = {}
    x = np.concatenate([np.asarray(a["ctx"])[0], np.asarray(a["x"])[0]], 0)
    out["x"] = x.T.reshape(KT, P, T).transpose(1, 0, 2).reshape(P, -1)
    both = np.stack([np.asarray(a["c_ctx"]), np.asarray(a["c"])[0]]).reshape(1, -1)
    out["c"] = np.repeat(both, P, 0)
    w = np.asarray(a["w_ada"]).reshape(DEPTH, DM, 24, 2, P)
    out["ada"] = w.transpose(0, 2, 4, 3, 1).reshape(DEPTH, 24, P, 2 * DM)
    w_in = np.asarray(a["w_in"])
    cut = [w_in[:, :, o:o + GW] for o in COL.values()]
    out["win"] = np.stack(cut, 1).reshape(DEPTH, 15, KT, P, GW).transpose(0, 1, 3, 2, 4).reshape(DEPTH, 15, P, -1)
    out["wout"] = np.asarray(a["w_out"]).reshape(DEPTH, KT, P, 4, GW).transpose(0, 3, 2, 1, 4).reshape(DEPTH, 4, P, -1)
    out["wup"] = np.asarray(a["w_up"]).reshape(DEPTH, KT, P, 22, GW).transpose(0, 3, 2, 1, 4).reshape(DEPTH, 22, P, -1)
    out["wdn"] = np.asarray(a["w_down"]).reshape(DEPTH, FT, P, KT, P).transpose(0, 3, 2, 1, 4).reshape(DEPTH, KT, P, -1)
    s = np.zeros((DEPTH, P, NW), f)
    vec = lambda v, n: np.asarray(v).reshape(DEPTH, n, P).transpose(0, 2, 1)
    s[:, :, W_N1:W_N1 + 8] = vec(a["norm1_w"], 8)
    s[:, :, W_N2:W_N2 + 8] = vec(a["norm2_w"], 8)
    s[:, :, W_BADA:W_BADA + 48] = vec(a["b_ada"], 48)
    s[:, :, W_DNC:W_DNC + 18] = np.asarray(a["dn_conv_w"]).reshape(DEPTH, 3, 6, P).transpose(0, 3, 2, 1).reshape(DEPTH, P, 18)
    s[:, :, W_FFC:W_FFC + 66] = np.asarray(a["ffn_conv_w"]).reshape(DEPTH, 3, FT, P).transpose(0, 3, 2, 1).reshape(DEPTH, P, 66)
    s[:, :, W_ALOG:W_ALOG + 8] = np.asarray(a["dn_a_log"]).reshape(DEPTH, 1, 8)
    s[:, :, W_DTB:W_DTB + 8] = np.asarray(a["dn_dt_bias"]).reshape(DEPTH, 1, 8)
    s[:, :, W_DNN:W_DNN + 64] = np.asarray(a["dn_norm_w"])[:, None, :]
    s[:, :, W_DFN:W_DFN + 64] = np.asarray(a["df_norm_w"])[:, None, :]
    s[:, :, W_HGN:W_HGN + 64] = np.asarray(a["hg_norm_w"])[:, None, :]
    s[:, :, W_LAM:W_LAM + 128] = np.asarray(a["df_lambda"]).reshape(DEPTH, 1, 128)
    lb = np.asarray(a["hg_lb_raw"]).reshape(DEPTH, 2, 2, P).transpose(3, 0, 1, 2).reshape(P, 8)
    s[:, :, W_LB:W_LB + 8] = lb
    rpb = np.asarray(a["na_rpb"])
    for b in range(2):
        r = rpb[:, :, 1 - b:15 - b, :].transpose(0, 3, 1, 2).reshape(DEPTH, 31, 56)
        s[:, 32 * b:32 * b + 31, W_RPB:W_RPB + 56] = r
    s[:, :, W_BA:] = w_in[:, :, COL_BA:COL_BA + 16].reshape(DEPTH, KT, P, 16).transpose(0, 2, 1, 3).reshape(DEPTH, P, -1)
    out["small"] = s
    out["fin"] = np.asarray(a["final_norm_w"]).reshape(KT, P).T
    out["const"], out["masks"] = shape_constants()
    return {k: np.ascontiguousarray(v) for k, v in out.items()}


INPUTS = ["x", "c", "ada", "win", "wout", "wup", "wdn", "small", "fin", "const", "masks"]


def schedule():
    steps, units = [], []

    fills = {}

    def unit(into=None, **u):
        units.append(u)
        if into is None:
            steps.append(("unit", u))
        else:
            fills[into].append(u)

    def group(l, g):
        names = [["dnq", "dnk", "dnv", "dng"], ["hgf", "hgb", "hgq", "hgv", "hgg"],
                 ["naq", "nak", "nav"], ["dfq", "dfk", "dfv"]][g]
        return l, g, names

    def emit_group(l, g, names, into=None):
        base = (g % 2) * ZG
        fm, tm = 0, 0
        for name in names:
            last = l == DEPTH - 1
            if name in ("dng", "hgg", "nav", "dfv", "hgv"):
                t0 = CT if last and name in ("dng", "hgg") else 0
                unit(into, kind="tm", l=l, col=list(COL).index(name), z=base + 6 * T + tm * TT * GW, t0=t0)
                tm += 1
            else:
                segs = SEG[1:] if last and name in ("naq", "dfq") else SEG
                scale = {"naq": HD ** -0.5, "dfq": 32 ** -0.5, "hgq": HD ** -0.5}.get(name, 1.0)
                unit(into, kind="fm", l=l, col=list(COL).index(name), z=base + FMPOS[name] * T, segs=segs, scale=scale)
                fm += 1
        if g == 0:
            unit(kind="ba", l=l)

    for l in range(DEPTH):
        last = l == DEPTH - 1
        segs = SEG[1:] if last else SEG
        if l == 0:
            for u in range(8):
                unit(kind="ada", l=0, u=u)
        steps.append(("norm", l, 0, SEG))
        rest = [(0, u) for u in range(8, 24)] if l == 0 else []
        emit_group(*group(l, 0))
        for g, mixer in enumerate(MIXERS):
            st = (mixer, l)
            steps.append(st)
            fills[st] = []
            if g < 3:
                emit_group(*group(l, g + 1), st)
            else:
                for u in range(4):
                    unit(st, kind="out", l=l, u=u, segs=segs, rows=OTHERS)
            gemms, fills[st][:] = list(fills[st]), []
            for u in gemms:
                units.remove(u)
            for u in gemms:
                units.append(u)
                fills[st].append(u)
                for _ in range(2):
                    if rest:
                        la, ua = rest.pop(0)
                        unit(st, kind="ada", l=la, u=ua)
        for u in range(4):
            unit(kind="out", l=l, u=u, segs=segs, rows=LASTS)
        steps.append(("norm", l, 1, segs))
        rest = [(1, u) for u in range(24)] if l == 0 else []
        pair = 0
        for part, (a, b) in enumerate(PARTS):
            for u in range(a // 2, b // 2):
                unit(kind="upg", l=l, u=u, part=part, segs=segs)
                unit(kind="upv", l=l, u=u, part=part, segs=segs)
                for _ in range(3 if u % 2 else 2):
                    if rest:
                        la, ua = rest.pop(0)
                        unit(kind="ada", l=la, u=ua)
            for m in range(KT):
                unit(kind="down", l=l, m=m, part=part, segs=segs)
    steps.append(("norm", DEPTH, 0, SEG[1:]))
    return steps, units, fills


MIXERS = ("dn", "hg", "na", "df")
OTHERS, LASTS = (0, 1, 2, 3, 6, 7), (4, 5)
FMPOS = dict(dnq=0, dnk=1 * 2, dnv=2 * 2, hgq=0, hgf=2, hgb=4, naq=0, nak=2, dfq=0, dfk=2)
ZG = 6 * T + 2 * TT * GW
PARTS = ((0, 12), (12, 22))
SLOT = KT * GW
SLOTS = 3


def bank_table(units):
    banks, turns = [], {"act": 0, "dve": 0}
    for u in units:
        u["banks"] = []
        k = u["kind"]
        if k == "ada":
            continue
        if k == "tm":
            outs = [("act", (t, t + 1)) for t in range(u["t0"], TT, 2)]
        elif k == "ba":
            outs = [("act", None)]
        elif k == "fm":
            outs = [("act", (f, s)) for f in range(2) for s in u["segs"]]
        elif k in ("out", "upv"):
            outs = [("dve", (f, s)) for f in range(2) for s in u["segs"]]
        elif k == "upg":
            outs = [("act", (f, s)) for f in range(2) for s in u["segs"]]
        else:
            outs = [("dve", (0, s)) for s in u["segs"]]
        for who, what in outs:
            turns[who] += 1
            b = dict(n=len(banks), who=who, turn=turns[who], what=what)
            u["banks"].append(b)
            banks.append(b)
    return banks


DN_PE = ["tr", "R", "kb", "kk", "kq", "N"] + [f"{x}{i}" for i in range(5) for x in "XY"] + \
        [f"{x}{j}" for j in range(2) for x in "KVO"]
DN_ACT = ["init", "kbT", "exp"] + [f"X{i}" for i in range(5)] + ["V0", "V1"]
DN_DVE = ["kb", "R", "NT", "at", "M"] + [f"L{i}" for i in range(5)] + ["R0", "S0", "R1", "S1", "O"]
HG_PE = ["T"] + [f"L{i}" for i in range(7)] + ["C0", "C1"]
HG_ACT = ["E", "T"]
HG_DVE = ["D", "E", "M1", "M2", "M3", "P0", "M4", "P1", "M5", "P2", "M6", "P3", "P4", "P5", "P6", "U0", "U1", "O"]


def filled(plan, points, piece, lag):
    n = 0
    for n, _ in enumerate(points):
        for u, some in plan[n]:
            if some == [None]:
                piece(u, some)
        for u, some in plan[n - lag] if n >= lag else ():
            if some != [None]:
                piece(u, some)
    assert n + 1 == len(plan), (n + 1, len(plan))
    for k in range(n + 1 - lag, n + 1):
        for u, some in plan[k]:
            if some != [None]:
                piece(u, some)


def planned(units, points):
    plan = [[] for _ in range(points)]
    n = sum(len(u["banks"]) for u in units)
    assert n <= points, (n, points)
    at = 0
    for u in units:
        if u["kind"] == "ada":
            plan[min(at * points // n, points - 1)].append((u, [None]))
        for b in u["banks"]:
            plan[at * points // n].append((u, [b]))
            at += 1
    return plan


class Turns:

    def __init__(self, chain):
        self.chain, self.counts, self.last = chain, {}, None

    def __call__(self, sem=None):
        sem = self.chain if sem is None else sem
        self.counts[sem.name] = self.counts.get(sem.name, 0) + 1
        self.last = (sem, self.counts[sem.name])
        return sem, 1


PR_PE = [f"n{i}" for i in range(4)] + ["cum"]
PR_ACT = [f"{x}{i}" for i in range(6) for x in "ms"] + [f"{x}{i}" for i in range(4) for x in "qr"] + ["b1", "b2", "b3"]
PR_DVE = [f"c{i}" for i in range(6)] + [f"l{i}" for i in range(4)] + ["b1", "b2", "b3", "b4"]
HP_ACT = ["lb1", "lb2"] + [f"{x}{i}" for i in range(4) for x in "ek"]
HP_DVE = ["lb1", "lb2"] + [f"{x}{i}" for i in range(4) for x in "clb"]
DP_PE = [f"r{i}" for i in range(4)]
DP_DVE = ["d"] + [f"r{i}" for i in range(4)] + ["lam"]


def at(order, n, name):
    return n * len(order) + order.index(name) + 1


def at2(order, n, name, d):
    return 2 * (n * len(order) + order.index(name)) + d + 1


def hybrid_backbone(nc, A, out):
    fp32, bf16, u8 = mybir.dt.float32, mybir.dt.bfloat16, mybir.dt.uint8
    ALU = mybir.AluOpType
    ACT = mybir.ActivationFunctionType
    AX = mybir.AxisListType
    MUL, ADD, SUB, MAX, MIN = ALU.mult, ALU.add, ALU.subtract, ALU.max, ALU.min

    steps, units, fills = schedule()
    banks = bank_table(units)
    del banks
    ctx = ExitStack()
    with ctx:
        def sb(name, cols, dt=fp32):
            return ctx.enter_context(nc.sbuf_tensor(name, [P, cols], dt))

        def sem(name):
            return ctx.enter_context(nc.semaphore(name))

        X = sb("residual", KT * T)
        H = sb("normed", KT * T)
        Y = sb("mixed", KT * T)
        Z = sb("projected", 2 * ZG)
        RING = sb("ring", SLOTS * SLOT)
        SC = sb("silu_c", 2 * DM)
        JUNK = sb("junk", DM, bf16)
        CST = sb("constants", NC_)
        MSK = sb("level_masks", 2 * (LEVELS + 1) * P, u8)
        SM = sb("small", DEPTH * NW)
        FIN = sb("final_w", KT)
        MOD = sb("modulation", DEPTH * 2 * 48)
        AB = sb("norm_gain", 5 * 2 * KT)
        LBV = sb("lower_bounds", 16)
        ST = sb("stats", 192)
        SCR = sb("scratch", 5120)
        PS = ctx.enter_context(nc.psum_tensor("psum", [P, 8 * 512], fp32))

        def bank(b, a=0, e=512):
            return PS[:, 512 * b + a:512 * b + e]

        def seg3(t, n, w=T):
            return t.rearrange("p (n w) -> p n w", n=n, w=w)

        Xv, Hv, Yv = seg3(X[:, :], KT), seg3(H[:, :], KT), seg3(Y[:, :], KT)
        IDN = CST[:, C_ID:C_ID + P]
        cc = lambda c, n=1: CST[:, c:c + n]
        sm = lambda l, c, n=1: SM[:, l * NW + c:l * NW + c + n]
        mod = lambda l, v, c, n=1: MOD[:, (2 * l + v) * 48 + c:(2 * l + v) * 48 + c + n]
        mask = lambda d, lv: MSK[:, ((LEVELS + 1) * d + lv) * P:((LEVELS + 1) * d + lv + 1) * P]
        h4 = lambda ap: ap.rearrange("p (h n) -> p h n", h=NH)
        four = lambda ap: ap[:, None, :].to_broadcast([ap.shape[0], NH, ap.shape[1]])

        loaded = sem("small_inputs_loaded")
        stored = sem("output_stored")
        arrived = [sem(f"weights_arrived_{i}") for i in range(SLOTS)]
        masks_ready = sem("level_masks_are_bytes")
        silu_ready = sem("silu_c_ready")
        ada_done = sem("ada_unit_done")
        gemm_ready = sem("gemm_bank_filled")
        gemm_act = sem("gemm_bank_emptied_by_act")
        gemm_dve = sem("gemm_bank_emptied_by_dve")
        sq_ready = sem("norm_square_ready")
        sq_used = sem("norm_square_summed")
        rstd_ready = sem("norm_rstd_ready")
        scaled = sem("norm_scaled")
        normed = sem("norm_shifted")
        conv_done = sem("ffn_conv_done")
        silu_done = sem("ffn_silu_done")
        prep_pe, prep_act, prep_dve = sem("prep_pe"), sem("prep_act"), sem("prep_dve")
        dn_pe, dn_act, dn_dve = sem("dn_pe"), sem("dn_act"), sem("dn_dve")
        hg_pe, hg_act, hg_dve = sem("hg_pe"), sem("hg_act"), sem("hg_dve")
        hp_act, hp_dve = sem("hg_prep_act"), sem("hg_prep_dve")
        dp_pe, dp_act, dp_dve = sem("df_prep_pe"), sem("df_prep_act"), sem("df_prep_dve")
        bias_pe, bias_dve = sem("na_bias_filled"), sem("na_bias_masked")
        at_s, at_max, at_exp, at_p = sem("at_scores"), sem("at_max"), sem("at_exp"), sem("at_probs")
        at_tr, at_pt, at_pv, at_o = sem("at_transposed"), sem("at_pt"), sem("at_pv"), sem("at_o")
        post_dve, post_act, post_pe, y_done = sem("post_dve"), sem("post_act"), sem("post_pe"), sem("y_tile_pair_done")
        pe_chain, act_chain, dve_chain = sem("pe_chain"), sem("act_chain"), sem("dve_chain")
        N_LOADS = 7

        release, nb, na = [], 0, 0
        ring_units = [u for u in units if u["kind"] != "ba"]
        for u in units:
            nb += len(u["banks"])
            if u["kind"] == "ada":
                na += 1
            if u["kind"] != "ba":
                u["r"] = len(release)
                release.append((ada_done, na) if u["kind"] == "ada" else (gemm_ready, nb))

        def slot(u, n=SLOT):
            o = (u["r"] % SLOTS) * SLOT
            return RING[:, o:o + n]

        def weights(u):
            return arrived[u["r"] % SLOTS], 16 * (u["r"] // SLOTS + 1)

        acts_before, dves_before = {}, {}
        turn = {"act": 0, "dve": 0}
        norms = pairs = pair = 0
        vals = []
        for st in steps:
            if st[0] == "norm":
                dves_before[norms] = turn["dve"]
                norms += 1
            elif st[0] != "unit":
                acts_before[st] = turn["act"]
            for u in [st[1]] if st[0] == "unit" else fills.get(st, ()):
                u["norms"], u["pairs"], u["acts"] = norms, pairs, turn["dve"]
                if u["kind"] == "upg":
                    u["pair"], u["vals2"] = pair, vals[-2] if pair >= 2 else 0
                for b in u["banks"]:
                    turn[b["who"]] = b["turn"]
                if u["kind"] == "upv":
                    u["pair"] = pair
                    pair += 1
                    vals.append(turn["dve"])
                if u["kind"] == "down" and u["m"]:
                    u["acts"] = part_acts
                else:
                    part_acts = u["acts"]
            if st[0] in MIXERS:
                pairs += (TT - (CT if st[1] == DEPTH - 1 else 0)) // 2

        ORD = ([0, 1, 2, 3, 4, 5], [1, 0, 5, 4, 3, 2])

        YS = 2 * T
        def dn_buf(d, name, n):
            off = dict(kb=0, rhs=0, kbT=256, vn=256, vb=512, kdec=768, D=1024, X=1024, t=1024, NT=1536,
                       at=2048, Tm=2560, TTm=3072)[name]
            return Y[:, YS + off:YS + off + n] if d == 0 else SCR[:, 1536 + off:1536 + off + n]
        O = SCR[:, 0:TT * GW]
        DNS = [Y[:, YS + 3584 + 128 * d:YS + 3712 + 128 * d] for d in range(2)]
        BAO = YS + 3840
        ba = lambda i: Y[:, BAO + 48 * i:BAO + 48 * (i + 1)]
        BETA, NBETA, LOGA, G, EG, EDEC, NEGB, TOT, EGL = 2, 3, 4, 5, 6, 7, 8, 9, 10
        PRB = SCR[:, 1536:1536 + 3 * T]
        FFG = [Y[:, p * 2 * T:(p + 1) * 2 * T] for p in range(2)]
        FFC = [Y[:, (p + 2) * 2 * T:(p + 3) * 2 * T] for p in range(2)]
        NSQ = [SCR[:, p * T:(p + 1) * T] for p in range(2)]
        RSTD = SCR[:, 2 * T:3 * T]
        HB = lambda d, f: Y[:, (2 + 2 * d + f) * T:(3 + 2 * d + f) * T]
        HE = Y[:, 6 * T:8 * T].rearrange("p (l n) -> p l n", l=LEVELS)
        QKT = [SCR[:, 1536 + 512 * i:2048 + 512 * i] for i in range(3)]
        ATT = SCR[:, 3072:3584]
        HQB, HKE, HKT = SCR[:, 3584:3840], SCR[:, 3840:4096], SCR[:, 4096:4352]
        HGS = [SCR[:, 4352 + 128 * d:4480 + 128 * d] for d in range(2)]
        HDE = ST[:, 96:100]
        NAB = SCR[:, 1536:3328]
        NPT = [SCR[:, 3328 + T * i:3328 + T * (i + 1)] for i in range(2)]
        NP_ = [Y[:, (4 + i) * T:(5 + i) * T] for i in range(2)]
        DPP = [SCR[:, 1536 + 1536 * i:3072 + 1536 * i] for i in range(2)]
        DPT = [Y[:, (4 + i) * T:(5 + i) * T] for i in range(2)]

        region = {"dn": 0, "hg": ZG, "na": 0, "df": ZG}
        fm = lambda g, f: Z[:, region[g] + f * T:region[g] + (f + 1) * T]
        tm = lambda g, i: Z[:, region[g] + 6 * T + i * TT * GW:region[g] + 6 * T + (i + 1) * TT * GW]

        items, parts0 = {}, {}
        n_items = n_parts = 0
        for st in steps:
            if st[0] in ("na", "df"):
                l = st[1]
                qt = range(CT if l == DEPTH - 1 else 0, TT)
                items[st] = (n_items, [(h, t) for h in range(NH) for t in qt])
                n_items += len(items[st][1])
                parts0[st] = n_parts
                n_parts += len(items[st][1]) * (1 if st[0] == "na" else 2)

        def part(st, i, j=0):
            return parts0[st] + (i + 1 if st[0] == "na" else 2 * i + j + 1)

        def new_pair(st, i):
            todo = items[st][1]
            return st[0] == "na" and i < len(todo) and todo[i][0] % 2 == 0 and (i == 0 or todo[i - 1][0] != todo[i][0])
        def points(st):
            return {"dn": 4 * TT, "hg": 4 * TT}.get(st[0]) or len(items[st][1]) + 2

        plans = {st: planned(us, points(st)) for st, us in fills.items()}
        posts, n_norm, n_pair = {}, 0, 0
        mixers = [st for st in steps if st[0] in ("dn", "hg", "na", "df")]
        for st in mixers:
            t0 = CT if st[1] == DEPTH - 1 else 0
            posts[st] = (n_norm, n_pair, t0)
            n_norm += st[0] != "na"
            n_pair += (TT - t0) // 2
        YT = {"dn": 0, "na": 2, "df": 4, "hg": 6}
        before = {st: sum((TT - posts[m][2]) // 2 for m in mixers[:i]) for i, st in enumerate(mixers)}
        norm_at = [st for st in steps if st[0] == "norm"]
        block = ctx.enter_context(nc.Block())

        @block.sync
        def _(sp):
            for dst, src in ((CST[:, :], A["const"]), (SC[:, :], A["c"]), (Z[:, 0:2 * (LEVELS + 1) * P], A["masks"]), (FIN[:, :], A["fin"])):
                sp.dma_start(dst, src[:, :]).then_inc(loaded, 16)
            for l in range(DEPTH):
                sp.dma_start(SM[:, l * NW:(l + 1) * NW], A["small"][l]).then_inc(loaded, 16)
            sp.dma_start(X[:, :], A["x"][:, :]).then_inc(loaded, 16)
            for r, u in enumerate(ring_units):
                if r >= SLOTS:
                    sp.wait_ge(*release[r - SLOTS])
                k, l = u["kind"], u["l"]
                n = SLOT
                if k == "ada":
                    src = A["ada"][l, u["u"]]
                elif k in ("fm", "tm"):
                    src = A["win"][l, u["col"]]
                elif k == "out":
                    src = A["wout"][l, u["u"]]
                elif k in ("upg", "upv"):
                    src = A["wup"][l, u["u"] + (0 if k == "upg" else FT // 2)]
                else:
                    a, b = PARTS[u["part"]]
                    n = (b - a) * P
                    src = A["wdn"][l, u["m"]][:, a * P:b * P]
                sp.dma_start(slot(u, n), src).then_inc(arrived[r % SLOTS], 16)
            sp.wait_ge(scaled, KT * len(norm_at))
            sp.dma_start(out[:, :, :], Hv[:, :, CTX:T]).then_inc(stored, 16)
            sp.wait_ge(stored, 16)

        @block.tensor
        def _(pe):
            own = Turns(pe_chain)
            mm, tr = nc.tensor.matmul, nc.tensor.transpose
            emptied = []

            def gemm_unit(u, some=None):
                k, l = u["kind"], u["l"]
                if k == "ada":
                    return
                if k != "ba":
                    pe.wait_ge(*weights(u))
                if k in ("fm", "tm", "ba", "upg", "upv"):
                    pe.wait_ge(normed, KT * u["norms"])
                if k == "out":
                    pe.wait_ge(y_done, u["pairs"])
                if k == "down":
                    pe.wait_ge(gemm_dve, u["acts"])
                for b in some or u["banks"]:
                    if len(emptied) >= 2:
                        pe.wait_ge(*emptied[-2])
                    emptied.append((gemm_act if b["who"] == "act" else gemm_dve, b["turn"]))
                    ps = bank(b["n"] % 2)
                    if k == "tm":
                        for i, t in enumerate(b["what"]):
                            for kk in range(KT):
                                last = mm(ps[:, i * GW:(i + 1) * GW], Hv[:, kk, t * P:(t + 1) * P],
                                          slot(u)[:, kk * GW:(kk + 1) * GW], start=kk == 0, stop=kk == KT - 1)
                                if kk % 2:
                                    yield
                    elif k == "ba":
                        for t in range(TT):
                            for kk in range(KT):
                                last = mm(ps[:, t * 16:(t + 1) * 16], Hv[:, kk, t * P:(t + 1) * P],
                                          sm(l, W_BA + kk * 16, 16), start=kk == 0, stop=kk == KT - 1)
                    else:
                        f, (a, e) = b["what"]
                        if k == "down":
                            p0, p1 = PARTS[u["part"]]
                            nk, src, step = p1 - p0, Z, P
                        else:
                            nk, src, step = KT, (Y if k == "out" else H), GW
                        ks = u["rows"] if k == "out" else range(nk)
                        for kk in ks:
                            o = kk * step + f * P
                            last = mm(ps[:, 0:e - a], slot(u)[:, o:o + P], src[:, kk * T + a:kk * T + e],
                                      start=kk == ks[0], stop=kk == ks[-1])
                            if e - a > CTX or kk % 2:
                                yield
                    last.then_inc(*own(gemm_ready))

            def norm(ni, segs):
                pe.wait_ge(rstd_ready, ni)
                for k in range(KT):
                    pe.wait_ge(sq_ready, KT * ni + k + 1)
                    for i, (a, e) in enumerate(segs):
                        last = mm(bank(2 + i, 0, e - a), cc(C_MEAN, P), NSQ[k % 2][:, a:e],
                                  start=k == 0, stop=k == KT - 1)
                    last.then_inc(*own(sq_used))

            def dn(l):
                for i in range(4):
                    pe.wait_ge(prep_act, at(PR_ACT, l, f"q{i}"))
                    mm(bank(2, 0, CTX), cc(C_BLK, P), PRB[:, (i % 2) * T:(i % 2) * T + CTX], start=True, stop=True)
                    mm(bank(3), cc(C_BLK, P), PRB[:, (i % 2) * T + CTX:(i % 2 + 1) * T], start=True, stop=True).then_inc(*own(prep_pe))
                pe.wait_ge(prep_dve, at(PR_DVE, l, "b2"))
                LG = ba(LOGA).rearrange("p (t d h) -> p t d h", t=TT, d=2)
                gp = bank(4, 0, 48).rearrange("p (t d h) -> p t d h", t=TT, d=2)
                for d in range(2):
                    mm(gp[:, :, d, :], cc(C_INC + d * P, P), LG[:, :, d, :], start=True, stop=True)
                mm(bank(4, 48, 96), cc(C_BLK, P), ba(LOGA), start=True, stop=True)
                for t in range(TT):
                    for d in range(2):
                        for hp in range(2):
                            o = 96 + ((t * 2 + d) * 2 + hp) * 2
                            for h in range(2):
                                last = mm(bank(4, o, o + 2)[64 * h:64 * h + 64, :],
                                          LG[:, t, d, 2 * hp + h:2 * hp + h + 1].to_broadcast([P, HD]),
                                          cc(C_CHK, 2), start=True, stop=True)
                last.then_inc(*own(prep_pe))
                pe.wait_ge(prep_dve, at(PR_DVE, l, "b4"))
                pe.wait_ge(prep_act, at(PR_ACT, l, "b3"))
                for n in range(TT):
                    g = TT * l + n
                    A, B, C = [bank(2), bank(5)], [bank(3), bank(6)], [bank(4), bank(7)]
                    tile = [ORD[d][n] for d in range(2)]
                    cols = [slice(t * P, (t + 1) * P) for t in tile]

                    def done(ins):
                        ins.then_inc(*own(dn_pe))

                    def by_rows(product):
                        for odd in range(2):
                            if odd:
                                last.then_inc(*own())
                                pe.wait_ge(*own.last)
                            for h in (odd, odd + 2):
                                last = product(h, slice(64 * odd, 64 * odd + 64))
                        done(last)

                    for d in range(2):
                        if g:
                            pe.wait_ge(dn_dve, at2(DN_DVE, g - 1, "O", d))
                        for i, f in enumerate((2, 3, 4, 5)):
                            last = tr(A[d][:, i * P:(i + 1) * P], fm("dn", f)[:, cols[d]], IDN)
                        done(last)
                        yield False
                    for d in range(2):
                        for h in range(NH):
                            last = mm(C[d][:, h * P:(h + 1) * P], LG[:, tile[d], d, h:h + 1].to_broadcast([P, P]),
                                      cc(C_INC + d * P, P), start=True, stop=True)
                        done(last)
                        yield False
                    yield True
                    for d in range(2):
                        pe.wait_ge(dn_dve, at2(DN_DVE, g, "kb", d))
                        for i in range(2):
                            last = tr(B[d][:, i * P:(i + 1) * P], dn_buf(d, "kb", 256)[:, i * P:(i + 1) * P], IDN)
                        done(last)
                        yield False
                    for d in range(2):
                        pe.wait_ge(dn_act, at2(DN_ACT, g, "kbT", d))
                        by_rows(lambda h, r: mm(
                            A[d][:, h * P:(h + 1) * P], fm("dn", 2 + h // 2)[r, cols[d]],
                            dn_buf(d, "kbT", 256)[r, (h // 2) * P:(h // 2 + 1) * P], start=True, stop=True))
                        yield False
                    for d in range(2):
                        by_rows(lambda h, r: mm(
                            B[d][:, h * P:(h + 1) * P], fm("dn", 2 + h // 2)[r, cols[d]],
                            fm("dn", h // 2)[r, cols[d]], start=True, stop=True))
                        yield False
                    for d in range(2):
                        pe.wait_ge(dn_dve, at2(DN_DVE, g, "NT", d))
                        for h in range(NH):
                            last = tr(C[d][:, h * P:(h + 1) * P], dn_buf(d, "NT", 512)[:, h * P:(h + 1) * P], IDN)
                        done(last)
                        yield False
                    yield True
                    for i in range(5):
                        for d in range(2):
                            pe.wait_ge(dn_dve, at2(DN_DVE, g, "M" if i == 0 else f"L{i - 1}", d))
                            if i < 5:
                                for h in range(NH):
                                    hs = slice(h * P, (h + 1) * P)
                                    last = mm(A[d][:, hs], dn_buf(d, "NT", 512)[:, hs], dn_buf(d, "Tm", 512)[:, hs],
                                              start=True, stop=True)
                            done(last)
                            yield False
                        for d in range(2):
                            pe.wait_ge(dn_act, at2(DN_ACT, g, f"X{i}", d))
                            for h in range(NH):
                                hs = slice(h * P, (h + 1) * P)
                                last = mm(B[d][:, hs], dn_buf(d, "X", 512)[:, hs], dn_buf(d, "TTm", 512)[:, hs],
                                          start=True, stop=True)
                            if i < 4:
                                for h in range(NH):
                                    hs = slice(h * P, (h + 1) * P)
                                    last = mm(C[d][:, hs], dn_buf(d, "TTm", 512)[:, hs], dn_buf(d, "X", 512)[:, hs],
                                              start=True, stop=True)
                            done(last)
                            yield False
                    yield True
                    for j in range(2):
                        if j:
                            yield True
                        for d in range(2):
                            pe.wait_ge(dn_dve, at2(DN_DVE, g, "L4" if j == 0 else "S0", d))
                            c = j if d == 0 else 1 - j
                            rows = slice(64 * c, 64 * c + 64)
                            t0 = tile[d] * P + 64 * c

                            def read(h, r):
                                for w in range(2):
                                    f = (2 if w == 0 else 0) + h // 2
                                    o = w * GW + h * HD
                                    last = mm(A[d][rows, o:o + HD], fm("dn", f)[r, t0:t0 + 64],
                                              DNS[d][r, (h // 2) * HD:(h // 2 + 1) * HD], start=True, stop=True)
                                return last
                            by_rows(read)
                            yield False
                        for d in range(2):
                            pe.wait_ge(dn_dve, at2(DN_DVE, g, f"R{j}", d))
                            c = j if d == 0 else 1 - j
                            rows = slice(64 * c, 64 * c + 64)
                            for h in range(NH):
                                last = mm(B[d][rows, h * HD:(h + 1) * HD],
                                          dn_buf(d, "TTm", 512)[rows, h * P + 64 * c:h * P + 64 * c + 64],
                                          dn_buf(d, "rhs", 256)[rows, h * HD:(h + 1) * HD], start=True, stop=True)
                            done(last)
                            yield False
                        for d in range(2):
                            pe.wait_ge(dn_act, at2(DN_ACT, g, f"V{j}", d))
                            c = j if d == 0 else 1 - j
                            rows = slice(64 * c, 64 * c + 64)
                            vn = dn_buf(d, "vn", 256)
                            for h in range(NH):
                                r = slice(64 * (h % 2), 64 * (h % 2) + 64)
                                mm(B[d][r, 256 + (h // 2) * HD:256 + (h // 2 + 1) * HD],
                                   dn_buf(d, "kdec", 256)[rows, h * HD:(h + 1) * HD], vn[rows, h * HD:(h + 1) * HD],
                                   start=True, stop=True)
                            for h in range(NH):
                                last = mm(C[d][rows, h * HD:(h + 1) * HD],
                                          dn_buf(d, "at", 512)[rows, h * P + 64 * c:h * P + 64 * c + 64],
                                          vn[rows, h * HD:(h + 1) * HD], start=True, stop=True)
                            done(last)
                            yield False

            def hg(l):
                pe.wait_ge(hp_dve, at(HP_DVE, l, "b3"))
                pe.wait_ge(hp_act, at(HP_ACT, l, "k3"))
                for n in range(TT):
                    for d in range(2):
                        q = 2 * (TT * l + n) + d
                        t = ORD[d][n]
                        cs = slice(t * P, (t + 1) * P)
                        pe.wait_ge(hg_dve, at(HG_DVE, q, "E"))
                        if q:
                            pe.wait_ge(hg_act, at(HG_ACT, q - 1, "T"))
                        for i in range(2):
                            last = tr(bank(2, i * P, (i + 1) * P), HKE[:, i * P:(i + 1) * P], IDN)
                        last.then_inc(*own(hg_pe))
                        yield False
                        yield True
                        for lv in range(LEVELS + 1):
                            if lv:
                                pe.wait_ge(hg_dve, at(HG_DVE, q, f"M{lv}"))
                            b = 3 + lv % 3
                            if lv >= 3:
                                pe.wait_ge(hg_dve, at(HG_DVE, q, f"P{lv - 3}"))
                            elif q:
                                pe.wait_ge(hg_dve, at(HG_DVE, q - 1, "P6"))
                            for h in (0, 2, 1, 3):
                                r = slice(64 * (h % 2), 64 * (h % 2) + 64)
                                f = h // 2
                                if h == 1:
                                    last.then_inc(*own())
                                    pe.wait_ge(*own.last)
                                if lv == 0:
                                    kk, qq = fm("hg", 2 + 2 * d + f)[r, cs], fm("hg", f)[r, cs]
                                else:
                                    w = QKT[lv % 3]
                                    qq, kk = w[r, f * P:(f + 1) * P], w[r, 256 + f * P:256 + (f + 1) * P]
                                last = mm(bank(b, h * P, (h + 1) * P), kk, qq, start=True, stop=True)
                            last.then_inc(*own(hg_pe))
                            yield False
                        yield True
                        for j in range(2):
                            c = j if d == 0 else 1 - j
                            rows = slice(64 * c, 64 * c + 64)
                            pe.wait_ge(hg_dve, at(HG_DVE, q, "P6" if j == 0 else "U0"))
                            pe.wait_ge(hg_act, at(HG_ACT, q, "T"))
                            if q:
                                pe.wait_ge(hg_dve, at(HG_DVE, q - 1, "O"))
                            v = tm("hg", 0)[:, t * GW:(t + 1) * GW]
                            for h in range(NH):
                                hc = slice(h * HD, (h + 1) * HD)
                                last = mm(bank(6)[rows, hc], ATT[rows, h * P + 64 * c:h * P + 64 * c + 64], v[rows, hc],
                                          start=h == 0, stop=False, skip_group_check=True)
                            for h in (0, 2, 1, 3):
                                r = slice(64 * (h % 2), 64 * (h % 2) + 64)
                                f = h // 2
                                hc = slice(h * HD, (h + 1) * HD)
                                if h < 2:
                                    last.then_inc(*own())
                                    pe.wait_ge(*own.last)
                                last = mm(bank(6)[rows, hc], HQB[r, f * P + 64 * c:f * P + 64 * c + 64],
                                          HGS[d][r, f * HD:(f + 1) * HD], start=False, stop=True, skip_group_check=True)
                            for h in range(NH):
                                r = slice(64 * (h % 2), 64 * (h % 2) + 64)
                                f = h // 2
                                hc = slice(h * HD, (h + 1) * HD)
                                last = mm(bank(7)[r, f * HD:(f + 1) * HD], HKT[rows, hc], v[rows, hc], start=True, stop=True)
                            last.then_inc(*own(hg_pe))
                            yield False

            def attend(st):
                kind, l = st
                i0, todo = items[st]
                na = kind == "na"
                v = tm(kind, 0)
                tr_b, pv_b = PS[:, 6 * 512:6 * 512 + T], bank(7, 256, 256 + HD)

                def bias(hp):
                    for rnd in range(4):
                        gi = 4 * (2 * l + hp) + rnd
                        if rnd >= 2:
                            pe.wait_ge(bias_dve, gi - 1)
                        for k in range(16):
                            s = 63 - (rnd * 16 + k)
                            last = mm(bank(2 + 2 * (rnd % 2), k * 28, (k + 1) * 28), CST[0:64, C_AJ + s:C_AJ + s + P],
                                      SM[0:64, l * NW + W_RPB + hp * 28:l * NW + W_RPB + (hp + 1) * 28],
                                      start=True, stop=True)
                        last.then_inc(*own(bias_pe))

                def scores(i, j):
                    h, t = todo[i]
                    s = 64 * (h % 2) + 32 * j
                    r = slice(s, s + (64 if na else 32))
                    qq = fm(kind, h // 2)[r, t * P:(t + 1) * P]
                    kk = fm(kind, 2 + h // 2)
                    b0 = 512 * (2 + 2 * ((i0 + i) % 2 if na else j))
                    if t >= CT:
                        mm(PS[:, b0:b0 + LAT], qq, kk[r, CTX:T], start=True, stop=True)
                    mm(PS[:, b0 + LAT:b0 + T], qq, kk[r, 0:CTX], start=True, stop=True).then_inc(*own(at_s))

                def keys_of(i):
                    return [(o, (o + CT) if o < 4 else o - 4) for o in (range(6) if todo[i][1] >= CT else (4, 5))]

                def values(i):
                    h, g = todo[i][0], i0 + i
                    pt = (NPT if na else DPT)[g % 2]
                    pe.wait_ge(at_pt, g + 1)
                    kts = keys_of(i)
                    for o, kt in kts:
                        last = mm(pv_b, pt[:, o * P:(o + 1) * P], v[:, kt * GW + h * HD:kt * GW + (h + 1) * HD],
                                  start=o == kts[0][0], stop=o == kts[-1][0])
                    last.then_inc(*own(at_pv))

                def transposes(i):
                    g = i0 + i
                    prob = NP_[g % 2] if na else DPP[g % 2][:, 0:T]
                    pe.wait_ge(at_p, g + 1)
                    pe.wait_ge(at_o, g)
                    for o, _ in keys_of(i):
                        last = tr(tr_b[:, o * P:(o + 1) * P], prob[:, o * P:(o + 1) * P], IDN)
                    last.then_inc(*own(at_tr))

                n = len(todo)
                for i in range(n + 2):
                    if new_pair(st, i):
                        if i:
                            pe.wait_ge(at_exp, part(st, i - 1))
                        bias(todo[i][0] // 2)
                        pe.wait_ge(bias_dve, 4 * (2 * l + todo[i][0] // 2) + 4)
                    if i < n:
                        for j in range(1 if na else 2):
                            back = 2 if na else 1
                            if i >= back:
                                pe.wait_ge(at_exp, part(st, i - back, j))
                            scores(i, j)
                            yield False
                    yield False
                    if i >= 2:
                        values(i - 2)
                    yield False
                    yield False
                    if 0 < i <= n:
                        transposes(i - 1)
                    yield True

            def df(st):
                l = st[1]
                for i in range(4):
                    mm(bank(2 + i), cc(C_ROT, P), fm("df", i)[:, CTX:T], start=True, stop=True).then_inc(*own(dp_pe))
                pe.wait_ge(dp_dve, at(DP_DVE, l, "lam"))
                yield from attend(st)

            def post(st):
                _, p0, t0 = posts[st]
                if st[0] != "na":
                    pe.wait_ge(post_dve, 2 * (posts[st][0] + 1))
                else:
                    pe.wait_ge(at_o, items[st][0] + len(items[st][1]))
                for i, t in enumerate(range(t0, TT, 2)):
                    b = 2 + i
                    for f in range(2):
                        for k in range(2):
                            o = f * GW + k * P
                            last = tr(bank(b, o, o + P), O[:, (t + k) * GW + f * P:(t + k) * GW + (f + 1) * P], IDN)
                    last.then_inc(*own(post_pe))

            pe.wait_ge(loaded, 16 * N_LOADS)
            for st in steps:
                kind = st[0]
                if kind == "unit":
                    for _ in gemm_unit(st[1]):
                        pass
                elif kind == "norm":
                    norm(norm_at.index(st), st[3])
                else:
                    pe.wait_ge(gemm_act, acts_before[st])
                    pe.wait_ge(y_done, before[st])
                    body = dn(st[1]) if kind == "dn" else hg(st[1]) if kind == "hg" else df(st) if kind == "df" else attend(st)
                    work, k = iter(()), 0
                    for shared in body:
                        if shared:
                            for _ in work:
                                pass
                            work = chain.from_iterable(gemm_unit(*piece) for piece in plans[st][k])
                            k += 1
                        else:
                            next(work, None)
                    for _ in work:
                        pass
                    post(st)

        @block.scalar
        def _(act):
            own = Turns(act_chain)
            af = nc.scalar.activation
            eps, one = cc(C_EPS), cc(C_ONE)

            def gemm_unit(u, some=None):
                k, l = u["kind"], u["l"]
                for b in some or u["banks"]:
                    if b is None or b["who"] != "act":
                        continue
                    act.wait_ge(gemm_ready, b["n"] + 1)
                    ps = bank(b["n"] % 2)
                    if k == "ba":
                        af(Y[:, BAO:BAO + 96], ps[:, 0:96], ACT.Copy).then_inc(*own(gemm_act))
                    elif k == "tm":
                        t = b["what"][0]
                        o = u["z"] + t * GW
                        af(Z[:, o:o + 2 * GW], ps, ACT.Copy).then_inc(*own(gemm_act))
                    elif k == "fm":
                        f, (a, e) = b["what"]
                        o = u["z"] + f * T
                        af(Z[:, o + a:o + e], ps[:, 0:e - a], ACT.Copy, scale=u["scale"]).then_inc(*own(gemm_act))
                    else:
                        f, (a, e) = b["what"]
                        p = u["pair"]
                        if p >= 2:
                            act.wait_ge(conv_done, p - 1)
                            act.wait_ge(gemm_dve, u["vals2"])
                        af(FFG[p % 2][:, f * T + a:f * T + e], ps[:, 0:e - a], ACT.Copy).then_inc(*own())
                        w1 = sm(l, W_FFC + (2 * u["u"] + f) * 3 + 1)
                        af(FFC[p % 2][:, f * T + a:f * T + e], ps[:, 0:e - a], ACT.Copy, scale=w1).then_inc(*own(gemm_act))
                if k == "upv":
                    p = u["pair"]
                    act.wait_ge(conv_done, p + 1)
                    a = u["segs"][0][0]
                    v = seg3(FFC[p % 2], 2)[:, :, a:T]
                    af(v, v, ACT.Silu).then_inc(*own(silu_done))

            def rsqrt(dst, src, scale=1.0, last=None):
                af(dst, src, ACT.Ln, bias=eps, scale=scale).then_inc(*own())
                act.wait_ge(*own.last)
                af(dst, dst, ACT.Exp, scale=-0.5).then_inc(*own(last))

            def norm(ni, segs, l):
                a0 = segs[0][0]
                if ni:
                    act.wait_ge(gemm_dve, dves_before[ni])
                for k in range(KT):
                    if KT * ni + k >= 2:
                        act.wait_ge(sq_used, KT * ni + k - 1)
                    af(NSQ[k % 2][:, a0:T], Xv[:, k, a0:T], ACT.Square).then_inc(*own(sq_ready))
                act.wait_ge(sq_used, KT * (ni + 1))
                for i, (a, e) in enumerate(segs):
                    af(RSTD[:, a:e], bank(2 + i, 0, e - a), ACT.Ln, bias=eps).then_inc(*own())
                act.wait_ge(*own.last)
                af(RSTD[:, a0:T], RSTD[:, a0:T], ACT.Exp, scale=-0.5).then_inc(*own(rstd_ready))
                if l == DEPTH:
                    return
                for k in range(KT):
                    act.wait_ge(scaled, KT * ni + k + 1)
                    for i, (a, e) in enumerate(segs):
                        shift = mod(l, 0 if a == 0 else 1, (0 if ni % 2 == 0 else 24) + k)
                        last = af(Hv[:, k, a:e], Hv[:, k, a:e], ACT.Identity, bias=shift)
                        last.then_inc(*own(normed if i == len(segs) - 1 else None))

            def dn(l):
                P3 = lambda i: PRB[:, i * T:(i + 1) * T]
                for f in range(6):
                    if f >= 2:
                        act.wait_ge(prep_act, at(PR_ACT, l, f"s{f - 2}"))
                    af(P3(f % 2), fm("dn", f), ACT.Copy, scale=sm(l, W_DNC + f * 3 + 1)).then_inc(*own(prep_act))
                    act.wait_ge(prep_dve, at(PR_DVE, l, f"c{f}"))
                    af(fm("dn", f), P3(f % 2), ACT.Silu).then_inc(*own(prep_act))
                for f in range(4):
                    act.wait_ge(prep_act, at(PR_ACT, l, f"s{f if f > 3 else 5}"))
                    if f >= 2:
                        act.wait_ge(prep_pe, at(PR_PE, l, f"n{f - 2}"))
                    af(P3(f % 2), fm("dn", f), ACT.Square).then_inc(*own(prep_act))
                    act.wait_ge(prep_pe, at(PR_PE, l, f"n{f}"))
                    if f:
                        act.wait_ge(prep_dve, at(PR_DVE, l, f"l{f - 1}"))
                    af(P3(2)[:, 0:CTX], bank(2, 0, CTX), ACT.Ln, bias=eps).then_inc(*own())
                    af(P3(2)[:, CTX:T], bank(3), ACT.Ln, bias=eps).then_inc(*own())
                    act.wait_ge(*own.last)
                    af(P3(2), P3(2), ACT.Exp, scale=-0.5).then_inc(*own(prep_act))
                act.wait_ge(prep_dve, at(PR_DVE, l, "b1"))
                af(ba(BETA), ba(NEGB), ACT.Exp, scale=-1.0).then_inc(*own())
                af(ba(EDEC), ba(EG), ACT.Exp, scale=-1.0).then_inc(*own())
                af(ba(TOT)[:, 0:8], sm(l, W_ALOG, 8), ACT.Exp).then_inc(*own())
                act.wait_ge(*own.last)
                af(ba(EDEC), ba(EDEC), ACT.Ln, bias=one).then_inc(*own(prep_act))
                act.wait_ge(prep_pe, at(PR_PE, l, "cum"))
                af(ba(G), bank(4, 0, 48), ACT.Copy).then_inc(*own())
                af(ba(TOT), bank(4, 48, 96), ACT.Copy).then_inc(*own())
                af(ba(EG), bank(4, 0, 48), ACT.Exp).then_inc(*own())
                af(ba(EGL), bank(4, 96, 144), ACT.Exp).then_inc(*own(prep_act))
                act.wait_ge(prep_dve, at(PR_DVE, l, "b3"))
                af(ba(EDEC), ba(EDEC), ACT.Exp).then_inc(*own(prep_act))
                for n in range(TT):
                    g = TT * l + n
                    B, A = [bank(3), bank(6)], [bank(2), bank(5)]
                    for d in range(2):
                        if n:
                            act.wait_ge(dn_dve, at2(DN_DVE, g - 1, "O", d))
                        af(h4(dn_buf(d, "Tm", 512)), four(IDN), ACT.Copy).then_inc(*own())
                        af(h4(dn_buf(d, "TTm", 512)), four(IDN), ACT.Copy).then_inc(*own(dn_act))
                    yield
                    for d in range(2):
                        act.wait_ge(dn_pe, at2(DN_PE, g, "kb", d))
                        af(dn_buf(d, "kbT", 256), B[d][:, 0:256], ACT.Copy).then_inc(*own(dn_act))
                    for d in range(2):
                        act.wait_ge(dn_dve, at2(DN_DVE, g, "R", d))
                        af(dn_buf(d, "D", 512), dn_buf(d, "D", 512), ACT.Exp).then_inc(*own(dn_act))
                    yield
                    for i in range(5):
                        for d in range(2):
                            act.wait_ge(dn_pe, at2(DN_PE, g, f"X{i}", d))
                            af(dn_buf(d, "X", 512), A[d], ACT.Copy).then_inc(*own(dn_act))
                    yield
                    for j in range(2):
                        if j:
                            yield
                        for d in range(2):
                            act.wait_ge(dn_pe, at2(DN_PE, g, f"V{j}", d))
                            c = j if d == 0 else 1 - j
                            rows = slice(64 * c, 64 * c + 64)
                            af(dn_buf(d, "vn", 256)[rows, :], B[d][rows, 0:256], ACT.Copy).then_inc(*own(dn_act))

            def hg(l):
                E1, L2 = PRB[:, 0:T], PRB[:, T:2 * T]
                act.wait_ge(hp_dve, at(HP_DVE, l, "lb1"))
                af(ST[:, 108:116], ST[:, 108:116], ACT.Exp).then_inc(*own(hp_act))
                act.wait_ge(hp_dve, at(HP_DVE, l, "lb2"))
                af(LBV[:, 4:8], LBV[:, 4:8], ACT.Ln).then_inc(*own(hp_act))
                act.wait_ge(*own.last)
                for i in range(4):
                    F = fm("hg", 2 + i)
                    act.wait_ge(hp_dve, at(HP_DVE, l, f"c{i}"))
                    if i:
                        act.wait_ge(hp_dve, at(HP_DVE, l, f"l{i - 1}"))
                    af(E1, F, ACT.Exp, scale=-1.0).then_inc(*own())
                    act.wait_ge(*own.last)
                    af(L2, E1, ACT.Ln, scale=LBV[:, i:i + 1], bias=one).then_inc(*own())
                    af(E1, E1, ACT.Ln, bias=one).then_inc(*own(hp_act))
                    act.wait_ge(hp_dve, at(HP_DVE, l, f"l{i}"))
                    af(F, F, ACT.Exp, scale=-1.0, bias=LBV[:, 4 + i:5 + i]).then_inc(*own(hp_act))
                for n in range(TT):
                    for d in range(2):
                        q = 2 * (TT * l + n) + d
                        act.wait_ge(hg_dve, at(HG_DVE, q, "D"))
                        he = Y[:, 6 * T:8 * T]
                        af(he, he, ACT.Abs).then_inc(*own())
                        act.wait_ge(*own.last)
                        af(he, he, ACT.Exp, scale=-1.0).then_inc(*own())
                        t = ORD[d][n]
                        if q:
                            act.wait_ge(hg_pe, at(HG_PE, q - 1, "C1"))
                        hbt = Y[:, (2 + 2 * d) * T:(4 + 2 * d) * T].rearrange("p (f n) -> p f n", f=2)[:, :, t * P:(t + 1) * P]
                        af(HQB.rearrange("p (f n) -> p f n", f=2), hbt, ACT.Exp).then_inc(*own())
                        ed = 63 if d == 0 else 0
                        bl = hbt.rearrange("p f (c j) -> p f c j", c=2)[:, :, :, ed]
                        af(HDE.rearrange("p (f c) -> p f c", f=2), bl, ACT.Exp).then_inc(*own())
                        af(HKE, HKE, ACT.Exp, scale=-1.0).then_inc(*own(hg_act))
                        yield
                        act.wait_ge(hg_pe, at(HG_PE, q, "T"))
                        af(HKT, bank(2, 0, 256), ACT.Copy).then_inc(*own(hg_act))
                        yield

            def attend(st):
                kind, l = st
                i0, todo = items[st]
                na = kind == "na"
                def exps(i):
                    h, t = todo[i]
                    g = i0 + i
                    a = 0 if t >= CT else LAT
                    s = ST[:, 8 * (g % 4):8 * (g % 4) + 8]
                    if i >= 2:
                        act.wait_ge(at_tr, g - 1)
                    if na:
                        act.wait_ge(at_max, part(st, i))
                        pr = NP_[g % 2]
                        b0 = 512 * (2 + 2 * (g % 2))
                        if a == 0:
                            af(pr[:, 0:LAT], pr[:, 0:LAT], ACT.Exp, bias=s[:, 0:1], accum_out=s[:, 2:3]).then_inc(*own())
                        af(pr[:, LAT:T], PS[:, b0 + LAT:b0 + T], ACT.Exp, bias=s[:, 0:1],
                           accum_out=s[:, 3:4]).then_inc(*own(at_exp))
                    else:
                        for j in range(2):
                            act.wait_ge(at_max, part(st, i, j))
                            b0 = 512 * (2 + 2 * j)
                            af(DPP[g % 2][:, j * T + a:(j + 1) * T], PS[:, b0 + a:b0 + T], ACT.Exp,
                               bias=s[:, j:j + 1], accum_out=s[:, 2 + j:3 + j]).then_inc(*own(at_exp))

                def evac(i):
                    g = i0 + i
                    a = 0 if todo[i][1] >= CT else LAT
                    act.wait_ge(at_tr, g + 1)
                    if i >= 2:
                        act.wait_ge(at_pv, g - 1)
                    af((NPT if na else DPT)[g % 2][:, a:T], PS[:, 6 * 512 + a:6 * 512 + T], ACT.Copy).then_inc(*own(at_pt))

                n = len(todo)
                for i in range(n + 2):
                    if i < n:
                        exps(i)
                    if 0 < i <= n:
                        evac(i - 1)
                    yield

            def df(st):
                act.wait_ge(dp_dve, at(DP_DVE, st[1], "d"))
                af(ST[:, 36:38], ST[:, 34:36], ACT.Exp).then_inc(*own(dp_act))
                yield from attend(st)

            def post(st):
                m, p0, t0 = posts[st]
                kind, l = st
                w = (TT - t0) * GW
                nt = TT - t0
                o = O[:, t0 * GW:TT * GW]
                if kind != "na":
                    if kind in ("dn", "hg"):
                        gate = tm(kind, 0 if kind == "dn" else 1)[:, t0 * GW:TT * GW]
                        af(gate, gate, ACT.Silu).then_inc(*own())
                    act.wait_ge(post_dve, 2 * m)
                    if kind == "dn":
                        act.wait_ge(dn_dve, at2(DN_DVE, TT * l + TT - 1, "O", 1))
                    elif kind == "hg":
                        act.wait_ge(hg_dve, at(HG_DVE, 2 * TT * (l + 1) - 1, "O"))
                        act.wait_ge(hg_pe, at(HG_PE, 2 * TT * (l + 1) - 1, "C1"))
                    else:
                        act.wait_ge(at_o, items[st][0] + len(items[st][1]))
                    sq = SCR[:, 1536:1536 + w]
                    af(sq, o, ACT.Square).then_inc(*own(post_act))
                    act.wait_ge(post_dve, 2 * m + 1)
                    rsqrt(ST[:, 40:40 + 4 * nt], ST[:, 40:40 + 4 * nt], 1.0 / HD, post_act)
                f = YT[kind]
                for i, t in enumerate(range(t0, TT, 2)):
                    act.wait_ge(post_pe, p0 + i + 1)
                    dst = Yv[:, f:f + 2, t * P:(t + 2) * P]
                    af(dst, bank(2 + i).rearrange("p (f n) -> p f n", f=2), ACT.Copy).then_inc(*own(y_done))

            act.wait_ge(loaded, 16 * N_LOADS)
            act.wait_ge(masks_ready, 1)
            af(SC[:, :], SC[:, :], ACT.Silu).then_inc(*own(silu_ready))
            for st in steps:
                kind = st[0]
                if kind == "unit":
                    gemm_unit(st[1])
                elif kind == "norm":
                    norm(norm_at.index(st), st[3], st[1])
                else:
                    act.wait_ge(y_done, before[st])
                    body = dn(st[1]) if kind == "dn" else hg(st[1]) if kind == "hg" else df(st) if kind == "df" else attend(st)
                    filled(plans[st], body, gemm_unit, 1)
                    post(st)

        @block.vector
        def _(dve):
            own = Turns(dve_chain)
            v = nc.vector
            tt, ts, stt, ttr = v.tensor_tensor, v.tensor_scalar, v.scalar_tensor_tensor, v.tensor_tensor_reduce

            def taps(dst, src, w, a, e, sem_=None):
                dve.wait_ge(*own.last)
                stt(dst[:, a + 1:e], src[:, a:e - 1], w(0), dst[:, a + 1:e], MUL, ADD).then_inc(*own())
                dve.wait_ge(*own.last)
                stt(dst[:, a:e - 1], src[:, a + 1:e], w(2), dst[:, a:e - 1], MUL, ADD).then_inc(*own(sem_))

            def gemm_unit(u, some=None):
                k, l = u["kind"], u["l"]
                if k == "ada":
                    dve.wait_ge(*weights(u))
                    dve.wait_ge(silu_ready, 1)
                    vecs = (0, 1) if (l < DEPTH - 1 or u["u"] < 8) else (1,)
                    for j in range(2):
                        m = 2 * u["u"] + j
                        for vec in vecs:
                            last = (j, vec) == (1, vecs[-1])
                            dve.wait_ge(*own.last) if own.last else None
                            ttr(out=JUNK[:, :], in0=slot(u)[:, j * DM:(j + 1) * DM], in1=SC[:, vec * DM:(vec + 1) * DM],
                                      scale=1.0, scalar=sm(l, W_BADA + m), op0=MUL, op1=ADD,
                                      accum_out=mod(l, vec, m)).then_inc(*own(ada_done if last else None))
                    return
                if k == "upg":
                    p = u["pair"]
                    dve.wait_ge(gemm_act, u["banks"][-1]["turn"])
                    for f in range(2):
                        for i, (a, e) in enumerate(u["segs"]):
                            last = f == 1 and i == len(u["segs"]) - 1
                            taps(FFC[p % 2][:, f * T:(f + 1) * T], FFG[p % 2][:, f * T:(f + 1) * T],
                                 lambda tap: sm(l, W_FFC + (2 * u["u"] + f) * 3 + tap), a, e, conv_done if last else None)
                for b in some or u["banks"]:
                    if b["who"] != "dve":
                        continue
                    dve.wait_ge(gemm_ready, b["n"] + 1)
                    f, (a, e) = b["what"]
                    ps = bank(b["n"] % 2)[:, 0:e - a]
                    if k == "upv":
                        p = u["pair"]
                        dve.wait_ge(silu_done, p + 1)
                        ft = 2 * u["u"] + f - PARTS[u["part"]][0]
                        tt(Z[:, ft * T + a:ft * T + e], ps, FFC[p % 2][:, f * T + a:f * T + e], MUL).then_inc(*own(gemm_dve))
                    else:
                        m = 2 * u["u"] + f if k == "out" else u["m"]
                        gate = mod(l, 0 if a == 0 else 1, (16 if k == "out" else 40) + m)
                        dve.wait_ge(*own.last)
                        stt(Xv[:, m, a:e], ps, gate, Xv[:, m, a:e], MUL, ADD).then_inc(*own(gemm_dve))

            def norm(ni, segs, l):
                for i, (a, e) in enumerate(segs):
                    g = AB[:, (2 * ni + i) * KT:(2 * ni + i + 1) * KT]
                    if l == DEPTH:
                        v.tensor_copy(g, FIN[:, :]).then_inc(*own())
                    else:
                        dve.wait_ge(*own.last)
                        stt(g, mod(l, 0 if a == 0 else 1, 8 if ni % 2 == 0 else 32, KT), 1.0,
                                  sm(l, W_N1 if ni % 2 == 0 else W_N2, KT), ADD, MUL).then_inc(*own())
                dve.wait_ge(*own.last)
                dve.wait_ge(rstd_ready, ni + 1)
                for k in range(KT):
                    for i, (a, e) in enumerate(segs):
                        g = AB[:, (2 * ni + i) * KT + k:(2 * ni + i) * KT + k + 1]
                        last = stt(Hv[:, k, a:e], Xv[:, k, a:e], g, RSTD[:, a:e], MUL, MUL)
                        last.then_inc(*own(scaled if i == len(segs) - 1 else None))

            def dn(l):
                for f in range(6):
                    dve.wait_ge(prep_act, at(PR_ACT, l, f"m{f}"))
                    dst = PRB[:, (f % 2) * T:(f % 2 + 1) * T]
                    w = lambda tap: sm(l, W_DNC + f * 3 + tap)
                    taps(dst, fm("dn", f), w, 0, CTX)
                    taps(dst, fm("dn", f), w, CTX, T, prep_dve)
                for f in range(4):
                    dve.wait_ge(prep_act, at(PR_ACT, l, f"r{f}"))
                    stt(fm("dn", f), fm("dn", f), HD ** -0.5 if f < 2 else 1.0, PRB[:, 2 * T:3 * T], MUL, MUL).then_inc(*own(prep_dve))
                raw = Y[:, BAO:BAO + 96].rearrange("p (t g h) -> p t g h", t=TT, g=4)
                as48 = lambda i: ba(i).rearrange("p (t d h) -> p t d h", t=TT, d=2)
                at8 = lambda i: ba(i).rearrange("p (t g) -> p t g", t=TT)
                raw8 = Y[:, BAO:BAO + 96].rearrange("p (t g) -> p t g", t=TT)
                ts(at8(NEGB), raw8[:, :, 0:8], -80.0, None, MAX).then_inc(*own())
                tt(at8(G), raw8[:, :, 8:16], sm(l, W_DTB, 8)[:, None, :].to_broadcast([P, TT, 8]), ADD).then_inc(*own())
                dve.wait_ge(*own.last)
                stt(ba(EG), ba(G), -1.0, ba(G), MUL, MAX).then_inc(*own(prep_dve))
                dve.wait_ge(prep_act, at(PR_ACT, l, "b1"))
                v.tensor_scalar_add(ba(BETA), ba(BETA), 1.0).then_inc(*own())
                stt(ba(G), ba(G), 0.0, ba(EDEC), MAX, ADD).then_inc(*own())
                dve.wait_ge(*own.last)
                v.reciprocal(ba(BETA), ba(BETA)).then_inc(*own())
                dve.wait_ge(*own.last)
                v.tensor_scalar_mul(ba(NBETA), ba(BETA), -1.0).then_inc(*own())
                stt(at8(LOGA), at8(G), -1.0, ba(TOT)[:, None, 0:8].to_broadcast([P, TT, 8]), MUL, MUL).then_inc(*own(prep_dve))
                dve.wait_ge(prep_act, at(PR_ACT, l, "b2"))
                tt(ba(EDEC), ba(TOT), ba(G), SUB).then_inc(*own(prep_dve))
                stt(ba(NEGB), ba(EG), -1.0, ba(BETA), MUL, MUL).then_inc(*own())
                v.memset(Y[:, YS + 3584:YS + 3840], 0.0).then_inc(*own(prep_dve))
                dve.wait_ge(prep_act, at(PR_ACT, l, "b3"))
                for n in range(TT):
                    g = TT * l + n
                    A, B, C = [bank(2), bank(5)], [bank(3), bank(6)], [bank(4), bank(7)]
                    tile = [ORD[d][n] for d in range(2)]

                    def col(i, d):
                        return ba(i)[:, tile[d] * 8 + d * 4:tile[d] * 8 + d * 4 + 4]

                    def over(i, d, rows=slice(0, P)):
                        c = col(i, d)[rows, :]
                        return c[:, :, None].to_broadcast([c.shape[0], NH, HD])

                    for d in range(2):
                        dve.wait_ge(dn_pe, at2(DN_PE, g, "tr", d))
                        kt, vt = h4(A[d][:, 0:256]), h4(A[d][:, 256:512])
                        tt(h4(dn_buf(d, "kdec", 256)), kt, over(EDEC, d), MUL).then_inc(*own())
                        tt(h4(dn_buf(d, "vb", 256)), vt, over(BETA, d), MUL).then_inc(*own())
                        tt(h4(dn_buf(d, "kb", 256)), kt, over(NBETA, d), MUL).then_inc(*own(dn_dve))
                    for d in range(2):
                        dve.wait_ge(dn_pe, at2(DN_PE, g, "R", d))
                        for h in range(NH):
                            hs = slice(h * P, (h + 1) * P)
                            last = stt(dn_buf(d, "D", 512)[:, hs], C[d][:, hs], col(G, d)[:, h:h + 1],
                                       cc(C_NEG + d * P, P), SUB, MIN)
                            last.then_inc(*own(dn_dve if h == NH - 1 else None))
                    yield
                    for d in range(2):
                        dve.wait_ge(dn_pe, at2(DN_PE, g, "kk", d))
                        dve.wait_ge(dn_act, at2(DN_ACT, g, "exp", d))
                        tt(dn_buf(d, "NT", 512), A[d], dn_buf(d, "D", 512), MUL).then_inc(*own(dn_dve))
                    for d in range(2):
                        dve.wait_ge(dn_pe, at2(DN_PE, g, "kq", d))
                        tt(dn_buf(d, "at", 512), B[d], dn_buf(d, "D", 512), MUL).then_inc(*own(dn_dve))

                    def grow(dst, lv, d, src, transposed, sem_=None):
                        m = mask(d if transposed else 1 - d, lv)
                        v.copy_predicated(h4(dn_buf(d, dst, 512)), four(m), h4(src)).then_inc(*own(sem_))

                    for d in range(2):
                        dve.wait_ge(dn_pe, at2(DN_PE, g, "N", d))
                        dve.wait_ge(dn_dve, at2(DN_DVE, g, "NT", d))
                        grow("Tm", 1, d, C[d], False)
                        grow("TTm", 1, d, dn_buf(d, "NT", 512), True, dn_dve)
                    yield
                    for i in range(5):
                        for d in range(2):
                            dve.wait_ge(dn_pe, at2(DN_PE, g, f"Y{i}", d))
                            dve.wait_ge(dn_dve, at2(DN_DVE, g, "M" if i == 0 else f"L{i - 1}", d))
                            if i < 4:
                                grow("Tm", i + 2, d, C[d], False)
                            grow("TTm", i + 2, d, B[d], True, dn_dve)
                    yield
                    for j in range(2):
                        if j:
                            yield
                        for d in range(2):
                            c = j if d == 0 else 1 - j
                            rows = slice(64 * c, 64 * c + 64)
                            rhs = dn_buf(d, "rhs", 256)[rows, :]
                            dve.wait_ge(dn_pe, at2(DN_PE, g, f"K{j}", d))
                            tt(h4(rhs), h4(A[d][rows, 0:256]), over(NEGB, d, rows), MUL).then_inc(*own())
                            dve.wait_ge(*own.last)
                            tt(rhs, rhs, dn_buf(d, "vb", 256)[rows, :], ADD).then_inc(*own(dn_dve))
                        for d in range(2):
                            c = j if d == 0 else 1 - j
                            dve.wait_ge(dn_pe, at2(DN_PE, g, f"O{j}", d))
                            for hp in range(2):
                                S = DNS[d][:, hp * HD:(hp + 1) * HD]
                                o = ((tile[d] * 2 + d) * 2 + hp) * 2 + c
                                last = stt(S, S, ba(EGL)[:, o:o + 1], B[d][:, 256 + hp * HD:256 + (hp + 1) * HD], MUL, ADD)
                                last.then_inc(*own(dn_dve if hp else None))
                    for d in range(2):
                        t = dn_buf(d, "t", 256)
                        o = O[:, tile[d] * GW:(tile[d] + 1) * GW]
                        first = ORD[1 - d].index(tile[d]) > n
                        tt(h4(t), h4(A[d][:, 256:512]), over(EG, d), MUL).then_inc(*own())
                        dve.wait_ge(*own.last)
                        if first:
                            tt(o, t, C[d][:, 0:256], ADD).then_inc(*own(dn_dve))
                        else:
                            tt(t, t, C[d][:, 0:256], ADD).then_inc(*own())
                            dve.wait_ge(*own.last)
                            tt(o, t, o, ADD).then_inc(*own(dn_dve))

            def hg(l):
                E1, L2, LF = PRB[:, 0:T], PRB[:, T:2 * T], PRB[:, 2 * T:3 * T]
                raw = [sm(i, W_LB, 8)[:, 4 * i:4 * i + 4] for i in range(DEPTH)]
                e = ST[:, 108:116]
                tt(ST[:, 104:108], raw[0], raw[1], MAX).then_inc(*own())
                dve.wait_ge(*own.last)
                for i in range(DEPTH):
                    tt(e[:, 4 * i:4 * i + 4], raw[i], ST[:, 104:108], SUB).then_inc(*own(hp_dve if i else None))
                dve.wait_ge(hp_act, at(HP_ACT, l, "lb1"))
                tt(ST[:, 104:108], e[:, 0:4], e[:, 4:8], ADD).then_inc(*own())
                dve.wait_ge(*own.last)
                v.reciprocal(ST[:, 104:108], ST[:, 104:108]).then_inc(*own())
                dve.wait_ge(*own.last)
                for i in range(DEPTH):
                    tt(e[:, 4 * i:4 * i + 4], e[:, 4 * i:4 * i + 4], ST[:, 104:108], MUL).then_inc(*own())
                dve.wait_ge(*own.last)
                if l == 0:
                    tt(LBV[:, 0:4], e[:, 0:4], e[:, 0:4], SUB).then_inc(*own())
                else:
                    tt(LBV[:, 0:4], e[:, 0:4], e[:, 4:8], ADD).then_inc(*own())
                    dve.wait_ge(*own.last)
                    tt(LBV[:, 0:4], LBV[:, 0:4], e[:, 0:4], SUB).then_inc(*own())
                dve.wait_ge(*own.last)
                ts(LBV[:, 4:8], LBV[:, 0:4], -1.0, 1.0, MUL, ADD).then_inc(*own())
                dve.wait_ge(*own.last)
                ts(LBV[:, 4:8], LBV[:, 4:8], 1e-18, None, MAX).then_inc(*own(hp_dve))
                for i in range(4):
                    F = fm("hg", 2 + i)
                    d, f = i // 2, i % 2
                    ts(F, F, -40.0, None, MAX).then_inc(*own(hp_dve))
                    dve.wait_ge(hp_act, at(HP_ACT, l, f"e{i}"))
                    tt(LF, L2, E1, SUB).then_inc(*own())
                    tt(F, F, E1, ADD).then_inc(*own(hp_dve))
                    hb, lf = HB(d, f), LF
                    if d == 1:
                        hb, lf = hb[:, ::-1], LF[:, ::-1]
                    dve.wait_ge(*own.last)
                    v.tensor_tensor_scan(hb, cc(C_SCAN, T), lf, 0.0, MUL, ADD).then_inc(*own(hp_dve))
                v.memset(SCR[:, 4352:4608], 0.0).then_inc(*own())
                dve.wait_ge(*own.last)
                dve.wait_ge(hp_act, at(HP_ACT, l, "k3"))
                for n in range(TT):
                    for d in range(2):
                        q = 2 * (TT * l + n) + d
                        t = ORD[d][n]
                        cs = slice(t * P, (t + 1) * P)
                        hb2 = Y[:, (2 + 2 * d) * T:(4 + 2 * d) * T].rearrange("p (f n) -> p f n", f=2)[:, :, cs]
                        two = lambda ap: ap.rearrange("p (f n) -> p f n", f=2)
                        if q:
                            dve.wait_ge(hg_pe, at(HG_PE, q - 1, "T"))
                        for lv in range(1, LEVELS + 1):
                            s = 1 << (lv - 1)
                            w = hb2.rearrange("p f (b j) -> p f b j", j=2 * s)
                            m = w[:, :, :, s - 1:s] if d == 0 else w[:, :, :, s:s + 1]
                            tt(two(HE[:, lv - 1, :]).rearrange("p f (b j) -> p f b j", j=2 * s), w,
                                     m.to_broadcast([P, 2, P // (2 * s), 2 * s]), SUB).then_inc(*own())
                        w = hb2.rearrange("p f (c j) -> p f c j", c=2)
                        m = w[:, :, :, 63:64] if d == 0 else w[:, :, :, 0:1]
                        tt(two(HKE).rearrange("p f (c j) -> p f c j", c=2), w, m.to_broadcast([P, 2, 2, 64]), SUB).then_inc(*own(hg_dve))
                        qk = Z[:, ZG:ZG + 6 * T].rearrange("p (x f n) -> p x f n", x=3, f=2)
                        qs, ks = qk[:, 0, :, cs], qk[:, 1 + d, :, cs]
                        dve.wait_ge(hg_act, at(HG_ACT, q, "E"))
                        tt(two(HQB), two(HQB), qs, MUL).then_inc(*own())
                        tt(two(HKE), two(HKE), ks, MUL).then_inc(*own(hg_dve))
                        if q:
                            dve.wait_ge(hg_pe, at(HG_PE, q - 1, "C1"))
                        v.memset(ATT, 0.0).then_inc(*own())

                        def weigh(lv):
                            if lv >= 4:
                                dve.wait_ge(hg_pe, at(HG_PE, q, f"L{lv - 3}"))
                            dst = QKT[lv % 3].rearrange("p (x f n) -> p x f n", x=2, f=2)
                            E = two(HE[:, lv - 1, :])
                            tt(dst[:, 0], qs, E, MUL).then_inc(*own())
                            tt(dst[:, 1], ks, E, MUL).then_inc(*own(hg_dve))

                        def take(lv):
                            dve.wait_ge(hg_pe, at(HG_PE, q, f"L{lv}"))
                            dve.wait_ge(*own.last)
                            v.copy_predicated(h4(ATT), four(mask(d, lv)), h4(bank(3 + lv % 3))).then_inc(*own(hg_dve))

                        yield
                        for name in HG_DVE[2:15]:
                            (weigh if name[0] == "M" else take)(int(name[1]))
                        yield
                        for j in range(2):
                            c = j if d == 0 else 1 - j
                            dve.wait_ge(hg_pe, at(HG_PE, q, f"C{j}"))
                            for f in range(2):
                                S = HGS[d][:, f * HD:(f + 1) * HD]
                                stt(S, S, HDE[:, 2 * f + c:2 * f + c + 1], bank(7, f * HD, (f + 1) * HD), MUL, ADD).then_inc(*own(hg_dve if f else None))
                        o = O[:, t * GW:(t + 1) * GW]
                        if ORD[1 - d].index(t) > n or (ORD[1 - d].index(t) == n and d == 0):
                            v.tensor_copy(o, bank(6, 0, 256)).then_inc(*own(hg_dve))
                        else:
                            tt(o, o, bank(6, 0, 256), ADD).then_inc(*own(hg_dve))

            def attend(st):
                kind, l = st
                i0, todo = items[st]
                na = kind == "na"
                stat = lambda g: ST[:, 8 * (g % 4):8 * (g % 4) + 8]

                def bias(hp):
                    for rnd in range(4):
                        gi = 4 * (2 * l + hp) + rnd
                        dve.wait_ge(bias_pe, gi + 1)
                        if rnd == 0:
                            dve.wait_ge(*own.last)
                        src = bank(2 + 2 * (rnd % 2), 0, 448).rearrange("p (k x) -> p k x", k=16)
                        dst = NAB.rearrange("p (x k) -> p k x", k=GRID)[:, rnd * 16:(rnd + 1) * 16, :]
                        m = cc(C_NAM + rnd * 16, 16)[:, :, None].to_broadcast([P, 16, 28])
                        tt(dst, src, m, ADD).then_inc(*own(bias_dve))
                    dve.wait_ge(*own.last)

                def maxes(i):
                    h, t = todo[i]
                    g = i0 + i
                    s = stat(g)
                    if i >= 2:
                        dve.wait_ge(at_tr, g - 1)
                    if na:
                        dve.wait_ge(at_s, part(st, i))
                        b0 = 512 * (2 + 2 * (g % 2))
                        if t < CT:
                            v.tensor_reduce(s[:, 0:1], PS[:, b0 + LAT:b0 + T], AX.X, MAX, negate=True).then_inc(*own(at_max))
                            return
                        qa = t - CT
                        o = ((h % 2) * 14 + 6 - 2 * qa) * GRID
                        ttr(out=NP_[g % 2][:, 0:LAT], in0=PS[:, b0:b0 + LAT], in1=NAB[:, o:o + LAT], scale=1.0,
                                  scalar=-3e38, op0=ADD, op1=MAX, accum_out=s[:, 4:5]).then_inc(*own())
                        v.tensor_reduce(s[:, 5:6], PS[:, b0 + LAT:b0 + T], AX.X, MAX).then_inc(*own())
                        dve.wait_ge(*own.last)
                        ts(s[:, 0:1], s[:, 4:5], s[:, 5:6], -1.0, MAX, MUL).then_inc(*own(at_max))
                    else:
                        a = 0 if t >= CT else LAT
                        for j in range(2):
                            b0 = 512 * (2 + 2 * j)
                            dve.wait_ge(at_s, part(st, i, j))
                            v.tensor_reduce(s[:, j:j + 1], PS[:, b0 + a:b0 + T], AX.X, MAX, negate=True).then_inc(*own(at_max))

                def probs(i):
                    h, t = todo[i]
                    g = i0 + i
                    s = stat(g)
                    dve.wait_ge(at_exp, part(st, i, 0 if na else 1))
                    if na:
                        if t >= CT:
                            tt(s[:, 6:7], s[:, 2:3], s[:, 3:4], ADD).then_inc(*own())
                            dve.wait_ge(*own.last)
                            v.reciprocal(s[:, 6:7], s[:, 6:7]).then_inc(*own(at_p))
                        else:
                            v.reciprocal(s[:, 6:7], s[:, 3:4]).then_inc(*own(at_p))
                    else:
                        a = 0 if t >= CT else LAT
                        v.reciprocal(s[:, 4:6], s[:, 2:4]).then_inc(*own())
                        dve.wait_ge(*own.last)
                        stt(s[:, 7:8], s[:, 2:3], s[:, 5:6], ST[:, 38:39], MUL, MUL).then_inc(*own())
                        dve.wait_ge(*own.last)
                        p0, p1 = DPP[g % 2][:, a:T], DPP[g % 2][:, T + a:2 * T]
                        stt(p0, p1, s[:, 7:8], p0, MUL, ADD).then_inc(*own(at_p))

                def outs(i):
                    h, t = todo[i]
                    g = i0 + i
                    s = stat(g)
                    dve.wait_ge(at_pv, g + 1)
                    dve.wait_ge(*own.last)
                    v.tensor_scalar_mul(O[:, t * GW + h * HD:t * GW + (h + 1) * HD], bank(7, 256, 256 + HD),
                                              s[:, 6:7] if na else s[:, 4:5]).then_inc(*own(at_o))

                n = len(todo)
                for i in range(n + 2):
                    if new_pair(st, i):
                        bias(todo[i][0] // 2)
                    if i < n:
                        maxes(i)
                    if i >= 2:
                        outs(i - 2)
                    if 0 < i <= n:
                        probs(i - 1)
                    yield

            def df(st):
                l = st[1]
                li = 0.8 - 0.6 * math.exp(-0.3 * l)
                lp = sm(l, W_LAM, 128)
                for k in range(2):
                    ttr(out=SCR[:, 1536:1568], in0=lp[:, 64 * k:64 * k + 32], in1=lp[:, 64 * k + 32:64 * k + 64], scale=1.0,
                              scalar=0.0, op0=MUL, op1=ADD, accum_out=ST[:, 34 + k:35 + k]).then_inc(*own(dp_dve if k else None))
                    dve.wait_ge(*own.last)
                for i in range(4):
                    dve.wait_ge(dp_pe, 4 * l + i + 1)
                    x = fm("df", i)[:, CTX:T]
                    tmp = SCR[:, 1536:2048]
                    dve.wait_ge(*own.last)
                    tt(tmp, bank(2 + i), cc(C_SIN, LAT), MUL).then_inc(*own())
                    tt(x, x, cc(C_COS, LAT), MUL).then_inc(*own())
                    dve.wait_ge(*own.last)
                    tt(x, x, tmp, ADD).then_inc(*own(dp_dve))
                dve.wait_ge(dp_act, at(["e"], l, "e"))
                ts(sm(l, W_DFN, HD), sm(l, W_DFN, HD), 1.0 - li, None, MUL).then_inc(*own())
                tt(ST[:, 38:39], ST[:, 37:38], ST[:, 36:37], SUB).then_inc(*own())
                dve.wait_ge(*own.last)
                v.tensor_scalar_add(ST[:, 38:39], ST[:, 38:39], -li).then_inc(*own(dp_dve))
                dve.wait_ge(*own.last)
                yield from attend(st)

            def post(st):
                m, p0, t0 = posts[st]
                kind, l = st
                if kind == "na":
                    return
                n = (TT - t0) * NH
                w = (TT - t0) * GW
                o = O[:, t0 * GW:TT * GW]
                o3 = o.rearrange("p (n e) -> p n e", e=HD)
                ss = ST[:, 40:40 + n]
                dve.wait_ge(post_act, 2 * m + 1)
                v.tensor_reduce(ss, SCR[:, 1536:1536 + w].rearrange("p (n e) -> p n e", e=HD), AX.X, ADD).then_inc(*own(post_dve))
                dve.wait_ge(post_act, 2 * m + 2)
                tt(o3, o3, ss[:, :, None].to_broadcast([P, n, HD]), MUL).then_inc(*own())
                dve.wait_ge(*own.last)
                nw = sm(l, {"dn": W_DNN, "df": W_DFN, "hg": W_HGN}[kind], HD)[:, None, :].to_broadcast([P, n, HD])
                if kind == "df":
                    tt(o3, o3, nw, MUL).then_inc(*own(post_dve))
                    return
                tt(o3, o3, nw, MUL).then_inc(*own())
                dve.wait_ge(*own.last)
                gate = tm(kind, 0 if kind == "dn" else 1)[:, t0 * GW:TT * GW]
                tt(o, o, gate, MUL).then_inc(*own(post_dve))

            dve.wait_ge(loaded, 16 * N_LOADS)
            v.tensor_copy(MSK[:, :], Z[:, 0:2 * (LEVELS + 1) * P]).then_inc(*own(masks_ready))
            for st in steps:
                kind = st[0]
                if kind == "unit":
                    gemm_unit(st[1])
                elif kind == "norm":
                    norm(norm_at.index(st), st[3], st[1])
                else:
                    dve.wait_ge(gemm_act, acts_before[st])
                    dve.wait_ge(y_done, before[st])
                    body = dn(st[1]) if kind == "dn" else hg(st[1]) if kind == "hg" else df(st) if kind == "df" else attend(st)
                    filled(plans[st], body, gemm_unit, 1)
                    post(st)


_OUT = (P, KT, LAT)


def kernel(**inputs):
    import concourse.bacc as _bacc
    from concourse import mybir as _mybir
    from concourse.bass_utils import run_bass_kernel_spmd as _run

    nc = _bacc.Bacc("TRN2", target_bir_lowering=False, num_devices=1)
    arrays = lay_out(inputs)
    aps = {}
    for name in INPUTS:
        a = arrays[name]
        aps[name] = nc.dram_tensor(f"in_{name}", a.shape, _mybir.dt.from_np(a.dtype), kind="ExternalInput").ap()
    out = nc.dram_tensor("out_0", _OUT, _mybir.dt.float32, kind="ExternalOutput").ap()
    hybrid_backbone(nc, aps, out)
    r = _run(nc, [{f"in_{k}": arrays[k] for k in INPUTS}], core_ids=[0])
    y = np.asarray(r.results[0]["out_0"])
    return np.ascontiguousarray(y.transpose(2, 1, 0).reshape(1, LAT, DM))
```

```python
import math
from contextlib import ExitStack
from itertools import chain

import numpy as np

import concourse.bass as bass
from concourse import mybir

P = 128
DM = 1024
KT = DM // P
LAT, CTX = 512, 256
T = LAT + CTX
TT = T // P
CT = CTX // P
SEG = ((0, CTX), (CTX, T))
DEPTH = 2
GW = 256
HD = 64
NH = 4
CH = 64
DFF = 2816
FT = DFF // P
EPS = 1e-6
LEVELS = 6
NEG = -1e30
GRID = 64

C_ID, C_MEAN, C_BLK, C_ROT = 0, 128, 256, 384
C_NEG = 512
C_INC = 768
C_AJ = 1024
C_NAM = 1278
C_CHK = 1342
C_EPS, C_ONE = 1344, 1345
C_COS, C_SIN, C_SCAN = 1346, 1858, 2370
NC_ = C_SCAN + T

W_N1, W_N2, W_BADA, W_DNC, W_FFC = 0, 8, 16, 64, 82
W_ALOG, W_DTB, W_DNN, W_DFN, W_HGN = 148, 156, 164, 228, 292
W_LAM, W_LB, W_RPB, W_BA = 356, 484, 492, 548
NW = W_BA + KT * 16
COL = dict(dnq=0, dnk=256, dnv=512, dng=768, naq=1040, nak=1296, nav=1552, dfq=1808, dfk=2064,
           dfv=2320, hgq=2576, hgv=2832, hgf=3088, hgb=3344, hgg=3600)
COL_BA = 1024


def shape_constants():
    c = np.zeros((P, NC_), np.float32)
    i = np.arange(P)
    c[:, C_ID:C_ID + P] = np.eye(P)
    c[:, C_MEAN:C_MEAN + P] = 1.0 / DM
    blk = (i[:, None] // CH) == (i[None, :] // CH)
    c[:, C_BLK:C_BLK + P] = blk
    for m in range(P):
        first = m % 16 < 8
        c[m + 8 if first else m - 8, C_ROT + m] = -1.0 if first else 1.0
    for d in range(2):
        inc = blk & ((i[:, None] <= i[None, :]) if d == 0 else (i[:, None] >= i[None, :]))
        c[:, C_NEG + d * P:C_NEG + (d + 1) * P] = np.where(inc, 0.0, NEG)
        c[:, C_INC + d * P:C_INC + (d + 1) * P] = inc
    for b in range(2):
        for dl in range(31):
            c[32 * b + dl, C_AJ + 64 * b + 78 - dl] = 1.0
    q = i % GRID
    start = np.clip(q - 8, 0, GRID - 16)
    k = np.arange(GRID)
    c[:, C_NAM:C_NAM + GRID] = np.where((k >= start[:, None]) & (k < start[:, None] + 16), 0.0, NEG)
    c[:, C_CHK] = i < CH
    c[:, C_CHK + 1] = i >= CH
    c[:, C_EPS] = EPS
    c[:, C_ONE] = 1.0
    t = np.arange(LAT)
    inv = (1.0 / (np.float32(10000.0) ** (np.arange(0, 16, 2, dtype=np.float32) / np.float32(16)))).astype(np.float32)
    for p in range(P):
        pos = (t // GRID if p % 32 < 16 else t % GRID).astype(np.float32)
        ang = pos * inv[p % 8]
        c[p, C_COS:C_COS + LAT] = np.cos(ang)
        c[p, C_SIN:C_SIN + LAT] = np.sin(ang)
    c[:, C_SCAN:C_SCAN + T] = (np.arange(T) % CH != 0)
    m = np.zeros((2, LEVELS + 1, P, P), np.float32)
    for d in range(2):
        m[d, 0] = np.eye(P)
        for lv in range(1, LEVELS + 1):
            s = 1 << (lv - 1)
            same = (i[:, None] // (2 * s)) == (i[None, :] // (2 * s))
            right = (i // s) % 2 == 1
            row, col = (~right, right) if d == 0 else (right, ~right)
            m[d, lv] = same & row[:, None] & col[None, :]
    return c, np.ascontiguousarray(m.transpose(2, 0, 1, 3).reshape(P, -1))


def lay_out(a):
    f = np.float32
    out = {}
    x = np.concatenate([np.asarray(a["ctx"])[0], np.asarray(a["x"])[0]], 0)
    out["x"] = x.T.reshape(KT, P, T).transpose(1, 0, 2).reshape(P, -1)
    both = np.stack([np.asarray(a["c_ctx"]), np.asarray(a["c"])[0]]).reshape(1, -1)
    out["c"] = np.repeat(both, P, 0)
    w = np.asarray(a["w_ada"]).reshape(DEPTH, DM, 24, 2, P)
    out["ada"] = w.transpose(0, 2, 4, 3, 1).reshape(DEPTH, 24, P, 2 * DM)
    w_in = np.asarray(a["w_in"])
    cut = [w_in[:, :, o:o + GW] for o in COL.values()]
    out["win"] = np.stack(cut, 1).reshape(DEPTH, 15, KT, P, GW).transpose(0, 1, 3, 2, 4).reshape(DEPTH, 15, P, -1)
    out["wout"] = np.asarray(a["w_out"]).reshape(DEPTH, KT, P, 4, GW).transpose(0, 3, 2, 1, 4).reshape(DEPTH, 4, P, -1)
    out["wup"] = np.asarray(a["w_up"]).reshape(DEPTH, KT, P, 22, GW).transpose(0, 3, 2, 1, 4).reshape(DEPTH, 22, P, -1)
    out["wdn"] = np.asarray(a["w_down"]).reshape(DEPTH, FT, P, KT, P).transpose(0, 3, 2, 1, 4).reshape(DEPTH, KT, P, -1)
    s = np.zeros((DEPTH, P, NW), f)
    vec = lambda v, n: np.asarray(v).reshape(DEPTH, n, P).transpose(0, 2, 1)
    s[:, :, W_N1:W_N1 + 8] = vec(a["norm1_w"], 8)
    s[:, :, W_N2:W_N2 + 8] = vec(a["norm2_w"], 8)
    s[:, :, W_BADA:W_BADA + 48] = vec(a["b_ada"], 48)
    s[:, :, W_DNC:W_DNC + 18] = np.asarray(a["dn_conv_w"]).reshape(DEPTH, 3, 6, P).transpose(0, 3, 2, 1).reshape(DEPTH, P, 18)
    s[:, :, W_FFC:W_FFC + 66] = np.asarray(a["ffn_conv_w"]).reshape(DEPTH, 3, FT, P).transpose(0, 3, 2, 1).reshape(DEPTH, P, 66)
    s[:, :, W_ALOG:W_ALOG + 8] = np.asarray(a["dn_a_log"]).reshape(DEPTH, 1, 8)
    s[:, :, W_DTB:W_DTB + 8] = np.asarray(a["dn_dt_bias"]).reshape(DEPTH, 1, 8)
    s[:, :, W_DNN:W_DNN + 64] = np.asarray(a["dn_norm_w"])[:, None, :]
    s[:, :, W_DFN:W_DFN + 64] = np.asarray(a["df_norm_w"])[:, None, :]
    s[:, :, W_HGN:W_HGN + 64] = np.asarray(a["hg_norm_w"])[:, None, :]
    s[:, :, W_LAM:W_LAM + 128] = np.asarray(a["df_lambda"]).reshape(DEPTH, 1, 128)
    lb = np.asarray(a["hg_lb_raw"]).reshape(DEPTH, 2, 2, P).transpose(3, 0, 1, 2).reshape(P, 8)
    s[:, :, W_LB:W_LB + 8] = lb
    rpb = np.asarray(a["na_rpb"])
    for b in range(2):
        r = rpb[:, :, 1 - b:15 - b, :].transpose(0, 3, 1, 2).reshape(DEPTH, 31, 56)
        s[:, 32 * b:32 * b + 31, W_RPB:W_RPB + 56] = r
    s[:, :, W_BA:] = w_in[:, :, COL_BA:COL_BA + 16].reshape(DEPTH, KT, P, 16).transpose(0, 2, 1, 3).reshape(DEPTH, P, -1)
    out["small"] = s
    out["fin"] = np.asarray(a["final_norm_w"]).reshape(KT, P).T
    out["const"], out["masks"] = shape_constants()
    return {k: np.ascontiguousarray(v) for k, v in out.items()}


INPUTS = ["x", "c", "ada", "win", "wout", "wup", "wdn", "small", "fin", "const", "masks"]


def schedule():
    steps, units = [], []

    fills = {}

    def unit(into=None, **u):
        units.append(u)
        if into is None:
            steps.append(("unit", u))
        else:
            fills[into].append(u)

    def emit_group(l, g, into=None):
        names = [["dnq", "dnk", "dnv", "dng"], ["hgf", "hgb", "hgq", "hgv", "hgg"],
                 ["naq", "nak", "nav"], ["dfq", "dfk", "dfv"]][g]
        base = (g % 2) * ZG
        fm, tm = 0, 0
        for name in names:
            last = l == DEPTH - 1
            if name in ("dng", "hgg", "nav", "dfv", "hgv"):
                t0 = CT if last and name in ("dng", "hgg") else 0
                unit(into, kind="tm", l=l, col=list(COL).index(name), z=base + 6 * T + tm * TT * GW, t0=t0)
                tm += 1
            else:
                segs = SEG[1:] if last and name in ("naq", "dfq") else SEG
                scale = {"naq": HD ** -0.5, "dfq": 32 ** -0.5, "hgq": HD ** -0.5}.get(name, 1.0)
                unit(into, kind="fm", l=l, col=list(COL).index(name), z=base + FMPOS[name] * T, segs=segs, scale=scale)
                fm += 1

    for l in range(DEPTH):
        last = l == DEPTH - 1
        segs = SEG[1:] if last else SEG
        if l == 0:
            for u in range(8):
                unit(kind="ada", l=0, u=u)
        steps.append(("norm", l, 0, SEG))
        rest = [(0, u) for u in range(8, 24)] + [(1, u) for u in range(EARLY)] if l == 0 else []
        emit_group(l, 0)
        for g, mixer in enumerate(MIXERS):
            st = (mixer, l)
            steps.append(st)
            fills[st] = []
            if g == 0:
                unit(st, kind="ba", l=l)
            if g < 3:
                emit_group(l, g + 1, st)
            else:
                for u in range(4):
                    unit(st, kind="out", l=l, u=u, segs=segs, rows=OTHERS)
            gemms, fills[st][:] = list(fills[st]), []
            for u in gemms:
                units.remove(u)
            for u in gemms:
                units.append(u)
                fills[st].append(u)
                for _ in range(2):
                    if rest:
                        la, ua = rest.pop(0)
                        unit(st, kind="ada", l=la, u=ua)
        for u in range(4):
            unit(kind="out", l=l, u=u, segs=segs, rows=LASTS)
        steps.append(("norm", l, 1, segs))
        assert not rest
        rest = [(1, u) for u in range(EARLY, 24)] if l == 0 else []
        pair = 0
        for part, (a, b) in enumerate(PARTS):
            for u in range(a // 2, b // 2):
                for kind in ("upg", "upv"):
                    unit(kind=kind, l=l, u=u, part=part, segs=segs)
                    if rest:
                        la, ua = rest.pop(0)
                        unit(kind="ada", l=la, u=ua)
            for m in range(KT):
                unit(kind="down", l=l, m=m, part=part, segs=segs)
    steps.append(("norm", DEPTH, 0, SEG[1:]))
    return steps, units, fills


EARLY = 6
MIXERS = ("dn", "hg", "na", "df")
OTHERS, LASTS = (0, 1, 2, 3, 6, 7), (4, 5)
FMPOS = dict(dnq=0, dnk=1 * 2, dnv=2 * 2, hgq=0, hgf=2, hgb=4, naq=0, nak=2, dfq=0, dfk=2)
ZG = 6 * T + 2 * TT * GW
PARTS = ((0, 12), (12, 22))
SLOT = KT * GW
SLOTS = 3


def bank_table(units):
    banks, turns = [], {"act": 0, "dve": 0}
    for u in units:
        u["banks"] = []
        k = u["kind"]
        if k == "ada":
            continue
        if k == "tm":
            outs = [("act", (t, t + 1)) for t in range(u["t0"], TT, 2)]
        elif k == "ba":
            outs = [("act", None)]
        elif k == "fm":
            outs = [("act", (f, s)) for f in range(2) for s in u["segs"]]
        elif k in ("out", "upv"):
            outs = [("dve", (f, s)) for f in range(2) for s in u["segs"]]
        elif k == "upg":
            outs = [("act", (f, s)) for f in range(2) for s in u["segs"]]
        else:
            outs = [("dve", (0, s)) for s in u["segs"]]
        for who, what in outs:
            turns[who] += 1
            b = dict(n=len(banks), who=who, turn=turns[who], what=what)
            u["banks"].append(b)
            banks.append(b)
    return banks


DN_PE = ["tr", "R", "kb", "kk", "kq", "N"] + [f"{x}{i}" for i in range(5) for x in "XY"] + \
        [f"{x}{j}" for j in range(2) for x in "KVO"]
DN_ACT = ["init", "kbT", "exp"] + [f"X{i}" for i in range(5)] + ["V0", "V1"]
DN_DVE = ["kb", "R", "NT", "at", "M"] + [f"L{i}" for i in range(5)] + ["R0", "S0", "R1", "S1", "O"]
HG_M = [f"M{i}" for i in range(1, LEVELS + 1)]
HG_LV = [f"L{i}" for i in range(LEVELS + 1)]
HG_P = [f"P{i}" for i in range(LEVELS + 1)]
HG_C = ["C0", "C1"]
HG_U = ["U0", "U1"]


def wanted(q):
    return q < 2 * TT * (DEPTH - 1) or q % (2 * TT) >= 2 * CT


def wanted_before(q):
    return sum(wanted(i) for i in range(q))


def filled(plan, points, piece, lag):
    n = 0
    for n, _ in enumerate(points):
        for u, some in plan[n]:
            if some == [None]:
                piece(u, some)
        for u, some in plan[n - lag] if n >= lag else ():
            if some != [None]:
                piece(u, some)
    assert n + 1 == len(plan), (n + 1, len(plan))
    for k in range(n + 1 - lag, n + 1):
        for u, some in plan[k]:
            if some != [None]:
                piece(u, some)


def planned(units, points):
    plan = [[] for _ in range(points)]
    n = sum(len(u["banks"]) for u in units)
    assert n <= points, (n, points)
    at = 0
    for u in units:
        if u["kind"] == "ada":
            plan[min(at * points // n, points - 1)].append((u, [None]))
        for b in u["banks"]:
            plan[at * points // n].append((u, [b]))
            at += 1
    return plan


class Turns:

    def __init__(self, chain):
        self.chain, self.counts, self.last = chain, {}, None

    def __call__(self, sem=None):
        sem = self.chain if sem is None else sem
        self.counts[sem.name] = self.counts.get(sem.name, 0) + 1
        self.last = (sem, self.counts[sem.name])
        return sem, 1


PR_PE = [f"n{i}" for i in range(4)] + ["cum"]
PR_ACT = [f"{x}{i}" for i in range(6) for x in "ms"] + [f"{x}{i}" for x in "qr" for i in range(4)] + ["b1", "b2", "b3"]
PR_DVE = [f"c{i}" for i in range(6)] + [f"l{i}" for i in range(4)] + ["b1", "b2", "b3", "b4"]
HP_ACT = ["lb1", "lb2"] + [f"{x}{i}" for x in "ek" for i in range(4)]
HP_DVE = ["lb1", "lb2"] + [f"c{i}" for i in range(4)] + [f"{x}{i}" for i in range(4) for x in "lb"]
DP_DVE = ["d"] + [f"r{i}" for i in range(4)] + ["lam"]


def at(order, n, name):
    return n * len(order) + order.index(name) + 1


def at2(order, n, name, d):
    return 2 * (n * len(order) + order.index(name)) + d + 1


def hybrid_backbone(nc, A, out):
    fp32, bf16, u8 = mybir.dt.float32, mybir.dt.bfloat16, mybir.dt.uint8
    ALU = mybir.AluOpType
    ACT = mybir.ActivationFunctionType
    AX = mybir.AxisListType
    MUL, ADD, SUB, MAX, MIN = ALU.mult, ALU.add, ALU.subtract, ALU.max, ALU.min

    steps, units, fills = schedule()
    banks = bank_table(units)
    del banks
    ctx = ExitStack()
    with ctx:
        def sb(name, cols, dt=fp32):
            return ctx.enter_context(nc.sbuf_tensor(name, [P, cols], dt))

        def sem(name):
            return ctx.enter_context(nc.semaphore(name))

        X = sb("residual", KT * T)
        H = sb("normed", KT * T)
        Y = sb("mixed", KT * T)
        Z = sb("projected", 2 * ZG)
        RING = sb("ring", SLOTS * SLOT)
        SC = sb("silu_c", 2 * DM)
        JUNK = sb("junk", DM, bf16)
        CST = sb("constants", NC_)
        MSK = sb("level_masks", 2 * (LEVELS + 1) * P, u8)
        SM = sb("small", DEPTH * NW)
        FIN = sb("final_w", KT)
        MOD = sb("modulation", DEPTH * 2 * 48)
        AB = sb("norm_gain", 5 * 2 * KT)
        LBV = sb("lower_bounds", 16)
        ST = sb("stats", 192)
        SCR = sb("scratch", 5120)
        PS = ctx.enter_context(nc.psum_tensor("psum", [P, 8 * 512], fp32))

        def bank(b, a=0, e=512):
            return PS[:, 512 * b + a:512 * b + e]

        def seg3(t, n, w=T):
            return t.rearrange("p (n w) -> p n w", n=n, w=w)

        Xv, Hv, Yv = seg3(X[:, :], KT), seg3(H[:, :], KT), seg3(Y[:, :], KT)
        IDN = CST[:, C_ID:C_ID + P]
        cc = lambda c, n=1: CST[:, c:c + n]
        sm = lambda l, c, n=1: SM[:, l * NW + c:l * NW + c + n]
        mod = lambda l, v, c, n=1: MOD[:, (2 * l + v) * 48 + c:(2 * l + v) * 48 + c + n]
        mask = lambda d, lv: MSK[:, ((LEVELS + 1) * d + lv) * P:((LEVELS + 1) * d + lv + 1) * P]
        h4 = lambda ap: ap.rearrange("p (h n) -> p h n", h=NH)
        four = lambda ap: ap[:, None, :].to_broadcast([ap.shape[0], NH, ap.shape[1]])

        loaded = sem("tokens_and_constants_loaded")
        stored = sem("output_stored")
        arrived = [sem(f"weights_arrived_{i}") for i in range(SLOTS)]
        masks_ready = sem("level_masks_are_bytes")
        silu_ready = sem("silu_c_ready")
        ada_done = sem("ada_unit_done")
        gemm_ready = sem("gemm_bank_filled")
        gemm_act = sem("gemm_bank_emptied_by_act")
        gemm_dve = sem("gemm_bank_emptied_by_dve")
        sq_ready = sem("norm_square_ready")
        sq_used = sem("norm_square_summed")
        rstd_ready = sem("norm_rstd_ready")
        scaled = sem("norm_scaled")
        normed = sem("norm_shifted")
        conv_done = sem("ffn_conv_done")
        silu_done = sem("ffn_silu_done")
        prep_pe, prep_act, prep_dve = sem("prep_pe"), sem("prep_act"), sem("prep_dve")
        dn_pe, dn_act, dn_dve = sem("dn_pe"), sem("dn_act"), sem("dn_dve")
        hg_diff, hg_exp, hg_weighed = sem("hg_log_decay_differences"), sem("hg_decays"), sem("hg_weighed")
        hg_factors, hg_out = sem("hg_state_factors"), sem("hg_output_taken")
        hg_tr, hg_kt = sem("hg_keys_transposed"), sem("hg_keys_token_major")
        hg_level, hg_taken = sem("hg_level_scores"), sem("hg_level_taken")
        hg_chunk, hg_state = sem("hg_chunk_products"), sem("hg_state_updated")
        hp_act, hp_dve = sem("hg_prep_act"), sem("hg_prep_dve")
        dp_pe, dp_act, dp_dve = sem("df_prep_pe"), sem("df_prep_act"), sem("df_prep_dve")
        bias_pe, bias_dve = sem("na_bias_filled"), sem("na_bias_masked")
        at_s, at_max, at_exp, at_p = sem("at_scores"), sem("at_max"), sem("at_exp"), sem("at_probs")
        at_tr, at_pt, at_pv, at_o = sem("at_transposed"), sem("at_pt"), sem("at_pv"), sem("at_o")
        post_dve, post_act, post_pe, y_done = sem("post_dve"), sem("post_act"), sem("post_pe"), sem("y_tile_pair_done")
        pe_chain, act_chain, dve_chain = sem("pe_chain"), sem("act_chain"), sem("dve_chain")
        N_LOADS = 4
        loaded_c = sem("conditioning_loaded")

        release, nb, na = [], 0, 0
        ring_units = [u for u in units if u["kind"] != "ba"]
        for u in units:
            nb += len(u["banks"])
            if u["kind"] == "ada":
                na += 1
            if u["kind"] != "ba":
                u["r"] = len(release)
                release.append((ada_done, na) if u["kind"] == "ada" else (gemm_ready, nb))

        def slot(u, n=SLOT):
            o = (u["r"] % SLOTS) * SLOT
            return RING[:, o:o + n]

        def weights(u):
            return arrived[u["r"] % SLOTS], 16 * (u["r"] // SLOTS + 1)

        acts_before, dves_before = {}, {}
        turn = {"act": 0, "dve": 0}
        norms = pairs = pair = 0
        vals = []
        for st in steps:
            if st[0] == "norm":
                dves_before[norms] = turn["dve"]
                norms += 1
            elif st[0] != "unit":
                acts_before[st] = turn["act"]
            for u in [st[1]] if st[0] == "unit" else fills.get(st, ()):
                u["norms"], u["pairs"], u["acts"] = norms, pairs, turn["dve"]
                if u["kind"] == "upg":
                    u["pair"], u["vals2"] = pair, vals[-2] if pair >= 2 else 0
                for b in u["banks"]:
                    turn[b["who"]] = b["turn"]
                if u["kind"] == "upv":
                    u["pair"] = pair
                    pair += 1
                    vals.append(turn["dve"])
                if u["kind"] == "down" and u["m"]:
                    u["acts"] = part_acts
                else:
                    part_acts = u["acts"]
            if st[0] in MIXERS:
                pairs += (TT - (CT if st[1] == DEPTH - 1 else 0)) // 2

        ORD = ([0, 1, 2, 3, 4, 5], [1, 0, 5, 4, 3, 2])

        YS = 2 * T
        def dn_buf(d, name, n):
            off = dict(kb=0, rhs=0, kbT=256, vn=256, vb=512, kdec=768, D=1024, X=1024, t=1024, NT=1536,
                       at=2048, Tm=2560, TTm=3072)[name]
            return Y[:, YS + off:YS + off + n] if d == 0 else SCR[:, 1536 + off:1536 + off + n]
        O = SCR[:, 0:TT * GW]
        DNS = [Y[:, YS + 3584 + 128 * d:YS + 3712 + 128 * d] for d in range(2)]
        BAO = YS + 3840
        ba = lambda i: Y[:, BAO + 48 * i:BAO + 48 * (i + 1)]
        BETA, NBETA, LOGA, G, EG, EDEC, NEGB, TOT, EGL = 2, 3, 4, 5, 6, 7, 8, 9, 10
        PRB = SCR[:, 1536:1536 + 3 * T]
        ROWS4 = [PRB[:, i * T:(i + 1) * T] for i in range(3)] + [SCR[:, 1536 + 3 * T:1536 + 4 * T]]
        SUMS = [(bank(2 + 5 * (i // 2), CTX * (i % 2), CTX * (i % 2) + CTX), bank(3 + i)) for i in range(4)]
        FFG = [Y[:, p * 2 * T:(p + 1) * 2 * T] for p in range(2)]
        FFC = [Y[:, (p + 2) * 2 * T:(p + 3) * 2 * T] for p in range(2)]
        NSQ = [SCR[:, p * T:(p + 1) * T] for p in range(2)]
        RSTD = SCR[:, 2 * T:3 * T]
        HB = lambda d, f: Y[:, (2 + 2 * d + f) * T:(3 + 2 * d + f) * T]
        HGZ = 6 * T + TT * GW
        HE = [w.rearrange("p (l n) -> p l n", l=LEVELS) for w in (Y[:, 6 * T:8 * T], Z[:, 4 * T:6 * T])]
        HGE = [Y[:, 6 * T:7 * T], Y[:, 7 * T:8 * T], Z[:, 4 * T:5 * T], Z[:, 5 * T:6 * T]]
        QKT = [SCR[:, 1536 + 512 * i:2048 + 512 * i] for i in range(3)]
        ATT = [SCR[:, 3072:3584], SCR[:, 4608:5120]]
        HQB = [SCR[:, 3584:3840], Z[:, HGZ:HGZ + 256]]
        HKE = [SCR[:, 3840:4096], Z[:, HGZ + 256:HGZ + 512]]
        HKT = [SCR[:, 4096:4352], Z[:, HGZ + 512:HGZ + 768]]
        HGS = [SCR[:, 4352 + 128 * d:4480 + 128 * d] for d in range(2)]
        HDE = [ST[:, 96 + 4 * d:100 + 4 * d] for d in range(2)]
        NAB = SCR[:, 1536:3328]
        NPT = [SCR[:, 3328 + T * i:3328 + T * (i + 1)] for i in range(2)]
        NP_ = [Y[:, (4 + i) * T:(5 + i) * T] for i in range(2)]
        DPP = [SCR[:, 1536 + 1536 * i:3072 + 1536 * i] for i in range(2)]
        DPT = [Y[:, (4 + i) * T:(5 + i) * T] for i in range(2)]

        region = {"dn": 0, "hg": ZG, "na": 0, "df": ZG}
        fm = lambda g, f: Z[:, region[g] + f * T:region[g] + (f + 1) * T]
        tm = lambda g, i: Z[:, region[g] + 6 * T + i * TT * GW:region[g] + 6 * T + (i + 1) * TT * GW]

        items, parts0 = {}, {}
        n_items = n_parts = 0
        for st in steps:
            if st[0] in ("na", "df"):
                l = st[1]
                qt = range(CT if l == DEPTH - 1 else 0, TT)
                items[st] = (n_items, [(h, t) for h in range(NH) for t in qt])
                n_items += len(items[st][1])
                parts0[st] = n_parts
                n_parts += len(items[st][1]) * (1 if st[0] == "na" else 2)

        def part(st, i, j=0):
            return parts0[st] + (i + 1 if st[0] == "na" else 2 * i + j + 1)

        def new_pair(st, i):
            todo = items[st][1]
            return st[0] == "na" and i < len(todo) and todo[i][0] % 2 == 0 and (i == 0 or todo[i - 1][0] != todo[i][0])
        def points(st):
            return {"dn": 5 + 4 * TT, "hg": 4 + 4 * TT}.get(st[0]) or len(items[st][1]) + 2

        plans = {st: planned(us, points(st)) for st, us in fills.items()}
        posts, n_norm, n_pair = {}, 0, 0
        mixers = [st for st in steps if st[0] in ("dn", "hg", "na", "df")]
        for st in mixers:
            t0 = CT if st[1] == DEPTH - 1 else 0
            posts[st] = (n_norm, n_pair, t0)
            n_norm += st[0] != "na"
            n_pair += (TT - t0) // 2
        YT = {"dn": 0, "na": 2, "df": 4, "hg": 6}
        before = {st: sum((TT - posts[m][2]) // 2 for m in mixers[:i]) for i, st in enumerate(mixers)}
        norm_at = [st for st in steps if st[0] == "norm"]
        block = ctx.enter_context(nc.Block())

        @block.sync
        def _(sp):
            sp.dma_start(SC[:, :], A["c"][:, :]).then_inc(loaded_c, 16)
            for l in range(DEPTH):
                sp.dma_start(SM[:, l * NW:(l + 1) * NW], A["small"][l]).then_inc(loaded_c, 16)
            for r, u in enumerate(ring_units):
                if r == SLOTS:
                    for dst, src in ((X[:, :], A["x"]), (CST[:, :], A["const"]), (Z[:, 0:2 * (LEVELS + 1) * P], A["masks"]), (FIN[:, :], A["fin"])):
                        sp.dma_start(dst, src[:, :]).then_inc(loaded, 16)
                if r >= SLOTS:
                    sp.wait_ge(*release[r - SLOTS])
                k, l = u["kind"], u["l"]
                n = SLOT
                if k == "ada":
                    src = A["ada"][l, u["u"]]
                elif k in ("fm", "tm"):
                    src = A["win"][l, u["col"]]
                elif k == "out":
                    src = A["wout"][l, u["u"]]
                elif k in ("upg", "upv"):
                    src = A["wup"][l, u["u"] + (0 if k == "upg" else FT // 2)]
                else:
                    a, b = PARTS[u["part"]]
                    n = (b - a) * P
                    src = A["wdn"][l, u["m"]][:, a * P:b * P]
                sp.dma_start(slot(u, n), src).then_inc(arrived[r % SLOTS], 16)
            sp.wait_ge(scaled, KT * len(norm_at))
            sp.dma_start(out[:, :, :], Hv[:, :, CTX:T]).then_inc(stored, 16)
            sp.wait_ge(stored, 16)

        @block.tensor
        def _(pe):
            own = Turns(pe_chain)
            mm, tr = nc.tensor.matmul, nc.tensor.transpose
            emptied = []

            def gemm_unit(u, some=None):
                k, l = u["kind"], u["l"]
                if k == "ada":
                    return
                if k != "ba":
                    pe.wait_ge(*weights(u))
                if k in ("fm", "tm", "ba", "upg", "upv"):
                    pe.wait_ge(normed, KT * u["norms"])
                if k == "out":
                    pe.wait_ge(y_done, u["pairs"])
                if k == "down":
                    pe.wait_ge(gemm_dve, u["acts"])
                for b in some or u["banks"]:
                    if len(emptied) >= 2:
                        pe.wait_ge(*emptied[-2])
                    emptied.append((gemm_act if b["who"] == "act" else gemm_dve, b["turn"]))
                    ps = bank(b["n"] % 2)
                    if k == "tm":
                        for i, t in enumerate(b["what"]):
                            for kk in range(KT):
                                last = mm(ps[:, i * GW:(i + 1) * GW], Hv[:, kk, t * P:(t + 1) * P],
                                          slot(u)[:, kk * GW:(kk + 1) * GW], start=kk == 0, stop=kk == KT - 1)
                                if kk % 2:
                                    yield
                    elif k == "ba":
                        for t in range(TT):
                            for kk in range(KT):
                                last = mm(ps[:, t * 16:(t + 1) * 16], Hv[:, kk, t * P:(t + 1) * P],
                                          sm(l, W_BA + kk * 16, 16), start=kk == 0, stop=kk == KT - 1)
                    else:
                        f, (a, e) = b["what"]
                        if k == "down":
                            p0, p1 = PARTS[u["part"]]
                            nk, src, step = p1 - p0, Z, P
                        else:
                            nk, src, step = KT, (Y if k == "out" else H), GW
                        ks = u["rows"] if k == "out" else range(nk)
                        for kk in ks:
                            o = kk * step + f * P
                            last = mm(ps[:, 0:e - a], slot(u)[:, o:o + P], src[:, kk * T + a:kk * T + e],
                                      start=kk == ks[0], stop=kk == ks[-1])
                            if e - a > CTX or kk % 2:
                                yield
                    last.then_inc(*own(gemm_ready))

            def norm(ni, segs):
                pe.wait_ge(rstd_ready, ni)
                for k in range(KT):
                    pe.wait_ge(sq_ready, KT * ni + k + 1)
                    for i, (a, e) in enumerate(segs):
                        last = mm(bank(2 + i, 0, e - a), cc(C_MEAN, P), NSQ[k % 2][:, a:e],
                                  start=k == 0, stop=k == KT - 1)
                    last.then_inc(*own(sq_used))

            def dn(l):
                for _ in range(5):
                    yield True
                for i in range(4):
                    pe.wait_ge(prep_act, at(PR_ACT, l, f"q{i}"))
                    mm(SUMS[i][0], cc(C_BLK, P), ROWS4[i][:, 0:CTX], start=True, stop=True)
                    mm(SUMS[i][1], cc(C_BLK, P), ROWS4[i][:, CTX:T], start=True, stop=True).then_inc(*own(prep_pe))
                pe.wait_ge(prep_dve, at(PR_DVE, l, "b2"))
                pe.wait_ge(prep_act, at(PR_ACT, l, "r3"))
                LG = ba(LOGA).rearrange("p (t d h) -> p t d h", t=TT, d=2)
                gp = bank(4, 0, 48).rearrange("p (t d h) -> p t d h", t=TT, d=2)
                for d in range(2):
                    mm(gp[:, :, d, :], cc(C_INC + d * P, P), LG[:, :, d, :], start=True, stop=True)
                mm(bank(4, 48, 96), cc(C_BLK, P), ba(LOGA), start=True, stop=True)
                for t in range(TT):
                    for d in range(2):
                        for hp in range(2):
                            o = 96 + ((t * 2 + d) * 2 + hp) * 2
                            for h in range(2):
                                last = mm(bank(4, o, o + 2)[64 * h:64 * h + 64, :],
                                          LG[:, t, d, 2 * hp + h:2 * hp + h + 1].to_broadcast([P, HD]),
                                          cc(C_CHK, 2), start=True, stop=True)
                last.then_inc(*own(prep_pe))
                pe.wait_ge(prep_dve, at(PR_DVE, l, "b4"))
                pe.wait_ge(prep_act, at(PR_ACT, l, "b3"))
                for n in range(TT):
                    g = TT * l + n
                    A, B, C = [bank(2), bank(5)], [bank(3), bank(6)], [bank(4), bank(7)]
                    tile = [ORD[d][n] for d in range(2)]
                    cols = [slice(t * P, (t + 1) * P) for t in tile]

                    def done(ins):
                        ins.then_inc(*own(dn_pe))

                    def by_rows(product):
                        for odd in range(2):
                            if odd:
                                last.then_inc(*own())
                                pe.wait_ge(*own.last)
                            for h in (odd, odd + 2):
                                last = product(h, slice(64 * odd, 64 * odd + 64))
                        done(last)

                    for d in range(2):
                        if g:
                            pe.wait_ge(dn_dve, at2(DN_DVE, g - 1, "O", d))
                        for i, f in enumerate((2, 3, 4, 5)):
                            last = tr(A[d][:, i * P:(i + 1) * P], fm("dn", f)[:, cols[d]], IDN)
                        done(last)
                        yield False
                    for d in range(2):
                        for h in range(NH):
                            last = mm(C[d][:, h * P:(h + 1) * P], LG[:, tile[d], d, h:h + 1].to_broadcast([P, P]),
                                      cc(C_INC + d * P, P), start=True, stop=True)
                        done(last)
                        yield False
                    yield True
                    for d in range(2):
                        pe.wait_ge(dn_dve, at2(DN_DVE, g, "kb", d))
                        for i in range(2):
                            last = tr(B[d][:, i * P:(i + 1) * P], dn_buf(d, "kb", 256)[:, i * P:(i + 1) * P], IDN)
                        done(last)
                        yield False
                    for d in range(2):
                        pe.wait_ge(dn_act, at2(DN_ACT, g, "kbT", d))
                        by_rows(lambda h, r: mm(
                            A[d][:, h * P:(h + 1) * P], fm("dn", 2 + h // 2)[r, cols[d]],
                            dn_buf(d, "kbT", 256)[r, (h // 2) * P:(h // 2 + 1) * P], start=True, stop=True))
                        yield False
                    for d in range(2):
                        by_rows(lambda h, r: mm(
                            B[d][:, h * P:(h + 1) * P], fm("dn", 2 + h // 2)[r, cols[d]],
                            fm("dn", h // 2)[r, cols[d]], start=True, stop=True))
                        yield False
                    for d in range(2):
                        pe.wait_ge(dn_dve, at2(DN_DVE, g, "NT", d))
                        for h in range(NH):
                            last = tr(C[d][:, h * P:(h + 1) * P], dn_buf(d, "NT", 512)[:, h * P:(h + 1) * P], IDN)
                        done(last)
                        yield False
                    yield True
                    for i in range(5):
                        for d in range(2):
                            pe.wait_ge(dn_dve, at2(DN_DVE, g, "M" if i == 0 else f"L{i - 1}", d))
                            for h in range(NH):
                                hs = slice(h * P, (h + 1) * P)
                                last = mm(A[d][:, hs], dn_buf(d, "NT", 512)[:, hs], dn_buf(d, "Tm", 512)[:, hs],
                                          start=True, stop=True)
                            done(last)
                            yield False
                        for d in range(2):
                            pe.wait_ge(dn_act, at2(DN_ACT, g, f"X{i}", d))
                            for h in range(NH):
                                hs = slice(h * P, (h + 1) * P)
                                last = mm(B[d][:, hs], dn_buf(d, "X", 512)[:, hs], dn_buf(d, "TTm", 512)[:, hs],
                                          start=True, stop=True)
                            if i < 4:
                                for h in range(NH):
                                    hs = slice(h * P, (h + 1) * P)
                                    last = mm(C[d][:, hs], dn_buf(d, "TTm", 512)[:, hs], dn_buf(d, "X", 512)[:, hs],
                                              start=True, stop=True)
                            done(last)
                            yield False
                    yield True
                    for j in range(2):
                        if j:
                            yield True
                        for d in range(2):
                            pe.wait_ge(dn_dve, at2(DN_DVE, g, "L4" if j == 0 else "S0", d))
                            c = j if d == 0 else 1 - j
                            rows = slice(64 * c, 64 * c + 64)
                            t0 = tile[d] * P + 64 * c

                            def read(h, r):
                                for w in range(2):
                                    f = (2 if w == 0 else 0) + h // 2
                                    o = w * GW + h * HD
                                    last = mm(A[d][rows, o:o + HD], fm("dn", f)[r, t0:t0 + 64],
                                              DNS[d][r, (h // 2) * HD:(h // 2 + 1) * HD], start=True, stop=True)
                                return last
                            by_rows(read)
                            yield False
                        for d in range(2):
                            pe.wait_ge(dn_dve, at2(DN_DVE, g, f"R{j}", d))
                            c = j if d == 0 else 1 - j
                            rows = slice(64 * c, 64 * c + 64)
                            for h in range(NH):
                                last = mm(B[d][rows, h * HD:(h + 1) * HD],
                                          dn_buf(d, "TTm", 512)[rows, h * P + 64 * c:h * P + 64 * c + 64],
                                          dn_buf(d, "rhs", 256)[rows, h * HD:(h + 1) * HD], start=True, stop=True)
                            done(last)
                            yield False
                        for d in range(2):
                            pe.wait_ge(dn_act, at2(DN_ACT, g, f"V{j}", d))
                            c = j if d == 0 else 1 - j
                            rows = slice(64 * c, 64 * c + 64)
                            vn = dn_buf(d, "vn", 256)
                            for h in range(NH):
                                r = slice(64 * (h % 2), 64 * (h % 2) + 64)
                                mm(B[d][r, 256 + (h // 2) * HD:256 + (h // 2 + 1) * HD],
                                   dn_buf(d, "kdec", 256)[rows, h * HD:(h + 1) * HD], vn[rows, h * HD:(h + 1) * HD],
                                   start=True, stop=True)
                            for h in range(NH):
                                last = mm(C[d][rows, h * HD:(h + 1) * HD],
                                          dn_buf(d, "at", 512)[rows, h * P + 64 * c:h * P + 64 * c + 64],
                                          vn[rows, h * HD:(h + 1) * HD], start=True, stop=True)
                            done(last)
                            yield False

            def hg(l):
                for _ in range(4):
                    yield True
                pe.wait_ge(hp_dve, at(HP_DVE, l, "b3"))
                pe.wait_ge(hp_act, at(HP_ACT, l, "k3"))

                def chunk(q, n, d, j):
                    t = ORD[d][n]
                    c = j if d == 0 else 1 - j
                    rows = slice(64 * c, 64 * c + 64)
                    if j == 0:
                        if wanted(q):
                            pe.wait_ge(hg_taken, at(HG_P, wanted_before(q), HG_P[-1]))
                        pe.wait_ge(hg_kt, q + 1)
                        if q:
                            pe.wait_ge(hg_state, at(HG_U, q - 1, "U1"))
                            pe.wait_ge(hg_out, wanted_before(q))
                    else:
                        pe.wait_ge(hg_state, at(HG_U, q, "U0"))
                    v = tm("hg", 0)[:, t * GW:(t + 1) * GW]
                    for h in range(NH) if wanted(q) else ():
                        hc = slice(h * HD, (h + 1) * HD)
                        last = mm(bank(6)[rows, hc], ATT[d][rows, h * P + 64 * c:h * P + 64 * c + 64], v[rows, hc],
                                  start=h == 0, stop=False, skip_group_check=True)
                    for h in (0, 2, 1, 3) if wanted(q) else ():
                        r = slice(64 * (h % 2), 64 * (h % 2) + 64)
                        f = h // 2
                        hc = slice(h * HD, (h + 1) * HD)
                        if h < 2:
                            last.then_inc(*own())
                            pe.wait_ge(*own.last)
                        last = mm(bank(6)[rows, hc], HQB[d][r, f * P + 64 * c:f * P + 64 * c + 64],
                                  HGS[d][r, f * HD:(f + 1) * HD], start=False, stop=True, skip_group_check=True)
                    for h in range(NH):
                        r = slice(64 * (h % 2), 64 * (h % 2) + 64)
                        f = h // 2
                        hc = slice(h * HD, (h + 1) * HD)
                        last = mm(bank(7)[r, f * HD:(f + 1) * HD], HKT[d][rows, hc], v[rows, hc], start=True, stop=True)
                    last.then_inc(*own(hg_chunk))

                for n in range(TT):
                    for d in range(2):
                        q = 2 * (TT * l + n) + d
                        before_ = (q - 1, n - 1 + d, 1 - d)
                        t = ORD[d][n]
                        cs = slice(t * P, (t + 1) * P)
                        pe.wait_ge(hg_factors, q + 1)
                        if q:
                            pe.wait_ge(hg_kt, q)
                        for i in range(2):
                            last = tr(bank(2, i * P, (i + 1) * P), HKE[d][:, i * P:(i + 1) * P], IDN)
                        last.then_inc(*own(hg_tr))
                        yield False
                        yield True
                        if not wanted(q) and n + d:
                            for j in range(2):
                                chunk(*before_, j)
                                yield False
                        for lv in range(LEVELS + 1) if wanted(q) else ():
                            w = wanted_before(q)
                            if lv:
                                pe.wait_ge(hg_weighed, at(HG_M, w, f"M{lv}"))
                            g = (LEVELS + 1) * w + lv
                            if g >= 3:
                                pe.wait_ge(hg_taken, g - 2)
                            for h in (0, 2, 1, 3):
                                r = slice(64 * (h % 2), 64 * (h % 2) + 64)
                                f = h // 2
                                if h == 1:
                                    last.then_inc(*own())
                                    pe.wait_ge(*own.last)
                                if lv == 0:
                                    kk, qq = fm("hg", 2 + 2 * d + f)[r, cs], fm("hg", f)[r, cs]
                                else:
                                    w = QKT[lv % 3]
                                    qq, kk = w[r, f * P:(f + 1) * P], w[r, 256 + f * P:256 + (f + 1) * P]
                                last = mm(bank(3 + g % 3, h * P, (h + 1) * P), kk, qq, start=True, stop=True)
                            last.then_inc(*own(hg_level))
                            yield False
                            if lv in (1, 3) and n + d:
                                chunk(*before_, lv // 2)
                                yield False
                        yield True
                for j in range(2):
                    chunk(2 * TT * (l + 1) - 1, TT - 1, 1, j)
                    yield False

            def attend(st):
                kind, l = st
                i0, todo = items[st]
                na = kind == "na"
                v = tm(kind, 0)
                tr_b, pv_b = PS[:, 6 * 512:6 * 512 + T], bank(7, 256, 256 + HD)

                def bias(hp):
                    for rnd in range(4):
                        gi = 4 * (2 * l + hp) + rnd
                        if rnd >= 2:
                            pe.wait_ge(bias_dve, gi - 1)
                        for k in range(16):
                            s = 63 - (rnd * 16 + k)
                            last = mm(bank(2 + 2 * (rnd % 2), k * 28, (k + 1) * 28), CST[0:64, C_AJ + s:C_AJ + s + P],
                                      SM[0:64, l * NW + W_RPB + hp * 28:l * NW + W_RPB + (hp + 1) * 28],
                                      start=True, stop=True)
                        last.then_inc(*own(bias_pe))

                def scores(i, j):
                    h, t = todo[i]
                    s = 64 * (h % 2) + 32 * j
                    r = slice(s, s + (64 if na else 32))
                    qq = fm(kind, h // 2)[r, t * P:(t + 1) * P]
                    kk = fm(kind, 2 + h // 2)
                    b0 = 512 * (2 + 2 * ((i0 + i) % 2 if na else j))
                    if t >= CT:
                        mm(PS[:, b0:b0 + LAT], qq, kk[r, CTX:T], start=True, stop=True)
                    mm(PS[:, b0 + LAT:b0 + T], qq, kk[r, 0:CTX], start=True, stop=True).then_inc(*own(at_s))

                def keys_of(i):
                    return [(o, (o + CT) if o < 4 else o - 4) for o in (range(6) if todo[i][1] >= CT else (4, 5))]

                def values(i):
                    h, g = todo[i][0], i0 + i
                    pt = (NPT if na else DPT)[g % 2]
                    pe.wait_ge(at_pt, g + 1)
                    kts = keys_of(i)
                    for o, kt in kts:
                        last = mm(pv_b, pt[:, o * P:(o + 1) * P], v[:, kt * GW + h * HD:kt * GW + (h + 1) * HD],
                                  start=o == kts[0][0], stop=o == kts[-1][0])
                    last.then_inc(*own(at_pv))

                def transposes(i):
                    g = i0 + i
                    prob = NP_[g % 2] if na else DPP[g % 2][:, 0:T]
                    pe.wait_ge(at_p, g + 1)
                    pe.wait_ge(at_o, g)
                    for o, _ in keys_of(i):
                        last = tr(tr_b[:, o * P:(o + 1) * P], prob[:, o * P:(o + 1) * P], IDN)
                    last.then_inc(*own(at_tr))

                n = len(todo)
                for i in range(n + 2):
                    if new_pair(st, i):
                        if i:
                            pe.wait_ge(at_exp, part(st, i - 1))
                        bias(todo[i][0] // 2)
                        pe.wait_ge(bias_dve, 4 * (2 * l + todo[i][0] // 2) + 4)
                    if i < n:
                        for j in range(1 if na else 2):
                            back = 2 if na else 1
                            if i >= back:
                                pe.wait_ge(at_exp, part(st, i - back, j))
                            scores(i, j)
                            yield False
                    yield False
                    if i >= 2:
                        values(i - 2)
                    yield False
                    yield False
                    if 0 < i <= n:
                        transposes(i - 1)
                    yield True

            def df(st):
                l = st[1]
                for i in range(4):
                    mm(bank(2 + i), cc(C_ROT, P), fm("df", i)[:, CTX:T], start=True, stop=True).then_inc(*own(dp_pe))
                pe.wait_ge(dp_dve, at(DP_DVE, l, "lam"))
                yield from attend(st)

            def post(st):
                _, p0, t0 = posts[st]
                if st[0] != "na":
                    pe.wait_ge(post_dve, 2 * (posts[st][0] + 1))
                else:
                    pe.wait_ge(at_o, items[st][0] + len(items[st][1]))
                for i, t in enumerate(range(t0, TT, 2)):
                    b = 2 + i
                    for f in range(2):
                        for k in range(2):
                            o = f * GW + k * P
                            last = tr(bank(b, o, o + P), O[:, (t + k) * GW + f * P:(t + k) * GW + (f + 1) * P], IDN)
                    last.then_inc(*own(post_pe))

            pe.wait_ge(loaded_c, 16 * (1 + DEPTH))
            pe.wait_ge(loaded, 16 * N_LOADS)
            for st in steps:
                kind = st[0]
                if kind == "unit":
                    for _ in gemm_unit(st[1]):
                        pass
                elif kind == "norm":
                    norm(norm_at.index(st), st[3])
                else:
                    pe.wait_ge(gemm_act, acts_before[st])
                    pe.wait_ge(y_done, before[st])
                    body = dn(st[1]) if kind == "dn" else hg(st[1]) if kind == "hg" else df(st) if kind == "df" else attend(st)
                    work, k = iter(()), 0
                    for shared in body:
                        if shared:
                            for _ in work:
                                pass
                            work = chain.from_iterable(gemm_unit(*piece) for piece in plans[st][k])
                            k += 1
                        else:
                            next(work, None)
                    for _ in work:
                        pass
                    post(st)

        @block.scalar
        def _(act):
            own = Turns(act_chain)
            af = nc.scalar.activation
            eps, one = cc(C_EPS), cc(C_ONE)

            def gemm_unit(u, some=None):
                k, l = u["kind"], u["l"]
                for b in some or u["banks"]:
                    if b is None or b["who"] != "act":
                        continue
                    act.wait_ge(gemm_ready, b["n"] + 1)
                    ps = bank(b["n"] % 2)
                    if k == "ba":
                        af(Y[:, BAO:BAO + 96], ps[:, 0:96], ACT.Copy).then_inc(*own(gemm_act))
                    elif k == "tm":
                        t = b["what"][0]
                        o = u["z"] + t * GW
                        af(Z[:, o:o + 2 * GW], ps, ACT.Copy).then_inc(*own(gemm_act))
                    elif k == "fm":
                        f, (a, e) = b["what"]
                        o = u["z"] + f * T
                        af(Z[:, o + a:o + e], ps[:, 0:e - a], ACT.Copy, scale=u["scale"]).then_inc(*own(gemm_act))
                    else:
                        f, (a, e) = b["what"]
                        p = u["pair"]
                        if p >= 2:
                            act.wait_ge(conv_done, p - 1)
                            act.wait_ge(gemm_dve, u["vals2"])
                        af(FFG[p % 2][:, f * T + a:f * T + e], ps[:, 0:e - a], ACT.Copy).then_inc(*own())
                        w1 = sm(l, W_FFC + (2 * u["u"] + f) * 3 + 1)
                        af(FFC[p % 2][:, f * T + a:f * T + e], ps[:, 0:e - a], ACT.Copy, scale=w1).then_inc(*own(gemm_act))
                if k == "upv":
                    p = u["pair"]
                    act.wait_ge(conv_done, p + 1)
                    a = u["segs"][0][0]
                    v = seg3(FFC[p % 2], 2)[:, :, a:T]
                    af(v, v, ACT.Silu).then_inc(*own(silu_done))

            def rsqrt(dst, src, scale=1.0, last=None):
                af(dst, src, ACT.Ln, bias=eps, scale=scale).then_inc(*own())
                act.wait_ge(*own.last)
                af(dst, dst, ACT.Exp, scale=-0.5).then_inc(*own(last))

            def norm(ni, segs, l):
                a0 = segs[0][0]
                if ni:
                    act.wait_ge(gemm_dve, dves_before[ni])
                for k in range(KT):
                    if KT * ni + k >= 2:
                        act.wait_ge(sq_used, KT * ni + k - 1)
                    af(NSQ[k % 2][:, a0:T], Xv[:, k, a0:T], ACT.Square).then_inc(*own(sq_ready))
                act.wait_ge(sq_used, KT * (ni + 1))
                for i, (a, e) in enumerate(segs):
                    af(RSTD[:, a:e], bank(2 + i, 0, e - a), ACT.Ln, bias=eps).then_inc(*own())
                act.wait_ge(*own.last)
                af(RSTD[:, a0:T], RSTD[:, a0:T], ACT.Exp, scale=-0.5).then_inc(*own(rstd_ready))
                if l == DEPTH:
                    return
                act.wait_ge(masks_ready, 1)
                for k in range(KT):
                    act.wait_ge(scaled, KT * ni + k + 1)
                    for i, (a, e) in enumerate(segs):
                        shift = mod(l, 0 if a == 0 else 1, (0 if ni % 2 == 0 else 24) + k)
                        last = af(Hv[:, k, a:e], Hv[:, k, a:e], ACT.Identity, bias=shift)
                        last.then_inc(*own(normed if i == len(segs) - 1 else None))

            def dn(l):
                P3 = lambda i: PRB[:, i * T:(i + 1) * T]
                for f in range(6):
                    if f >= 2:
                        act.wait_ge(prep_act, at(PR_ACT, l, f"s{f - 2}"))
                    af(P3(f % 2), fm("dn", f), ACT.Copy, scale=sm(l, W_DNC + f * 3 + 1)).then_inc(*own(prep_act))
                    act.wait_ge(prep_dve, at(PR_DVE, l, f"c{f}"))
                    af(fm("dn", f), P3(f % 2), ACT.Silu).then_inc(*own(prep_act))
                    if f < 5:
                        yield
                for f in range(4):
                    act.wait_ge(prep_act, at(PR_ACT, l, "s5"))
                    af(ROWS4[f], fm("dn", f), ACT.Square).then_inc(*own(prep_act))
                for f in range(4):
                    act.wait_ge(prep_pe, at(PR_PE, l, f"n{f | 1}"))
                    af(ROWS4[f][:, 0:CTX], SUMS[f][0], ACT.Ln, bias=eps).then_inc(*own())
                    af(ROWS4[f][:, CTX:T], SUMS[f][1], ACT.Ln, bias=eps).then_inc(*own())
                act.wait_ge(*own.last)
                for f in range(4):
                    af(ROWS4[f], ROWS4[f], ACT.Exp, scale=-0.5).then_inc(*own(prep_act))
                act.wait_ge(hp_dve, at(HP_DVE, l, "lb1"))
                af(ST[:, 108:116], ST[:, 108:116], ACT.Exp).then_inc(*own(hp_act))
                act.wait_ge(prep_dve, at(PR_DVE, l, "b1"))
                af(ba(BETA), ba(NEGB), ACT.Exp, scale=-1.0).then_inc(*own())
                af(ba(EDEC), ba(EG), ACT.Exp, scale=-1.0).then_inc(*own())
                af(ba(TOT)[:, 0:8], sm(l, W_ALOG, 8), ACT.Exp).then_inc(*own())
                act.wait_ge(*own.last)
                af(ba(EDEC), ba(EDEC), ACT.Ln, bias=one).then_inc(*own(prep_act))
                act.wait_ge(prep_pe, at(PR_PE, l, "cum"))
                af(ba(G), bank(4, 0, 48), ACT.Copy).then_inc(*own())
                af(ba(TOT), bank(4, 48, 96), ACT.Copy).then_inc(*own())
                af(ba(EG), bank(4, 0, 48), ACT.Exp).then_inc(*own())
                af(ba(EGL), bank(4, 96, 144), ACT.Exp).then_inc(*own(prep_act))
                act.wait_ge(prep_dve, at(PR_DVE, l, "b3"))
                af(ba(EDEC), ba(EDEC), ACT.Exp).then_inc(*own(prep_act))
                act.wait_ge(hp_dve, at(HP_DVE, l, "lb2"))
                af(LBV[:, 4:8], LBV[:, 4:8], ACT.Ln).then_inc(*own(hp_act))
                for n in range(TT):
                    g = TT * l + n
                    B, A = [bank(3), bank(6)], [bank(2), bank(5)]
                    for d in range(2):
                        if n:
                            act.wait_ge(dn_dve, at2(DN_DVE, g - 1, "O", d))
                        af(h4(dn_buf(d, "Tm", 512)), four(IDN), ACT.Copy).then_inc(*own())
                        af(h4(dn_buf(d, "TTm", 512)), four(IDN), ACT.Copy).then_inc(*own(dn_act))
                    yield
                    for d in range(2):
                        act.wait_ge(dn_pe, at2(DN_PE, g, "kb", d))
                        af(dn_buf(d, "kbT", 256), B[d][:, 0:256], ACT.Copy).then_inc(*own(dn_act))
                    for d in range(2):
                        act.wait_ge(dn_dve, at2(DN_DVE, g, "R", d))
                        af(dn_buf(d, "D", 512), dn_buf(d, "D", 512), ACT.Exp).then_inc(*own(dn_act))
                    yield
                    for i in range(5):
                        for d in range(2):
                            act.wait_ge(dn_pe, at2(DN_PE, g, f"X{i}", d))
                            af(dn_buf(d, "X", 512), A[d], ACT.Copy).then_inc(*own(dn_act))
                    yield
                    for j in range(2):
                        if j:
                            yield
                        for d in range(2):
                            act.wait_ge(dn_pe, at2(DN_PE, g, f"V{j}", d))
                            c = j if d == 0 else 1 - j
                            rows = slice(64 * c, 64 * c + 64)
                            af(dn_buf(d, "vn", 256)[rows, :], B[d][rows, 0:256], ACT.Copy).then_inc(*own(dn_act))

            def hg(l):
                act.wait_ge(*own.last)
                for i in range(4):
                    act.wait_ge(hp_dve, at(HP_DVE, l, f"c{i}"))
                    af(HGE[i], fm("hg", 2 + i), ACT.Exp, scale=-1.0).then_inc(*own())
                yield
                act.wait_ge(*own.last)
                for i in range(4):
                    af(ROWS4[i], HGE[i], ACT.Ln, scale=LBV[:, i:i + 1], bias=one).then_inc(*own())
                    af(HGE[i], HGE[i], ACT.Ln, bias=one).then_inc(*own(hp_act))
                    if i % 2:
                        yield
                for i in range(4):
                    F = fm("hg", 2 + i)
                    act.wait_ge(hp_dve, at(HP_DVE, l, f"l{i}"))
                    af(F, F, ACT.Exp, scale=-1.0, bias=LBV[:, 4 + i:5 + i]).then_inc(*own(hp_act))
                yield

                def decays(q, n, d):
                    t = ORD[d][n]
                    he = [Y[:, 6 * T:8 * T], Z[:, 4 * T:6 * T]][d]
                    act.wait_ge(hg_diff, q + 1)
                    if wanted(q):
                        af(he, he, ACT.Abs).then_inc(*own())
                        act.wait_ge(*own.last)
                        af(he, he, ACT.Exp, scale=-1.0).then_inc(*own())
                    if q >= 2:
                        act.wait_ge(hg_chunk, at(HG_C, q - 2, "C1"))
                        act.wait_ge(hg_state, at(HG_U, q - 2, "U1"))
                    hbt = Y[:, (2 + 2 * d) * T:(4 + 2 * d) * T].rearrange("p (f n) -> p f n", f=2)[:, :, t * P:(t + 1) * P]
                    if wanted(q):
                        af(HQB[d].rearrange("p (f n) -> p f n", f=2), hbt, ACT.Exp).then_inc(*own())
                    ed = 63 if d == 0 else 0
                    bl = hbt.rearrange("p f (c j) -> p f c j", c=2)[:, :, :, ed]
                    af(HDE[d].rearrange("p (f c) -> p f c", f=2), bl, ACT.Exp).then_inc(*own())
                    af(HKE[d], HKE[d], ACT.Exp, scale=-1.0).then_inc(*own(hg_exp))

                for n in range(TT):
                    for d in range(2):
                        q = 2 * (TT * l + n) + d
                        if n == d == 0:
                            decays(q, n, d)
                        act.wait_ge(hg_tr, q + 1)
                        if q >= 2:
                            act.wait_ge(hg_chunk, at(HG_C, q - 2, "C1"))
                        af(HKT[d], bank(2, 0, 256), ACT.Copy).then_inc(*own(hg_kt))
                        yield
                        if (n, d) != (TT - 1, 1):
                            decays(q + 1, n + d, 1 - d)
                        yield

            def attend(st):
                kind, l = st
                i0, todo = items[st]
                na = kind == "na"
                def exps(i):
                    h, t = todo[i]
                    g = i0 + i
                    a = 0 if t >= CT else LAT
                    s = ST[:, 8 * (g % 4):8 * (g % 4) + 8]
                    if i >= 2:
                        act.wait_ge(at_tr, g - 1)
                    if na:
                        act.wait_ge(at_max, part(st, i))
                        pr = NP_[g % 2]
                        b0 = 512 * (2 + 2 * (g % 2))
                        if a == 0:
                            af(pr[:, 0:LAT], pr[:, 0:LAT], ACT.Exp, bias=s[:, 0:1], accum_out=s[:, 2:3]).then_inc(*own())
                        af(pr[:, LAT:T], PS[:, b0 + LAT:b0 + T], ACT.Exp, bias=s[:, 0:1],
                           accum_out=s[:, 3:4]).then_inc(*own(at_exp))
                    else:
                        for j in range(2):
                            act.wait_ge(at_max, part(st, i, j))
                            b0 = 512 * (2 + 2 * j)
                            af(DPP[g % 2][:, j * T + a:(j + 1) * T], PS[:, b0 + a:b0 + T], ACT.Exp,
                               bias=s[:, j:j + 1], accum_out=s[:, 2 + j:3 + j]).then_inc(*own(at_exp))

                def evac(i):
                    g = i0 + i
                    a = 0 if todo[i][1] >= CT else LAT
                    act.wait_ge(at_tr, g + 1)
                    if i >= 2:
                        act.wait_ge(at_pv, g - 1)
                    af((NPT if na else DPT)[g % 2][:, a:T], PS[:, 6 * 512 + a:6 * 512 + T], ACT.Copy).then_inc(*own(at_pt))

                n = len(todo)
                for i in range(n + 2):
                    if i < n:
                        exps(i)
                    if 0 < i <= n:
                        evac(i - 1)
                    yield

            def df(st):
                act.wait_ge(dp_dve, at(DP_DVE, st[1], "d"))
                af(ST[:, 36:38], ST[:, 34:36], ACT.Exp).then_inc(*own(dp_act))
                yield from attend(st)

            def post(st):
                m, p0, t0 = posts[st]
                kind, l = st
                w = (TT - t0) * GW
                nt = TT - t0
                o = O[:, t0 * GW:TT * GW]
                if kind != "na":
                    if kind in ("dn", "hg"):
                        gate = tm(kind, 0 if kind == "dn" else 1)[:, t0 * GW:TT * GW]
                        af(gate, gate, ACT.Silu).then_inc(*own())
                    act.wait_ge(post_dve, 2 * m)
                    if kind == "dn":
                        act.wait_ge(dn_dve, at2(DN_DVE, TT * l + TT - 1, "O", 1))
                    elif kind == "hg":
                        act.wait_ge(hg_out, wanted_before(2 * TT * (l + 1)))
                        act.wait_ge(hg_chunk, at(HG_C, 2 * TT * (l + 1) - 1, "C1"))
                    else:
                        act.wait_ge(at_o, items[st][0] + len(items[st][1]))
                    sq = SCR[:, 1536:1536 + w]
                    af(sq, o, ACT.Square).then_inc(*own(post_act))
                    act.wait_ge(post_dve, 2 * m + 1)
                    rsqrt(ST[:, 40:40 + 4 * nt], ST[:, 40:40 + 4 * nt], 1.0 / HD, post_act)
                f = YT[kind]
                for i, t in enumerate(range(t0, TT, 2)):
                    act.wait_ge(post_pe, p0 + i + 1)
                    dst = Yv[:, f:f + 2, t * P:(t + 2) * P]
                    af(dst, bank(2 + i).rearrange("p (f n) -> p f n", f=2), ACT.Copy).then_inc(*own(y_done))

            act.wait_ge(loaded_c, 16 * (1 + DEPTH))
            af(SC[:, :], SC[:, :], ACT.Silu).then_inc(*own(silu_ready))
            act.wait_ge(loaded, 16 * N_LOADS)
            for st in steps:
                kind = st[0]
                if kind == "unit":
                    gemm_unit(st[1])
                elif kind == "norm":
                    norm(norm_at.index(st), st[3], st[1])
                else:
                    act.wait_ge(y_done, before[st])
                    body = dn(st[1]) if kind == "dn" else hg(st[1]) if kind == "hg" else df(st) if kind == "df" else attend(st)
                    filled(plans[st], body, gemm_unit, 1)
                    post(st)

        @block.vector
        def _(dve):
            own = Turns(dve_chain)
            v = nc.vector
            tt, ts, stt, ttr = v.tensor_tensor, v.tensor_scalar, v.scalar_tensor_tensor, v.tensor_tensor_reduce

            def taps(dst, src, w, a, e, sem_=None):
                dve.wait_ge(*own.last)
                stt(dst[:, a + 1:e], src[:, a:e - 1], w(0), dst[:, a + 1:e], MUL, ADD).then_inc(*own())
                dve.wait_ge(*own.last)
                stt(dst[:, a:e - 1], src[:, a + 1:e], w(2), dst[:, a:e - 1], MUL, ADD).then_inc(*own(sem_))

            def gemm_unit(u, some=None):
                k, l = u["kind"], u["l"]
                if k == "ada":
                    dve.wait_ge(*weights(u))
                    dve.wait_ge(silu_ready, 1)
                    vecs = (0, 1) if (l < DEPTH - 1 or u["u"] < 8) else (1,)
                    for j in range(2):
                        m = 2 * u["u"] + j
                        for vec in vecs:
                            last = (j, vec) == (1, vecs[-1])
                            dve.wait_ge(*own.last) if own.last else None
                            ttr(out=JUNK[:, :], in0=slot(u)[:, j * DM:(j + 1) * DM], in1=SC[:, vec * DM:(vec + 1) * DM],
                                      scale=1.0, scalar=sm(l, W_BADA + m), op0=MUL, op1=ADD,
                                      accum_out=mod(l, vec, m)).then_inc(*own(ada_done if last else None))
                    return
                if k == "upg":
                    p = u["pair"]
                    dve.wait_ge(gemm_act, u["banks"][-1]["turn"])
                    for f in range(2):
                        for i, (a, e) in enumerate(u["segs"]):
                            last = f == 1 and i == len(u["segs"]) - 1
                            taps(FFC[p % 2][:, f * T:(f + 1) * T], FFG[p % 2][:, f * T:(f + 1) * T],
                                 lambda tap: sm(l, W_FFC + (2 * u["u"] + f) * 3 + tap), a, e, conv_done if last else None)
                for b in some or u["banks"]:
                    if b["who"] != "dve":
                        continue
                    dve.wait_ge(gemm_ready, b["n"] + 1)
                    f, (a, e) = b["what"]
                    ps = bank(b["n"] % 2)[:, 0:e - a]
                    if k == "upv":
                        p = u["pair"]
                        dve.wait_ge(silu_done, p + 1)
                        ft = 2 * u["u"] + f - PARTS[u["part"]][0]
                        tt(Z[:, ft * T + a:ft * T + e], ps, FFC[p % 2][:, f * T + a:f * T + e], MUL).then_inc(*own(gemm_dve))
                    else:
                        m = 2 * u["u"] + f if k == "out" else u["m"]
                        gate = mod(l, 0 if a == 0 else 1, (16 if k == "out" else 40) + m)
                        dve.wait_ge(*own.last)
                        stt(Xv[:, m, a:e], ps, gate, Xv[:, m, a:e], MUL, ADD).then_inc(*own(gemm_dve))

            def norm(ni, segs, l):
                if ni == 0:
                    dve.wait_ge(loaded, 16 * N_LOADS)
                    v.tensor_copy(MSK[:, :], Z[:, 0:2 * (LEVELS + 1) * P]).then_inc(*own(masks_ready))
                for i, (a, e) in enumerate(segs):
                    g = AB[:, (2 * ni + i) * KT:(2 * ni + i + 1) * KT]
                    if l == DEPTH:
                        v.tensor_copy(g, FIN[:, :]).then_inc(*own())
                    else:
                        dve.wait_ge(*own.last)
                        stt(g, mod(l, 0 if a == 0 else 1, 8 if ni % 2 == 0 else 32, KT), 1.0,
                                  sm(l, W_N1 if ni % 2 == 0 else W_N2, KT), ADD, MUL).then_inc(*own())
                dve.wait_ge(*own.last)
                dve.wait_ge(rstd_ready, ni + 1)
                for k in range(KT):
                    for i, (a, e) in enumerate(segs):
                        g = AB[:, (2 * ni + i) * KT + k:(2 * ni + i) * KT + k + 1]
                        last = stt(Hv[:, k, a:e], Xv[:, k, a:e], g, RSTD[:, a:e], MUL, MUL)
                        last.then_inc(*own(scaled if i == len(segs) - 1 else None))

            def bounds_shifted(l):
                e = ST[:, 108:116]
                raw = [sm(i, W_LB, 8)[:, 4 * i:4 * i + 4] for i in range(DEPTH)]
                tt(ST[:, 104:108], raw[0], raw[1], MAX).then_inc(*own())
                dve.wait_ge(*own.last)
                for i in range(DEPTH):
                    tt(e[:, 4 * i:4 * i + 4], raw[i], ST[:, 104:108], SUB).then_inc(*own(hp_dve if i else None))

            def bounds(l):
                e = ST[:, 108:116]
                dve.wait_ge(hp_act, at(HP_ACT, l, "lb1"))
                tt(ST[:, 104:108], e[:, 0:4], e[:, 4:8], ADD).then_inc(*own())
                dve.wait_ge(*own.last)
                v.reciprocal(ST[:, 104:108], ST[:, 104:108]).then_inc(*own())
                dve.wait_ge(*own.last)
                for i in range(DEPTH):
                    tt(e[:, 4 * i:4 * i + 4], e[:, 4 * i:4 * i + 4], ST[:, 104:108], MUL).then_inc(*own())
                dve.wait_ge(*own.last)
                if l == 0:
                    tt(LBV[:, 0:4], e[:, 0:4], e[:, 0:4], SUB).then_inc(*own())
                else:
                    tt(LBV[:, 0:4], e[:, 0:4], e[:, 4:8], ADD).then_inc(*own())
                    dve.wait_ge(*own.last)
                    tt(LBV[:, 0:4], LBV[:, 0:4], e[:, 0:4], SUB).then_inc(*own())
                dve.wait_ge(*own.last)
                ts(LBV[:, 4:8], LBV[:, 0:4], -1.0, 1.0, MUL, ADD).then_inc(*own())
                dve.wait_ge(*own.last)
                ts(LBV[:, 4:8], LBV[:, 4:8], 1e-18, None, MAX).then_inc(*own(hp_dve))

            def dn(l):
                bounds_shifted(l)
                for f in range(6):
                    dve.wait_ge(prep_act, at(PR_ACT, l, f"m{f}"))
                    dst = PRB[:, (f % 2) * T:(f % 2 + 1) * T]
                    w = lambda tap: sm(l, W_DNC + f * 3 + tap)
                    taps(dst, fm("dn", f), w, 0, CTX)
                    taps(dst, fm("dn", f), w, CTX, T, prep_dve)
                    if f < 5:
                        yield
                for f in range(4):
                    dve.wait_ge(prep_act, at(PR_ACT, l, f"r{f}"))
                    stt(fm("dn", f), fm("dn", f), HD ** -0.5 if f < 2 else 1.0, ROWS4[f], MUL, MUL).then_inc(*own(prep_dve))
                raw = Y[:, BAO:BAO + 96].rearrange("p (t g h) -> p t g h", t=TT, g=4)
                at8 = lambda i: ba(i).rearrange("p (t g) -> p t g", t=TT)
                raw8 = Y[:, BAO:BAO + 96].rearrange("p (t g) -> p t g", t=TT)
                ts(at8(NEGB), raw8[:, :, 0:8], -80.0, None, MAX).then_inc(*own())
                tt(at8(G), raw8[:, :, 8:16], sm(l, W_DTB, 8)[:, None, :].to_broadcast([P, TT, 8]), ADD).then_inc(*own())
                dve.wait_ge(*own.last)
                stt(ba(EG), ba(G), -1.0, ba(G), MUL, MAX).then_inc(*own(prep_dve))
                dve.wait_ge(prep_act, at(PR_ACT, l, "b1"))
                v.tensor_scalar_add(ba(BETA), ba(BETA), 1.0).then_inc(*own())
                stt(ba(G), ba(G), 0.0, ba(EDEC), MAX, ADD).then_inc(*own())
                dve.wait_ge(*own.last)
                v.reciprocal(ba(BETA), ba(BETA)).then_inc(*own())
                dve.wait_ge(*own.last)
                v.tensor_scalar_mul(ba(NBETA), ba(BETA), -1.0).then_inc(*own())
                stt(at8(LOGA), at8(G), -1.0, ba(TOT)[:, None, 0:8].to_broadcast([P, TT, 8]), MUL, MUL).then_inc(*own(prep_dve))
                dve.wait_ge(prep_act, at(PR_ACT, l, "b2"))
                tt(ba(EDEC), ba(TOT), ba(G), SUB).then_inc(*own(prep_dve))
                stt(ba(NEGB), ba(EG), -1.0, ba(BETA), MUL, MUL).then_inc(*own())
                v.memset(Y[:, YS + 3584:YS + 3840], 0.0).then_inc(*own(prep_dve))
                bounds(l)
                dve.wait_ge(prep_act, at(PR_ACT, l, "b3"))
                for n in range(TT):
                    g = TT * l + n
                    A, B, C = [bank(2), bank(5)], [bank(3), bank(6)], [bank(4), bank(7)]
                    tile = [ORD[d][n] for d in range(2)]

                    def col(i, d):
                        return ba(i)[:, tile[d] * 8 + d * 4:tile[d] * 8 + d * 4 + 4]

                    def over(i, d, rows=slice(0, P)):
                        c = col(i, d)[rows, :]
                        return c[:, :, None].to_broadcast([c.shape[0], NH, HD])

                    for d in range(2):
                        dve.wait_ge(dn_pe, at2(DN_PE, g, "tr", d))
                        kt, vt = h4(A[d][:, 0:256]), h4(A[d][:, 256:512])
                        tt(h4(dn_buf(d, "kdec", 256)), kt, over(EDEC, d), MUL).then_inc(*own())
                        tt(h4(dn_buf(d, "vb", 256)), vt, over(BETA, d), MUL).then_inc(*own())
                        tt(h4(dn_buf(d, "kb", 256)), kt, over(NBETA, d), MUL).then_inc(*own(dn_dve))
                    for d in range(2):
                        dve.wait_ge(dn_pe, at2(DN_PE, g, "R", d))
                        for h in range(NH):
                            hs = slice(h * P, (h + 1) * P)
                            last = stt(dn_buf(d, "D", 512)[:, hs], C[d][:, hs], col(G, d)[:, h:h + 1],
                                       cc(C_NEG + d * P, P), SUB, MIN)
                            last.then_inc(*own(dn_dve if h == NH - 1 else None))
                    yield
                    for d in range(2):
                        dve.wait_ge(dn_pe, at2(DN_PE, g, "kk", d))
                        dve.wait_ge(dn_act, at2(DN_ACT, g, "exp", d))
                        tt(dn_buf(d, "NT", 512), A[d], dn_buf(d, "D", 512), MUL).then_inc(*own(dn_dve))
                    for d in range(2):
                        dve.wait_ge(dn_pe, at2(DN_PE, g, "kq", d))
                        tt(dn_buf(d, "at", 512), B[d], dn_buf(d, "D", 512), MUL).then_inc(*own(dn_dve))

                    def grow(dst, lv, d, src, transposed, sem_=None):
                        m = mask(d if transposed else 1 - d, lv)
                        v.copy_predicated(h4(dn_buf(d, dst, 512)), four(m), h4(src)).then_inc(*own(sem_))

                    for d in range(2):
                        dve.wait_ge(dn_pe, at2(DN_PE, g, "N", d))
                        dve.wait_ge(dn_dve, at2(DN_DVE, g, "NT", d))
                        grow("Tm", 1, d, C[d], False)
                        grow("TTm", 1, d, dn_buf(d, "NT", 512), True, dn_dve)
                    yield
                    for i in range(5):
                        for d in range(2):
                            dve.wait_ge(dn_pe, at2(DN_PE, g, f"Y{i}", d))
                            dve.wait_ge(dn_dve, at2(DN_DVE, g, "M" if i == 0 else f"L{i - 1}", d))
                            if i < 4:
                                grow("Tm", i + 2, d, C[d], False)
                            grow("TTm", i + 2, d, B[d], True, dn_dve)
                    yield
                    for j in range(2):
                        if j:
                            yield
                        for d in range(2):
                            c = j if d == 0 else 1 - j
                            rows = slice(64 * c, 64 * c + 64)
                            rhs = dn_buf(d, "rhs", 256)[rows, :]
                            dve.wait_ge(dn_pe, at2(DN_PE, g, f"K{j}", d))
                            tt(h4(rhs), h4(A[d][rows, 0:256]), over(NEGB, d, rows), MUL).then_inc(*own())
                            dve.wait_ge(*own.last)
                            tt(rhs, rhs, dn_buf(d, "vb", 256)[rows, :], ADD).then_inc(*own(dn_dve))
                        for d in range(2):
                            c = j if d == 0 else 1 - j
                            dve.wait_ge(dn_pe, at2(DN_PE, g, f"O{j}", d))
                            for hp in range(2):
                                S = DNS[d][:, hp * HD:(hp + 1) * HD]
                                o = ((tile[d] * 2 + d) * 2 + hp) * 2 + c
                                last = stt(S, S, ba(EGL)[:, o:o + 1], B[d][:, 256 + hp * HD:256 + (hp + 1) * HD], MUL, ADD)
                                last.then_inc(*own(dn_dve if hp else None))
                    for d in range(2):
                        t = dn_buf(d, "t", 256)
                        o = O[:, tile[d] * GW:(tile[d] + 1) * GW]
                        first = ORD[1 - d].index(tile[d]) > n
                        tt(h4(t), h4(A[d][:, 256:512]), over(EG, d), MUL).then_inc(*own())
                        dve.wait_ge(*own.last)
                        if first:
                            tt(o, t, C[d][:, 0:256], ADD).then_inc(*own(dn_dve))
                        else:
                            tt(t, t, C[d][:, 0:256], ADD).then_inc(*own())
                            dve.wait_ge(*own.last)
                            tt(o, t, o, ADD).then_inc(*own(dn_dve))

            def hg(l):
                for i in range(4):
                    F = fm("hg", 2 + i)
                    ts(F, F, -40.0, None, MAX).then_inc(*own(hp_dve))
                yield
                for i in range(4):
                    F = fm("hg", 2 + i)
                    d, f = i // 2, i % 2
                    dve.wait_ge(hp_act, at(HP_ACT, l, f"e{i}"))
                    tt(ROWS4[i], ROWS4[i], HGE[i], SUB).then_inc(*own())
                    tt(F, F, HGE[i], ADD).then_inc(*own(hp_dve))
                    hb, lf = HB(d, f), ROWS4[i]
                    if d == 1:
                        hb, lf = hb[:, ::-1], lf[:, ::-1]
                    dve.wait_ge(*own.last)
                    v.tensor_tensor_scan(hb, cc(C_SCAN, T), lf, 0.0, MUL, ADD).then_inc(*own(hp_dve))
                    if i % 2:
                        yield
                yield
                dve.wait_ge(*own.last)
                v.memset(SCR[:, 4352:4608], 0.0).then_inc(*own())
                dve.wait_ge(*own.last)
                dve.wait_ge(hp_act, at(HP_ACT, l, "k3"))
                two = lambda ap: ap.rearrange("p (f n) -> p f n", f=2)
                qk = Z[:, ZG:ZG + 6 * T].rearrange("p (x f n) -> p x f n", x=3, f=2)

                def differences(q, n, d):
                    t = ORD[d][n]
                    hb2 = Y[:, (2 + 2 * d) * T:(4 + 2 * d) * T].rearrange("p (f n) -> p f n", f=2)[:, :, t * P:(t + 1) * P]
                    for lv in range(1, LEVELS + 1) if wanted(q) else ():
                        s = 1 << (lv - 1)
                        w = hb2.rearrange("p f (b j) -> p f b j", j=2 * s)
                        m = w[:, :, :, s - 1:s] if d == 0 else w[:, :, :, s:s + 1]
                        tt(two(HE[d][:, lv - 1, :]).rearrange("p f (b j) -> p f b j", j=2 * s), w,
                                 m.to_broadcast([P, 2, P // (2 * s), 2 * s]), SUB).then_inc(*own())
                    w = hb2.rearrange("p f (c j) -> p f c j", c=2)
                    m = w[:, :, :, 63:64] if d == 0 else w[:, :, :, 0:1]
                    if q >= 2:
                        dve.wait_ge(hg_tr, q - 1)
                    tt(two(HKE[d]).rearrange("p f (c j) -> p f c j", c=2), w, m.to_broadcast([P, 2, 2, 64]), SUB).then_inc(*own(hg_diff))

                def operands(n, d):
                    cs = slice(ORD[d][n] * P, (ORD[d][n] + 1) * P)
                    return qk[:, 0, :, cs], qk[:, 1 + d, :, cs]

                def factors(q, n, d):
                    qs, ks = operands(n, d)
                    dve.wait_ge(hg_exp, q + 1)
                    if wanted(q):
                        tt(two(HQB[d]), two(HQB[d]), qs, MUL).then_inc(*own())
                    tt(two(HKE[d]), two(HKE[d]), ks, MUL).then_inc(*own(hg_factors))

                def weigh(q, n, d, lv):
                    if not wanted(q):
                        return
                    qs, ks = operands(n, d)
                    w = wanted_before(q)
                    if lv >= 4:
                        dve.wait_ge(hg_level, at(HG_LV, w, f"L{lv - 3}"))
                    elif w:
                        dve.wait_ge(hg_level, at(HG_LV, w - 1, f"L{lv + 3}"))
                    dst = QKT[lv % 3].rearrange("p (x f n) -> p x f n", x=2, f=2)
                    E = two(HE[d][:, lv - 1, :])
                    tt(dst[:, 0], qs, E, MUL).then_inc(*own())
                    tt(dst[:, 1], ks, E, MUL).then_inc(*own(hg_weighed))

                def take(q, d, lv):
                    if not wanted(q):
                        return
                    w = wanted_before(q)
                    dve.wait_ge(hg_level, at(HG_LV, w, f"L{lv}"))
                    dve.wait_ge(*own.last)
                    v.copy_predicated(h4(ATT[d]), four(mask(d, lv)), h4(bank(3 + ((LEVELS + 1) * w + lv) % 3))).then_inc(*own(hg_taken))

                def update(q, d, j):
                    c = j if d == 0 else 1 - j
                    dve.wait_ge(hg_chunk, at(HG_C, q, f"C{j}"))
                    for f in range(2):
                        S = HGS[d][:, f * HD:(f + 1) * HD]
                        stt(S, S, HDE[d][:, 2 * f + c:2 * f + c + 1], bank(7, f * HD, (f + 1) * HD), MUL, ADD).then_inc(*own(hg_state if f else None))

                def output(q, n, d):
                    if not wanted(q):
                        return
                    t = ORD[d][n]
                    o = O[:, t * GW:(t + 1) * GW]
                    if ORD[1 - d].index(t) > n or (ORD[1 - d].index(t) == n and d == 0):
                        v.tensor_copy(o, bank(6, 0, 256)).then_inc(*own(hg_out))
                    else:
                        tt(o, o, bank(6, 0, 256), ADD).then_inc(*own(hg_out))

                for n in range(TT):
                    for d in range(2):
                        q = 2 * (TT * l + n) + d
                        first, last_ = n == d == 0, n + d == TT
                        if first:
                            differences(q, n, d)
                            factors(q, n, d)
                            for lv in range(1, 4):
                                weigh(q, n, d, lv)
                        if q >= 2:
                            dve.wait_ge(hg_chunk, at(HG_C, q - 2, "C1"))
                        if wanted(q):
                            v.memset(ATT[d], 0.0).then_inc(*own())
                        if not last_:
                            differences(q + 1, n + d, 1 - d)
                        yield
                        take(q, d, 0)
                        weigh(q, n, d, 4)
                        take(q, d, 1)
                        if not first:
                            update(q - 1, 1 - d, 0)
                        weigh(q, n, d, 5)
                        take(q, d, 2)
                        weigh(q, n, d, 6)
                        take(q, d, 3)
                        if not first:
                            update(q - 1, 1 - d, 1)
                            output(q - 1, n - 1 + d, 1 - d)
                        take(q, d, 4)
                        if not last_:
                            factors(q + 1, n + d, 1 - d)
                            weigh(q + 1, n + d, 1 - d, 1)
                        take(q, d, 5)
                        if not last_:
                            weigh(q + 1, n + d, 1 - d, 2)
                        take(q, d, 6)
                        if not last_:
                            weigh(q + 1, n + d, 1 - d, 3)
                        yield
                for j in range(2):
                    update(2 * TT * (l + 1) - 1, 1, j)
                output(2 * TT * (l + 1) - 1, TT - 1, 1)

            def attend(st):
                kind, l = st
                i0, todo = items[st]
                na = kind == "na"
                stat = lambda g: ST[:, 8 * (g % 4):8 * (g % 4) + 8]

                def bias(hp):
                    for rnd in range(4):
                        gi = 4 * (2 * l + hp) + rnd
                        dve.wait_ge(bias_pe, gi + 1)
                        if rnd == 0:
                            dve.wait_ge(*own.last)
                        src = bank(2 + 2 * (rnd % 2), 0, 448).rearrange("p (k x) -> p k x", k=16)
                        dst = NAB.rearrange("p (x k) -> p k x", k=GRID)[:, rnd * 16:(rnd + 1) * 16, :]
                        m = cc(C_NAM + rnd * 16, 16)[:, :, None].to_broadcast([P, 16, 28])
                        tt(dst, src, m, ADD).then_inc(*own(bias_dve))
                    dve.wait_ge(*own.last)

                def maxes(i):
                    h, t = todo[i]
                    g = i0 + i
                    s = stat(g)
                    if i >= 2:
                        dve.wait_ge(at_tr, g - 1)
                    if na:
                        dve.wait_ge(at_s, part(st, i))
                        b0 = 512 * (2 + 2 * (g % 2))
                        if t < CT:
                            v.tensor_reduce(s[:, 0:1], PS[:, b0 + LAT:b0 + T], AX.X, MAX, negate=True).then_inc(*own(at_max))
                            return
                        qa = t - CT
                        o = ((h % 2) * 14 + 6 - 2 * qa) * GRID
                        ttr(out=NP_[g % 2][:, 0:LAT], in0=PS[:, b0:b0 + LAT], in1=NAB[:, o:o + LAT], scale=1.0,
                                  scalar=-3e38, op0=ADD, op1=MAX, accum_out=s[:, 4:5]).then_inc(*own())
                        v.tensor_reduce(s[:, 5:6], PS[:, b0 + LAT:b0 + T], AX.X, MAX).then_inc(*own())
                        dve.wait_ge(*own.last)
                        ts(s[:, 0:1], s[:, 4:5], s[:, 5:6], -1.0, MAX, MUL).then_inc(*own(at_max))
                    else:
                        a = 0 if t >= CT else LAT
                        for j in range(2):
                            b0 = 512 * (2 + 2 * j)
                            dve.wait_ge(at_s, part(st, i, j))
                            v.tensor_reduce(s[:, j:j + 1], PS[:, b0 + a:b0 + T], AX.X, MAX, negate=True).then_inc(*own(at_max))

                def probs(i):
                    h, t = todo[i]
                    g = i0 + i
                    s = stat(g)
                    dve.wait_ge(at_exp, part(st, i, 0 if na else 1))
                    if na:
                        if t >= CT:
                            tt(s[:, 6:7], s[:, 2:3], s[:, 3:4], ADD).then_inc(*own())
                            dve.wait_ge(*own.last)
                            v.reciprocal(s[:, 6:7], s[:, 6:7]).then_inc(*own(at_p))
                        else:
                            v.reciprocal(s[:, 6:7], s[:, 3:4]).then_inc(*own(at_p))
                    else:
                        a = 0 if t >= CT else LAT
                        v.reciprocal(s[:, 4:6], s[:, 2:4]).then_inc(*own())
                        dve.wait_ge(*own.last)
                        stt(s[:, 7:8], s[:, 2:3], s[:, 5:6], ST[:, 38:39], MUL, MUL).then_inc(*own())
                        dve.wait_ge(*own.last)
                        p0, p1 = DPP[g % 2][:, a:T], DPP[g % 2][:, T + a:2 * T]
                        stt(p0, p1, s[:, 7:8], p0, MUL, ADD).then_inc(*own(at_p))

                def outs(i):
                    h, t = todo[i]
                    g = i0 + i
                    s = stat(g)
                    dve.wait_ge(at_pv, g + 1)
                    dve.wait_ge(*own.last)
                    v.tensor_scalar_mul(O[:, t * GW + h * HD:t * GW + (h + 1) * HD], bank(7, 256, 256 + HD),
                                              s[:, 6:7] if na else s[:, 4:5]).then_inc(*own(at_o))

                n = len(todo)
                for i in range(n + 2):
                    if new_pair(st, i):
                        bias(todo[i][0] // 2)
                    if i < n:
                        maxes(i)
                    if i >= 2:
                        outs(i - 2)
                    if 0 < i <= n:
                        probs(i - 1)
                    yield

            def df(st):
                l = st[1]
                li = 0.8 - 0.6 * math.exp(-0.3 * l)
                lp = sm(l, W_LAM, 128)
                for k in range(2):
                    ttr(out=SCR[:, 1536:1568], in0=lp[:, 64 * k:64 * k + 32], in1=lp[:, 64 * k + 32:64 * k + 64], scale=1.0,
                              scalar=0.0, op0=MUL, op1=ADD, accum_out=ST[:, 34 + k:35 + k]).then_inc(*own(dp_dve if k else None))
                    dve.wait_ge(*own.last)
                for i in range(4):
                    dve.wait_ge(dp_pe, 4 * l + i + 1)
                    x = fm("df", i)[:, CTX:T]
                    tmp = SCR[:, 1536:2048]
                    dve.wait_ge(*own.last)
                    tt(tmp, bank(2 + i), cc(C_SIN, LAT), MUL).then_inc(*own())
                    tt(x, x, cc(C_COS, LAT), MUL).then_inc(*own())
                    dve.wait_ge(*own.last)
                    tt(x, x, tmp, ADD).then_inc(*own(dp_dve))
                dve.wait_ge(dp_act, at(["e"], l, "e"))
                ts(sm(l, W_DFN, HD), sm(l, W_DFN, HD), 1.0 - li, None, MUL).then_inc(*own())
                tt(ST[:, 38:39], ST[:, 37:38], ST[:, 36:37], SUB).then_inc(*own())
                dve.wait_ge(*own.last)
                v.tensor_scalar_add(ST[:, 38:39], ST[:, 38:39], -li).then_inc(*own(dp_dve))
                dve.wait_ge(*own.last)
                yield from attend(st)

            def post(st):
                m, p0, t0 = posts[st]
                kind, l = st
                if kind == "na":
                    return
                n = (TT - t0) * NH
                w = (TT - t0) * GW
                o = O[:, t0 * GW:TT * GW]
                o3 = o.rearrange("p (n e) -> p n e", e=HD)
                ss = ST[:, 40:40 + n]
                dve.wait_ge(post_act, 2 * m + 1)
                v.tensor_reduce(ss, SCR[:, 1536:1536 + w].rearrange("p (n e) -> p n e", e=HD), AX.X, ADD).then_inc(*own(post_dve))
                dve.wait_ge(post_act, 2 * m + 2)
                tt(o3, o3, ss[:, :, None].to_broadcast([P, n, HD]), MUL).then_inc(*own())
                dve.wait_ge(*own.last)
                nw = sm(l, {"dn": W_DNN, "df": W_DFN, "hg": W_HGN}[kind], HD)[:, None, :].to_broadcast([P, n, HD])
                if kind == "df":
                    tt(o3, o3, nw, MUL).then_inc(*own(post_dve))
                    return
                tt(o3, o3, nw, MUL).then_inc(*own())
                dve.wait_ge(*own.last)
                gate = tm(kind, 0 if kind == "dn" else 1)[:, t0 * GW:TT * GW]
                tt(o, o, gate, MUL).then_inc(*own(post_dve))

            dve.wait_ge(loaded_c, 16 * (1 + DEPTH))
            for st in steps:
                kind = st[0]
                if kind == "unit":
                    gemm_unit(st[1])
                elif kind == "norm":
                    norm(norm_at.index(st), st[3], st[1])
                else:
                    dve.wait_ge(gemm_act, acts_before[st])
                    dve.wait_ge(y_done, before[st])
                    body = dn(st[1]) if kind == "dn" else hg(st[1]) if kind == "hg" else df(st) if kind == "df" else attend(st)
                    filled(plans[st], body, gemm_unit, 1)
                    post(st)


_OUT = (P, KT, LAT)


def kernel(**inputs):
    import concourse.bacc as _bacc
    from concourse import mybir as _mybir
    from concourse.bass_utils import run_bass_kernel_spmd as _run

    nc = _bacc.Bacc("TRN2", target_bir_lowering=False, num_devices=1)
    arrays = lay_out(inputs)
    aps = {}
    for name in INPUTS:
        a = arrays[name]
        aps[name] = nc.dram_tensor(f"in_{name}", a.shape, _mybir.dt.from_np(a.dtype), kind="ExternalInput").ap()
    out = nc.dram_tensor("out_0", _OUT, _mybir.dt.float32, kind="ExternalOutput").ap()
    hybrid_backbone(nc, aps, out)
    r = _run(nc, [{f"in_{k}": arrays[k] for k in INPUTS}], core_ids=[0])
    y = np.asarray(r.results[0]["out_0"])
    return np.ascontiguousarray(y.transpose(2, 1, 0).reshape(1, LAT, DM))
```
